# Optimizing a Trainium2 kernel written in Bass

```python
import math
import numpy as np
import jax
import jax.numpy as jnp
from jax import lax

D_MODEL = 1024
BATCH = 1
SEQ = 2048
DEPTH = 2

GRID_W = 64
CTX_LEN = 256

NA_HEAD_DIM = 64
NA_WIDTH = D_MODEL // 4
NA_HEADS = NA_WIDTH // NA_HEAD_DIM
NA_WIN_ROWS = 8
NA_WIN_COLS = 16

DN_HEAD_DIM = 128
DN_WIDTH = D_MODEL // 2
DN_HEADS = DN_WIDTH // DN_HEAD_DIM
DN_CONV_W = 5
DN_CHUNK = 64

HY_WIDTH = D_MODEL // 4
HY_ORDER = 2
HY_CONV_W = 3
HY_EMB = 33
HY_HIDDEN = 64
HY_DECAY_TARGET = 1e-2
HY_FAST_DECAY = 0.3
HY_SLOW_DECAY = 1.5

MIX_WIDTH = NA_WIDTH + DN_WIDTH + HY_WIDTH
IN_SIZES = (3 * NA_WIDTH, NA_WIDTH, 3 * DN_WIDTH, DN_WIDTH, 2 * DN_HEADS, 2 * DN_HEADS, 3 * HY_WIDTH, HY_WIDTH)
IN_WIDTH = sum(IN_SIZES)

ROPE_BASE = 10000.0
NORM_EPS = 1e-6
ADA_SCALE = 0.5

kernel_name = 'hybrid_na_deltanet_hyena_block'

def rms_norm(x, g):
    xf = x.astype(jnp.float32)
    y = xf * lax.rsqrt(jnp.mean(jnp.square(xf), axis=-1, keepdims=True) + NORM_EPS)
    return (y * g.astype(jnp.float32)).astype(x.dtype)

def l2_normalize(x):
    xf = x.astype(jnp.float32)
    return xf * lax.rsqrt(jnp.sum(jnp.square(xf), axis=-1, keepdims=True) + NORM_EPS)

def split_cols(h):
    return jnp.split(h, np.cumsum(IN_SIZES)[:-1].tolist(), axis=-1)

def dwconv_centred(x, w):
    k, ch = w.shape
    return lax.conv_general_dilated(x, w.astype(x.dtype)[:, None, :], (1,), [(k // 2, k // 2)],
                                    dimension_numbers=('NWC', 'WIO', 'NWC'), feature_group_count=ch)

def modulation(cond, w_ada, b_ada):
    m = jnp.matmul(jax.nn.silu(cond), w_ada) + b_ada
    return jnp.split(m, 3, axis=-1)

def heads(t, n_heads, head_dim):
    return t.reshape(t.shape[0], t.shape[1], n_heads, head_dim)

def axial_rope(x):
    l, dh = x.shape[1], x.shape[-1]
    half = dh // 2
    nf = half // 2
    t = jnp.arange(l)
    inv = ROPE_BASE ** (-jnp.arange(nf, dtype=jnp.float32) / nf)
    xf = x.astype(jnp.float32)

    def rot(xp, pos):
        ang = pos.astype(jnp.float32)[:, None] * inv[None, :]
        cos = jnp.cos(ang)[None, :, None, :]
        sin = jnp.sin(ang)[None, :, None, :]
        a, b = xp[..., :nf], xp[..., nf:]
        return jnp.concatenate([a * cos - b * sin, b * cos + a * sin], axis=-1)

    out = jnp.concatenate([rot(xf[..., :half], t // GRID_W), rot(xf[..., half:], t % GRID_W)], axis=-1)
    return out.astype(x.dtype)

def na_latent(q, k, v, k_ctx, v_ctx, rpb):
    b, l, h, dh = q.shape
    rows = l // GRID_W
    kr = min(NA_WIN_ROWS, rows)
    kc = NA_WIN_COLS
    r = jnp.arange(rows)
    col = jnp.arange(GRID_W)
    band = jnp.clip(r - kr // 2, 0, rows - kr)[:, None] + jnp.arange(kr)[None, :]
    c0 = jnp.clip(col - kc // 2, 0, GRID_W - kc)
    in_win = (col[None, :] >= c0[:, None]) & (col[None, :] < c0[:, None] + kc)
    qg = q.reshape(b, rows, GRID_W, h, dh)
    kg = k.reshape(b, rows, GRID_W, h, dh)[:, band]
    vg = v.reshape(b, rows, GRID_W, h, dh)[:, band]
    scale = dh ** -0.5
    s_loc = jnp.einsum('brqhd,brkwhd->brhqkw', qg, kg).astype(jnp.float32) * scale
    dr = band - r[:, None] + (NA_WIN_ROWS - 1)
    dc = jnp.clip(col[None, :] - col[:, None], -(kc - 1), kc - 1) + (kc - 1)
    bias = rpb.astype(jnp.float32)[:, dr][:, :, :, dc]
    bias = jnp.transpose(bias, (1, 0, 3, 2, 4))
    s_loc = jnp.where(in_win[:, None, :], s_loc + bias, -jnp.inf)
    s_ctx = jnp.einsum('brqhd,bchd->brhqc', qg, k_ctx).astype(jnp.float32) * scale
    n_loc = kr * GRID_W
    s = jnp.concatenate([s_loc.reshape(b, rows, h, GRID_W, n_loc), s_ctx], axis=-1)
    p = jax.nn.softmax(s, axis=-1).astype(v.dtype)
    p_loc = p[..., :n_loc].reshape(b, rows, h, GRID_W, kr, GRID_W)
    o = (jnp.einsum('brhqkw,brkwhd->brqhd', p_loc, vg)
         + jnp.einsum('brhqc,bchd->brqhd', p[..., n_loc:], v_ctx))
    return o.reshape(b, l, h * dh)

def dense_ctx_attention(q, k, v):
    b, l, h, dh = q.shape
    s = jnp.einsum('bqhd,bkhd->bhqk', q, k).astype(jnp.float32) * dh ** -0.5
    p = jax.nn.softmax(s, axis=-1).astype(v.dtype)
    return jnp.einsum('bhqk,bkhd->bqhd', p, v).reshape(b, l, h * dh)

def dn_inputs(qkv_raw, b_raw, a_raw, conv_w, a_log, dt_bias, rope):
    bsz, l, _ = qkv_raw.shape
    qkv = jax.nn.silu(dwconv_centred(qkv_raw, conv_w))
    q, k, v = [heads(t, DN_HEADS, DN_HEAD_DIM) for t in jnp.split(qkv, 3, axis=-1)]
    if rope:
        q, k = axial_rope(q), axial_rope(k)
    q = l2_normalize(q) * (DN_HEAD_DIM ** -0.5)
    k = l2_normalize(k)
    v = v.astype(jnp.float32)
    beta = jax.nn.sigmoid(b_raw.astype(jnp.float32)).reshape(bsz, l, 2, DN_HEADS)
    g = -jnp.exp(a_log.astype(jnp.float32)) * jax.nn.softplus(
        a_raw.astype(jnp.float32).reshape(bsz, l, 2, DN_HEADS) + dt_bias.astype(jnp.float32))
    beta = jnp.transpose(beta, (2, 0, 3, 1))
    g = jnp.transpose(g, (2, 0, 3, 1))
    to_bhl = lambda t: jnp.transpose(t, (0, 2, 1, 3))
    return to_bhl(q), to_bhl(k), to_bhl(v), beta, g

def gated_delta_chunked(q, k, v, beta, g, s0):
    b, h, l, _ = q.shape
    dv = v.shape[-1]
    n = l // DN_CHUNK
    q, k, v = [t.reshape(b, h, n, DN_CHUNK, t.shape[-1]) for t in (q, k, v)]
    beta = beta.reshape(b, h, n, DN_CHUNK)
    gc = jnp.cumsum(g.reshape(b, h, n, DN_CHUNK), axis=-1)
    pos = jnp.arange(DN_CHUNK)
    tri = pos[:, None] >= pos[None, :]
    strict = pos[:, None] > pos[None, :]
    diff = gc[..., :, None] - gc[..., None, :]
    decay = jnp.where(tri, jnp.exp(jnp.where(tri, diff, 0.0)), 0.0)
    kb = k * beta[..., None]
    a_kk = jnp.where(strict, jnp.einsum('bhnid,bhnjd->bhnij', kb, k) * decay, 0.0)
    rhs = jnp.concatenate([v * beta[..., None], kb * jnp.exp(gc)[..., None]], axis=-1)
    sol = lax.linalg.triangular_solve(a_kk + jnp.eye(DN_CHUNK, dtype=jnp.float32), rhs,
                                      left_side=True, lower=True, unit_diagonal=True)
    u, w = sol[..., :dv], sol[..., dv:]
    a_qk = jnp.where(tri, jnp.einsum('bhnid,bhnjd->bhnij', q, k) * decay, 0.0)

    def step(s, xs):
        q_i, k_i, u_i, w_i, g_i, aqk_i = xs
        v_new = u_i - jnp.einsum('bhcd,bhde->bhce', w_i, s)
        o_i = (jnp.einsum('bhcd,bhde->bhce', q_i * jnp.exp(g_i)[..., None], s)
               + jnp.einsum('bhij,bhje->bhie', aqk_i, v_new))
        g_last = g_i[..., -1]
        s = (s * jnp.exp(g_last)[..., None, None]
             + jnp.einsum('bhcd,bhce->bhde', k_i * jnp.exp(g_last[..., None] - g_i)[..., None], v_new))
        return s, o_i

    xs = tuple(jnp.moveaxis(t, 2, 0) for t in (q, k, u, w, gc, a_qk))
    s_fin, o = lax.scan(step, s0, xs)
    return jnp.moveaxis(o, 0, 2).reshape(b, h, l, dv), s_fin

def dn_bidirectional(q, k, v, beta, g, s0):
    flip = lambda t: jnp.flip(t, axis=2)
    o_f, s_f = gated_delta_chunked(q, k, v, beta[0], g[0], s0[0])
    o_b, s_b = gated_delta_chunked(flip(q), flip(k), flip(v), flip(beta[1]), flip(g[1]), s0[1])
    return o_f + flip(o_b), jnp.stack([s_f, s_b])

def dn_output(o, z, norm_w):
    b, h, l, dv = o.shape
    o = jnp.transpose(o, (0, 2, 1, 3))
    y = rms_norm(o, norm_w) * jax.nn.silu(z.reshape(b, l, h, dv).astype(jnp.float32))
    return y.reshape(b, l, h * dv).astype(z.dtype)

def hyena_filters(l, w1, b1, w2, b2, w3, b3, freq, wout):
    f32 = jnp.float32
    t = jnp.linspace(0.0, 1.0, l, dtype=f32)[:, None]
    bands = (HY_EMB - 1) // 2
    fr = jnp.linspace(1e-4, bands - 1, bands, dtype=f32)
    ang = (2.0 * math.pi / l) * jnp.arange(l, dtype=f32)[:, None] * fr[None, :]
    z = jnp.concatenate([t, jnp.cos(ang), -jnp.sin(ang)], axis=-1)
    freq = freq.astype(f32)
    hid = jnp.sin(freq[0] * (z @ w1.astype(f32) + b1.astype(f32)))
    hid = jnp.sin(freq[1] * (hid @ w2.astype(f32) + b2.astype(f32)))
    hid = jnp.sin(freq[2] * (hid @ w3.astype(f32) + b3.astype(f32)))
    filt = (hid @ wout.astype(f32)).reshape(l, HY_ORDER, 2, HY_WIDTH)
    max_decay = math.log(HY_DECAY_TARGET) / HY_FAST_DECAY
    min_decay = math.log(HY_DECAY_TARGET) / HY_SLOW_DECAY
    deltas = jnp.abs(jnp.linspace(min_decay, max_decay, HY_WIDTH, dtype=f32))
    window = jnp.exp(-t * deltas[None, :])
    return filt * window[:, None, None, :]

def bidir_long_conv(u, h_fwd, h_bwd):
    b, l, ch = u.shape
    n = 2 * l
    kern = jnp.concatenate([h_fwd, jnp.zeros((1, ch), jnp.float32), h_bwd[:0:-1]], axis=0)
    y = jnp.fft.irfft(jnp.fft.rfft(u.astype(jnp.float32), n=n, axis=1) * jnp.fft.rfft(kern, n=n, axis=0)[None],
                      n=n, axis=1)
    return y[:, :l]

def hyena_mix(vx_raw, z, conv_w, filt, skip):
    vx = dwconv_centred(vx_raw, conv_w).astype(jnp.float32)
    v, x1, x2 = jnp.split(vx, 3, axis=-1)
    y = v
    for n, gate in enumerate((x1, x2)):
        y = gate * (bidir_long_conv(y, filt[:, n, 0], filt[:, n, 1]) + y * skip[n].astype(jnp.float32))
    return (y * jax.nn.silu(z.astype(jnp.float32))).astype(z.dtype)

def setup_inputs(seed: int = 0) -> dict:
    key = jax.random.key(seed)
    ks = jax.random.split(key, 26)
    f32 = jnp.float32
    nrm = lambda kk, shape, s: jax.random.normal(kk, shape, f32) * s
    d = D_MODEL
    dt = jnp.exp(jax.random.uniform(ks[13], (DEPTH, 2, DN_HEADS), f32, math.log(1e-3), math.log(1e-1)))
    return {
        'x': nrm(ks[0], (BATCH, SEQ, d), 1.0),
        'c': nrm(ks[1], (BATCH, d), 1.0),
        'ctx': nrm(ks[2], (BATCH, CTX_LEN, d), 1.0),
        'c_ctx': nrm(ks[3], (d,), 1.0),
        'w_ada': nrm(ks[4], (DEPTH, d, 3 * d), ADA_SCALE * d ** -0.5),
        'b_ada': nrm(ks[5], (DEPTH, 3 * d), 0.02),
        'g_pre': 1.0 + nrm(ks[6], (DEPTH, d), 0.02),
        'g_post': 1.0 + nrm(ks[7], (DEPTH, d), 0.02),
        'w_in': nrm(ks[8], (DEPTH, d, IN_WIDTH), d ** -0.5),
        'w_out': nrm(ks[9], (DEPTH, MIX_WIDTH, d), MIX_WIDTH ** -0.5),
        'na_rpb': nrm(ks[10], (DEPTH, NA_HEADS, 2 * NA_WIN_ROWS - 1, 2 * NA_WIN_COLS - 1), 0.1),
        'dn_conv': nrm(ks[11], (DEPTH, DN_CONV_W, 3 * DN_WIDTH), DN_CONV_W ** -0.5),
        'dn_a_log': jnp.log(jax.random.uniform(ks[12], (DEPTH, 2, DN_HEADS), f32, 1.0, 16.0)),
        'dn_dt_bias': dt + jnp.log(-jnp.expm1(-dt)),
        'dn_norm': 1.0 + nrm(ks[14], (DEPTH, DN_HEAD_DIM), 0.02),
        'hy_conv': nrm(ks[15], (DEPTH, HY_CONV_W, 3 * HY_WIDTH), HY_CONV_W ** -0.5),
        'hy_w1': nrm(ks[16], (DEPTH, HY_EMB, HY_HIDDEN), HY_EMB ** -0.5),
        'hy_b1': nrm(ks[17], (DEPTH, HY_HIDDEN), 0.1),
        'hy_w2': nrm(ks[18], (DEPTH, HY_HIDDEN, HY_HIDDEN), HY_HIDDEN ** -0.5),
        'hy_b2': nrm(ks[19], (DEPTH, HY_HIDDEN), 0.1),
        'hy_w3': nrm(ks[20], (DEPTH, HY_HIDDEN, HY_HIDDEN), HY_HIDDEN ** -0.5),
        'hy_b3': nrm(ks[21], (DEPTH, HY_HIDDEN), 0.1),
        'hy_freq': 1.0 + nrm(ks[22], (DEPTH, 3, HY_HIDDEN), 0.02),
        'hy_wout': nrm(ks[23], (DEPTH, HY_HIDDEN, HY_ORDER * 2 * HY_WIDTH), 0.1 * HY_HIDDEN ** -0.5),
        'hy_skip': nrm(ks[24], (DEPTH, HY_ORDER, HY_WIDTH), 0.5),
    }

def reference(x, c, ctx, c_ctx, w_ada, b_ada, g_pre, g_post, w_in, w_out, na_rpb, dn_conv, dn_a_log, dn_dt_bias,
              dn_norm, hy_conv, hy_w1, hy_b1, hy_w2, hy_b2, hy_w3, hy_b3, hy_freq, hy_wout, hy_skip):
    bsz, l, _ = x.shape
    lc = ctx.shape[1]
    for i in range(DEPTH):
        last = i == DEPTH - 1
        shift_x, scale_x, gate_x = modulation(c, w_ada[i], b_ada[i])
        shift_c, scale_c, gate_c = modulation(c_ctx, w_ada[i], b_ada[i])
        hx = rms_norm(x, g_pre[i]) * (1.0 + scale_x[:, None]) + shift_x[:, None]
        hc = rms_norm(ctx, g_pre[i]) * (1.0 + scale_c) + shift_c
        na_qkv_x, na_z_x, dn_qkv_x, dn_z_x, dn_b_x, dn_a_x, hy_vx_x, hy_z_x = split_cols(hx @ w_in[i])
        na_qkv_c, na_z_c, dn_qkv_c, dn_z_c, dn_b_c, dn_a_c, hy_vx_c, hy_z_c = split_cols(hc @ w_in[i])

        q_x, k_x, v_x = [heads(t, NA_HEADS, NA_HEAD_DIM) for t in jnp.split(na_qkv_x, 3, axis=-1)]
        q_c, k_c, v_c = [heads(t, NA_HEADS, NA_HEAD_DIM) for t in jnp.split(na_qkv_c, 3, axis=-1)]
        out_a_x = na_latent(q_x, k_x, v_x, k_c, v_c, na_rpb[i]) * jax.nn.silu(na_z_x)

        dq_c, dk_c, dv_c, beta_c, g_c = dn_inputs(dn_qkv_c, dn_b_c, dn_a_c, dn_conv[i], dn_a_log[i], dn_dt_bias[i], False)
        s0 = jnp.zeros((2, bsz, DN_HEADS, DN_HEAD_DIM, DN_HEAD_DIM), jnp.float32)
        do_c, s_ctx = dn_bidirectional(dq_c, dk_c, dv_c, beta_c, g_c, s0)
        dq_x, dk_x, dv_x, beta_x, g_x = dn_inputs(dn_qkv_x, dn_b_x, dn_a_x, dn_conv[i], dn_a_log[i], dn_dt_bias[i], True)
        do_x, _ = dn_bidirectional(dq_x, dk_x, dv_x, beta_x, g_x, s_ctx)
        out_b_x = dn_output(do_x, dn_z_x, dn_norm[i])

        filt_x = hyena_filters(l, hy_w1[i], hy_b1[i], hy_w2[i], hy_b2[i], hy_w3[i], hy_b3[i], hy_freq[i], hy_wout[i])
        out_c_x = hyena_mix(hy_vx_x, hy_z_x, hy_conv[i], filt_x, hy_skip[i])

        mix_x = jnp.concatenate([out_a_x, out_b_x, out_c_x], axis=-1)
        new_x = x + gate_x[:, None] * rms_norm(mix_x @ w_out[i], g_post[i])

        if not last:
            out_a_c = dense_ctx_attention(q_c, k_c, v_c) * jax.nn.silu(na_z_c)
            out_b_c = dn_output(do_c, dn_z_c, dn_norm[i])
            filt_c = hyena_filters(lc, hy_w1[i], hy_b1[i], hy_w2[i], hy_b2[i], hy_w3[i], hy_b3[i], hy_freq[i], hy_wout[i])
            out_c_c = hyena_mix(hy_vx_c, hy_z_c, hy_conv[i], filt_c, hy_skip[i])
            mix_c = jnp.concatenate([out_a_c, out_b_c, out_c_c], axis=-1)
            ctx = ctx + gate_c * rms_norm(mix_c @ w_out[i], g_post[i])
        x = new_x
    return x


_drawn_inputs = setup_inputs


def setup_inputs(seed=0):
    import zlib

    import numpy as np

    out = dict(_drawn_inputs(seed))
    spreads = {}
    factors = {'ctx': 4.693,
     'g_pre': 3.63,
     'g_post': 6.844,
     'na_rpb': 8.0,
     'dn_norm': 8.0,
     'hy_freq': 4.815}
    for name, (base, spread) in spreads.items():
        noise = np.random.default_rng([zlib.crc32(name.encode()), seed]).standard_normal(out[name].shape)
        drawn = base * np.exp(spread * noise) if base else spread * noise
        out[name] = jnp.asarray(drawn.astype(out[name].dtype))
    for name, factor in factors.items():
        out[name] = (out[name] * factor).astype(out[name].dtype)
    return out
```

```python
import math
from contextlib import ExitStack

import numpy as np
import concourse.bass as bass
from concourse import mybir

F32 = mybir.dt.float32
ALU = mybir.AluOpType
ACT = mybir.ActivationFunctionType
AX = mybir.AxisListType

P = 128
D = 1024
KT = D // P
SEQ, CTX = 2048, 256
T = CTX + SEQ
NT = T // P
DEPTH = 2
IN_WIDTH = 4112
EPS = 1e-6
C_NAQ, C_NAK, C_NAV, C_NAZ = 0, 256, 512, 768
C_DN, C_DNZ, C_DNB, C_HY, C_HYZ = 1024, 2560, 3072, 3088, 3856
GRID = 64
ROWS = SEQ // GRID
NEG = -1e30
CHUNKS = [(0, 512), (512, 512), (1024, 512), (1536, 512), (2048, 256)]


class Phase:

    def __init__(self, nc, tag):
        self.nc, self.tag, self.stack, self.sems = nc, tag, ExitStack(), []

    def __enter__(self):
        return self

    def sb(self, name, shape):
        return self.stack.enter_context(self.nc.sbuf_tensor(f"{self.tag}_{name}", shape, F32))

    def ps(self, name, shape):
        return self.stack.enter_context(self.nc.psum_tensor(f"{self.tag}_{name}", shape, F32))

    def sem(self, name):
        s = self.stack.enter_context(self.nc.semaphore(f"{self.tag}_{name}"))
        self.sems.append(s)
        return s

    def __exit__(self, kind, value, trace):
        if kind is None:
            for s in self.sems:
                self.nc.sync.sem_clear(s)
            self.nc.all_engine_barrier()
        self.stack.close()


def wait(eng, sem, value):
    if isinstance(value, int) and value <= 0:
        return
    eng.wait_ge(sem, value)


def at(eng, value):
    return value if isinstance(value, int) else eng.snap(value)


def repeat(eng, n, body, unroll=2, lo=0):
    first, last = lo // unroll, n // unroll
    if first == 0:
        for u in range(unroll):
            body(0, u)
        first = 1
    if last > first:
        with eng.Fori(first, last) as j:
            for u in range(unroll):
                body(j, u)


def modulation(nc, tag, c, c_ctx, w_ada, b_ada, g_pre, g_post, aff, gate_dram):
    GW, NG = 384, 8
    MB = GW // P
    with Phase(nc, tag) as ph:
        cond = ph.sb("cond", [P, 2, KT])
        act = ph.sb("act", [P, KT, 2])
        wa = ph.sb("wa", [P, 2, KT, GW])
        bias = ph.sb("bias", [P, 3 * KT])
        gp = ph.sb("gp", [P, 2, KT])
        mod = ph.sb("mod", [P, 3 * KT, 2])
        gate = ph.sb("gate", [P, 2, KT])
        ps = ph.ps("ps", [P, 2, 512])
        small, wl = ph.sem("small"), [ph.sem("w0"), ph.sem("w1")]
        silu, mm, ev, fin, st = ph.sem("silu"), ph.sem("mm"), ph.sem("ev"), ph.sem("fin"), ph.sem("st")
        wd = w_ada.rearrange("(k p) n -> p k n", p=P)
        with nc.Block() as block:

            @block.sync
            def _(sp):
                def load(j, u):
                    col = at(sp, (2 * j + u) * GW)
                    wait(sp, mm, 2 * j + u - 1)
                    sp.dma_start(wa[:, u, :, :], wd[:, :, bass.ds(col, GW)]).then_inc(wl[u], 16)
                repeat(sp, NG, load)
                sp.wait_ge(fin, 2)
                for j in range(2):
                    sp.dma_start(gate_dram[j].rearrange("(k p) -> p k", p=P), gate[:, j, :],
                                 allow_slow_non_contiguous=True).then_inc(st, 16)
                sp.wait_ge(st, 32)

            @block.scalar
            def _(act_e):
                act_e.dma_start(cond[:, 0, :], c.rearrange("(k p) -> p k", p=P), allow_slow_non_contiguous=True).then_inc(small, 16)
                act_e.dma_start(cond[:, 1, :], c_ctx.rearrange("(k p) -> p k", p=P), allow_slow_non_contiguous=True).then_inc(small, 16)
                act_e.dma_start(bias[:, :], b_ada.rearrange("(m p) -> p m", p=P), allow_slow_non_contiguous=True).then_inc(small, 16)
                act_e.dma_start(gp[:, 0, :], g_pre.rearrange("(k p) -> p k", p=P), allow_slow_non_contiguous=True).then_inc(small, 16)
                act_e.dma_start(gp[:, 1, :], g_post.rearrange("(k p) -> p k", p=P), allow_slow_non_contiguous=True).then_inc(small, 16)
                act_e.wait_ge(small, 80)
                nc.scalar.activation(act[:, :, :].rearrange("p k j -> p j k"), cond[:, :, :], ACT.Silu).then_inc(silu, 1)

            @block.tensor
            def _(pe):
                pe.wait_ge(silu, 1)

                def group(j, u):
                    wait(pe, wl[u], 16 * (j + 1))
                    wait(pe, ev, 2 * j + u - 1)
                    for m in range(MB):
                        for k in range(KT):
                            last = nc.tensor.matmul(ps[:, u, 2 * m:2 * m + 2], wa[:, u, k, m * P:(m + 1) * P],
                                                    act[:, k, :], start=(k == 0), stop=(k == KT - 1))
                    last.then_inc(mm, 1)
                repeat(pe, NG, group)

            @block.vector
            def _(dve):
                dve.wait_ge(small, 80)

                def copy(j, u):
                    wait(dve, mm, 2 * j + u + 1)
                    nc.vector.tensor_copy(mod[:, bass.ds((2 * j + u) * MB, MB), :],
                                          ps[:, u, 0:2 * MB].rearrange("p (m j) -> p m j", j=2)).then_inc(ev, 1)
                repeat(dve, NG, copy)
                dve.wait_ge(ev, NG)
                for j in range(2):
                    nc.vector.tensor_tensor(mod[:, :, j], mod[:, :, j], bias[:, :], ALU.add).then_inc(ev, 1)
                dve.wait_ge(ev, NG + 2)
                for j in range(2):
                    nc.vector.tensor_tensor(gate[:, j, :], mod[:, 2 * KT:, j], gp[:, 1, :], ALU.mult).then_inc(fin, 1)
                for j in range(2):
                    nc.vector.tensor_copy(aff[:, 1, :, j], mod[:, 0:KT, j]).then_inc(fin, 1)
                    nc.vector.scalar_tensor_tensor(out=aff[:, 0, :, j], in0=mod[:, KT:2 * KT, j], scalar=1.0,
                                                   in1=gp[:, 0, :], op0=ALU.add, op1=ALU.mult).then_inc(fin, 1)
                dve.wait_ge(fin, 6)


def norm_project(nc, tag, srcs, aff, w_in, ident_dram, proj):
    with Phase(nc, tag) as ph:
        ident = ph.sb("ident", [P, P])
        hT = ph.sb("hT", [P, KT, T])
        x = ph.sb("x", [P, 2, D])
        sq = ph.sb("sq", [P, D])
        xn = ph.sb("xn", [P, 2, D])
        st4 = ph.sb("st4", [P, 2, 4])
        w = ph.sb("w", [P, 2, KT, P])
        wba = ph.sb("wba", [P, KT, 16])
        o = ph.sb("o", [P, 2, T])
        psT = ph.ps("psT", [P, 2, 512])
        ps = ph.ps("ps", [P, 5, 512])
        const = ph.sem("const")
        xl = [ph.sem("xl0"), ph.sem("xl1")]
        ssq, ms, rt, rs, nrm, tr, hv = (ph.sem(s) for s in ("ssq", "ms", "rt", "rs", "nrm", "tr", "hv"))
        wl = [ph.sem("wl0"), ph.sem("wl1")]
        stored = [ph.sem("so0"), ph.sem("so1")]
        bal, mm, evv, eva = ph.sem("bal"), ph.sem("mm"), ph.sem("evv"), ph.sem("eva")
        wd = w_in.rearrange("(k p) n -> p k n", p=P)
        NB = 32
        rounds = [(src, first, n, j) for src, first, n, j in srcs]

        with nc.Block() as block:

            @block.sync
            def _(sp):
                sp.dma_start(ident[:, :], ident_dram).then_inc(const, 16)
                sp.dma_start(wba[:, :, :], wd[:, :, C_DNB:C_DNB + 16]).then_inc(bal, 16)
                for src, first, n, _ in rounds:
                    def load(j, u):
                        row = at(sp, (2 * j + u - first) * P)
                        wait(sp, nrm, 2 * j + u - 1)
                        sp.dma_start(x[:, u, :], src[bass.ds(row, P), :]).then_inc(xl[u], 16)
                    repeat(sp, first + n, load, lo=first)

                def store(j, u, off, m=P):
                    b = 2 * j + u
                    wait(sp, eva, 2 * (b + 1))
                    sp.dma_start(proj[bass.ds(b * P + off, m), 0:1024], o[0:m, u, 0:1024]).then_inc(stored[u], 16)
                    wait(sp, evv, 3 * (b + 1))
                    sp.dma_start(proj[bass.ds(b * P + off, m), 1024:T], o[0:m, u, 1024:T]).then_inc(stored[u], 16)

                def blocks(j, off, prev_off):
                    for u in range(2):
                        b = 2 * j + u
                        wait(sp, mm, 5 * (b - 1))
                        sp.dma_start(w[:, u, :, :], wd[:, :, bass.ds(b * P + off, P)]).then_inc(wl[u], 16)
                        if u:
                            store(j, 0, off)
                        elif not (isinstance(j, int) and j == 0):
                            store(j - 1 if isinstance(j, int) else j + -1, 1, prev_off)
                blocks(0, 0, 0)
                with sp.Fori(1, 12) as j:
                    blocks(j, 0, 0)
                blocks(12, 16, 0)
                with sp.Fori(13, 16) as j:
                    blocks(j, 16, 16)
                store(15, 1, 16)
                store(16, 0, C_DNB - 32 * P, 16)
                sp.wait_ge(stored[0], 32 * 17)
                sp.wait_ge(stored[1], 32 * 16)

            @block.scalar
            def _(act):
                for _, first, n, mj in rounds:
                    def tile(j, u):
                        i = 2 * j + u
                        wait(act, xl[u], 16 * (j + 1))
                        wait(act, ms, i)
                        wait(act, rs, i - 1)
                        nc.scalar.activation(sq[:, :], x[:, u, :], ACT.Square, accum_out=st4[:, u, 0:1]).then_inc(ssq, 1)
                        wait(act, ms, i + 1)
                        nc.scalar.activation(st4[:, u, 2:3], st4[:, u, 1:2], ACT.Sqrt).then_inc(rt, 1)
                        for h in range(2):
                            wait(act, tr, 2 * i + h + 1)
                            for q in range(4):
                                k = 4 * h + q
                                last = nc.scalar.activation(hT[:, k, bass.ds(i * P, P)], psT[:, h, q * P:(q + 1) * P],
                                                            ACT.Identity, scale=aff[:, 0, k, mj:mj + 1],
                                                            bias=aff[:, 1, k, mj:mj + 1])
                            last.then_inc(hv, 1)
                    repeat(act, first + n, tile, lo=first)

                def evict(j, u, m=P):
                    b = 2 * j + u
                    wait(act, stored[u], 32 * j)
                    for c in (0, 1):
                        wait(act, mm, 5 * b + c + 1)
                        nc.scalar.activation(o[0:m, u, CHUNKS[c][0]:CHUNKS[c][0] + CHUNKS[c][1]],
                                             ps[0:m, c, 0:CHUNKS[c][1]], ACT.Copy).then_inc(eva, 1)
                repeat(act, NB, evict)
                evict(16, 0, 16)

            @block.vector
            def _(dve):
                for _, first, n, _ in rounds:
                    def tile(j, u):
                        i = 2 * j + u
                        wait(dve, ssq, i + 1)
                        nc.vector.tensor_scalar(st4[:, u, 1:2], st4[:, u, 0:1], 1.0 / D, EPS, ALU.mult, ALU.add).then_inc(ms, 1)
                        wait(dve, rt, i + 1)
                        nc.vector.reciprocal(st4[:, u, 3:4], st4[:, u, 2:3]).then_inc(rs, 1)
                        wait(dve, rs, i + 1)
                        wait(dve, tr, 2 * (i - 1))
                        nc.vector.tensor_scalar(xn[:, u, :], x[:, u, :], st4[:, u, 3:4], None, ALU.mult).then_inc(nrm, 1)
                    repeat(dve, first + n, tile, lo=first)

                def evict(j, u, m=P):
                    b = 2 * j + u
                    wait(dve, stored[u], 32 * j)
                    for c in (2, 3, 4):
                        wait(dve, mm, 5 * b + c + 1)
                        nc.vector.tensor_copy(o[0:m, u, CHUNKS[c][0]:CHUNKS[c][0] + CHUNKS[c][1]],
                                              ps[0:m, c, 0:CHUNKS[c][1]]).then_inc(evv, 1)
                repeat(dve, NB, evict)
                evict(16, 0, 16)

            @block.tensor
            def _(pe):
                pe.wait_ge(const, 16)

                def tile(j, u):
                    i = 2 * j + u
                    wait(pe, nrm, i + 1)
                    for h in range(2):
                        wait(pe, hv, 2 * i + h - 1)
                        for q in range(4):
                            last = nc.tensor.transpose(psT[:, h, q * P:(q + 1) * P],
                                                       xn[:, u, (4 * h + q) * P:(4 * h + q + 1) * P], ident[:, :])
                        last.then_inc(tr, 1)
                repeat(pe, NT, tile)
                pe.wait_ge(hv, 2 * NT)

                def block_(j, u, m=P):
                    b = 2 * j + u
                    if m == P:
                        wait(pe, wl[u], 16 * (j + 1))
                    else:
                        pe.wait_ge(bal, 16)
                    for c, (t0, tn) in enumerate(CHUNKS):
                        if c < 2:
                            wait(pe, eva, 2 * (b - 1) + c + 1)
                        else:
                            wait(pe, evv, 3 * (b - 1) + c - 1)
                        for k in range(KT):
                            lhsT = w[:, u, k, :] if m == P else wba[:, k, :]
                            last = nc.tensor.matmul(ps[0:m, c, 0:tn], lhsT, hT[:, k, t0:t0 + tn],
                                                    start=(k == 0), stop=(k == KT - 1))
                        last.then_inc(mm, 1)
                repeat(pe, NB, block_)
                block_(16, 0, 16)


H = 4
DN = H * P
LEVELS = 7


def short_conv(nc, tag, proj, row0, tiles, weight, silu, out_ctx, out):
    taps = weight.shape[0]
    h = taps // 2
    W = T + h
    with Phase(nc, tag) as ph:
        wcol = ph.sb("wcol", [P, taps, tiles])
        x = ph.sb("x", [P, 2, W + 2 * h])
        acc = ph.sb("acc", [P, 2, W])
        y = ph.sb("y", [P, 2, W])
        wl, zero = ph.sem("wl"), ph.sem("zero")
        xl = [ph.sem("xl0"), ph.sem("xl1")]
        stored = [ph.sem("so0"), ph.sem("so1")]
        first, tap, done = ph.sem("first"), ph.sem("tap"), ph.sem("done")
        VT = taps - 1
        with nc.Block() as block:

            @block.sync
            def _(sp):
                sp.wait_ge(zero, 1)

                def load(j, u):
                    row = at(sp, row0 + (2 * j + u) * P)
                    wait(sp, tap, VT * (2 * j + u - 1))
                    sp.dma_start(x[:, u, h:h + CTX], proj[bass.ds(row, P), 0:CTX]).then_inc(xl[u], 16)
                    sp.dma_start(x[:, u, 2 * h + CTX:2 * h + T], proj[bass.ds(row, P), CTX:T]).then_inc(xl[u], 16)
                repeat(sp, tiles, load)

            @block.gpsimd
            def _(pool):
                for u in range(2):
                    nc.gpsimd.memset(x[:, u, 0:h], 0.0)
                    nc.gpsimd.memset(x[:, u, h + CTX:2 * h + CTX], 0.0)
                    last = nc.gpsimd.memset(x[:, u, 2 * h + T:3 * h + T], 0.0)
                last.then_inc(zero, 1)

            @block.scalar
            def _(act):
                for t in range(taps):
                    act.dma_start(wcol[:, t, :], weight[t].rearrange("(f p) -> p f", p=P),
                                  allow_slow_non_contiguous=True).then_inc(wl, 16)
                act.wait_ge(wl, 16 * taps)
                act.wait_ge(zero, 1)

                def finish(i, j, u):
                    wait(act, tap, VT * (i + 1))
                    wait(act, stored[u], 32 * j)
                    nc.scalar.activation(y[:, u, :], acc[:, u, :], ACT.Silu if silu else ACT.Copy).then_inc(done, 1)
                    wait(act, done, i + 1)
                    act.dma_start(out_ctx[bass.ds(i * P, P), :], y[:, u, 0:CTX]).then_inc(stored[u], 16)
                    act.dma_start(out[bass.ds(i * P, P), :], y[:, u, CTX + h:W]).then_inc(stored[u], 16)

                def tile(j, u):
                    i = 2 * j + u
                    wait(act, xl[u], 32 * (j + 1))
                    nc.scalar.activation(acc[:, u, :], x[:, u, 0:W], ACT.Identity,
                                         scale=wcol[:, 0, bass.ds(i, 1)]).then_inc(first, 1)
                    finish(i, j, u)
                repeat(act, tiles, tile)
                act.wait_ge(stored[0], 16 * tiles)
                act.wait_ge(stored[1], 16 * tiles)

            @block.vector
            def _(dve):
                dve.wait_ge(wl, 16 * taps)

                def tile(j, u):
                    i = 2 * j + u
                    wait(dve, first, i + 1)
                    for t in range(1, taps):
                        wait(dve, tap, VT * i + t - 1)
                        nc.vector.scalar_tensor_tensor(out=acc[:, u, :], in0=x[:, u, t:t + W],
                                                       scalar=wcol[:, t, bass.ds(i, 1)], in1=acc[:, u, :],
                                                       op0=ALU.mult, op1=ALU.add).then_inc(tap, 1)
                repeat(dve, tiles, tile)


G_, GC, BETA, EGC, NBEG, EKD, ELAST = range(7)


def dn_gates(nc, tag, proj, a_log, dt_bias, ident_dram, tri_dram, col):
    N8 = 2 * H
    with Phase(nc, tag) as ph:
        ident = ph.sb("ident", [P, P])
        tri = ph.sb("tri", [P, 3, P])
        ba = ph.sb("ba", [16, T])
        raw = ph.sb("raw", [P, NT, 16])
        rows = ph.sb("rows", [P, 2, N8])
        t = ph.sb("t", [P, 4, NT, N8])
        ps = ph.ps("ps", [P, 3, 512])
        ld, pe_s, v, a = ph.sem("ld"), ph.sem("products"), ph.sem("vector"), ph.sem("scalar")
        b3 = lambda r: rows[:, r:r + 1, :].to_broadcast([P, NT, N8])
        with nc.Block() as block:

            @block.sync
            def _(sp):
                sp.dma_start(ident[:, :], ident_dram).then_inc(ld, 16)
                sp.dma_start(tri[:, :, :], tri_dram).then_inc(ld, 16)
                sp.dma_start(ba[:, :], proj[C_DNB:C_DNB + 16, :]).then_inc(ld, 16)
                sp.dma_start(rows[:, 0, :], a_log.partition_broadcast(P)).then_inc(ld, 16)
                sp.dma_start(rows[:, 1, :], dt_bias.partition_broadcast(P)).then_inc(ld, 16)

            @block.tensor
            def _(pe):
                pe.wait_ge(ld, 80)
                for i in range(NT):
                    last = nc.tensor.transpose(ps[:, 0, 16 * i:16 * i + 16], ba[:, i * P:(i + 1) * P], ident[0:16, 0:16])
                last.then_inc(pe_s, 1)
                pe.wait_ge(v, 6)
                nc.tensor.matmul(ps[:, 1, 0:NT * H], tri[:, 0, :], col[:, G_, :, 0:H], start=True, stop=True)
                nc.tensor.matmul(ps[:, 1, NT * H:NT * N8], tri[:, 1, :], col[:, G_, :, H:N8], start=True, stop=True)
                nc.tensor.matmul(ps[:, 2, 0:NT * N8], tri[:, 2, :], col[:, G_, :, :], start=True, stop=True).then_inc(pe_s, 1)

            @block.scalar
            def _(act):
                act.wait_ge(v, 2)
                nc.scalar.activation(t[:, 1, :, :], t[:, 0, :, :], ACT.Exp).then_inc(a, 1)
                nc.scalar.activation(t[:, 3, :, :], raw[:, :, 0:N8], ACT.Exp, scale=-1.0).then_inc(a, 1)
                nc.scalar.activation(rows[:, 0, :], rows[:, 0, :], ACT.Exp).then_inc(a, 1)
                act.wait_ge(a, 1)
                nc.scalar.activation(t[:, 0, :, :], t[:, 1, :, :], ACT.Ln, bias=1.0).then_inc(a, 1)
                act.wait_ge(v, 9)
                nc.scalar.activation(col[:, EGC, :, :], col[:, GC, :, :], ACT.Exp).then_inc(a, 1)
                nc.scalar.activation(col[:, EKD, :, :], t[:, 1, :, :], ACT.Exp).then_inc(a, 1)
                nc.scalar.activation(col[:, ELAST, :, :], ps[:, 2, 0:NT * N8].rearrange("p (n e) -> p n e", e=N8),
                                     ACT.Exp).then_inc(a, 1)
                act.wait_ge(a, 7)

            @block.vector
            def _(dve):
                def step(ins, n):
                    ins.then_inc(v, 1)
                    dve.wait_ge(v, n)
                dve.wait_ge(pe_s, 1)
                dve.wait_ge(ld, 80)
                step(nc.vector.tensor_copy(raw[:, :, :], ps[:, 0, 0:NT * 16].rearrange("p (n e) -> p n e", e=16)), 1)
                nc.vector.tensor_tensor(t[:, 2, :, :], raw[:, :, N8:16], b3(1), ALU.add).then_inc(pe_s, 1)
                dve.wait_ge(pe_s, 2)
                step(nc.vector.scalar_tensor_tensor(out=t[:, 0, :, :], in0=t[:, 2, :, :], scalar=-1.0, in1=t[:, 2, :, :],
                                                    op0=ALU.mult, op1=ALU.min), 2)
                dve.wait_ge(a, 4)
                step(nc.vector.scalar_tensor_tensor(out=t[:, 2, :, :], in0=t[:, 2, :, :], scalar=0.0, in1=t[:, 0, :, :],
                                                    op0=ALU.max, op1=ALU.add), 3)
                step(nc.vector.tensor_scalar(rows[:, 0, :], rows[:, 0, :], -1.0, None, ALU.mult), 4)
                step(nc.vector.tensor_scalar(t[:, 3, :, :], t[:, 3, :, :], 1.0, None, ALU.add), 5)
                step(nc.vector.tensor_tensor(col[:, G_, :, :], t[:, 2, :, :], b3(0), ALU.mult), 6)
                step(nc.vector.reciprocal(col[:, BETA, :, :], t[:, 3, :, :]), 7)
                dve.wait_ge(pe_s, 3)
                step(nc.vector.tensor_copy(col[:, GC, :, :].rearrange("p n (d h) -> p d n h", d=2),
                                           ps[:, 1, 0:NT * N8].rearrange("p (d n h) -> p d n h", d=2, h=H)), 8)
                step(nc.vector.tensor_tensor(t[:, 1, :, :], ps[:, 2, 0:NT * N8].rearrange("p (n e) -> p n e", e=N8),
                                             col[:, GC, :, :], ALU.subtract), 9)
                dve.wait_ge(a, 7)
                step(nc.vector.scalar_tensor_tensor(out=col[:, NBEG, :, :], in0=col[:, BETA, :, :], scalar=-1.0,
                                                    in1=col[:, EGC, :, :], op0=ALU.mult, op1=ALU.mult), 10)


def dn_tokens(nc, tag, dnT, rope_dram, ident_dram, qkv):
    with Phase(nc, tag) as ph:
        ident = ph.sb("ident", [P, P])
        f = ph.sb("f", [P, 2, 12, P])
        rope = ph.sb("rope", [P, 2, 2, P])
        t1 = ph.sb("t1", [P, 2, 2 * DN])
        t2 = ph.sb("t2", [P, 2, 2 * DN])
        sq = ph.sb("sq", [P, 2 * DN])
        n8 = ph.sb("n8", [P, 2, 4, 2 * H])
        o = ph.sb("o", [P, 2, 3 * DN])
        ps = [ph.ps("ps0", [P, 3, 512]), ph.ps("ps1", [P, 3, 512])]
        const = ph.sem("const")
        ld, stored = [ph.sem("ld0"), ph.sem("ld1")], [ph.sem("so0"), ph.sem("so1")]
        tr, rot, sums, vout, sqs, ssum, rt, rs, nrm = (ph.sem(s) for s in
            ("transposed", "rotated", "summed", "v_out", "squares", "square_sums", "roots", "inverse", "normalised"))
        src = dnT.rearrange("(f p) t -> p f t", p=P)
        with nc.Block() as block:

            @block.sync
            def _(sp):
                sp.dma_start(ident[:, :], ident_dram).then_inc(const, 16)

                def load(j, u):
                    i = 2 * j + u
                    wait(sp, rot, 3 * (i - 1))
                    sp.dma_start(f[:, u, :, :], src[:, :, bass.ds(i * P, P)]).then_inc(ld[u], 16)
                    sp.dma_start(rope[:, u, :, :], rope_dram[bass.ds(i * P, P), :, :]).then_inc(ld[u], 16)
                repeat(sp, NT, load)

            @block.tensor
            def _(pe):
                pe.wait_ge(const, 16)

                def tile(j, u):
                    i = 2 * j + u
                    wait(pe, ld[u], 32 * (j + 1))
                    wait(pe, rot, 3 * (i - 1))
                    wait(pe, vout, i - 1)
                    for m in range(12):
                        last = nc.tensor.transpose(ps[u][:, m // 4, (m % 4) * P:(m % 4 + 1) * P], f[:, u, m, :], ident[:, :])
                    last.then_inc(tr, 1)
                repeat(pe, NT, tile)

            @block.vector
            def _(dve):
                def tile(j, u):
                    i = 2 * j + u
                    wait(dve, tr, i + 1)
                    wait(dve, sums, i - 1)
                    x = ps[u][:, 0:2, :].rearrange("p a (h e) -> p (a h) e", e=P)
                    nc.vector.tensor_tensor(t1[:, u, :].rearrange("p (h e) -> p h e", e=P), x,
                                            rope[:, u, 0:1, :].to_broadcast([P, 2 * H, P]), ALU.mult).then_inc(rot, 1)
                    x4 = ps[u][:, 0:2, :].rearrange("p a (h g b e) -> p (a h) g b e", g=2, b=2, e=32)
                    t4 = t2[:, u, :].rearrange("p (h g b e) -> p h g b e", g=2, b=2, e=32)
                    s4 = rope[:, u, 1, :].rearrange("p (g b e) -> p g b e", g=2, b=2)
                    for b in range(2):
                        sb = s4[:, :, b, :].unsqueeze(1).to_broadcast([P, 2 * H, 2, 32])
                        nc.vector.tensor_tensor(t4[:, :, :, b, :], x4[:, :, :, 1 - b, :], sb, ALU.mult).then_inc(rot, 1)
                    wait(dve, sqs, i + 1)
                    nc.vector.tensor_reduce(out=n8[:, u, 0, :], in_=sq[:, :].rearrange("p (h e) -> p h e", e=P),
                                            axis=AX.X, op=ALU.add).then_inc(ssum, 1)
                    wait(dve, ssum, 2 * i + 1)
                    nc.vector.tensor_scalar(n8[:, u, 1, :], n8[:, u, 0, :], EPS, None, ALU.add).then_inc(ssum, 1)
                    wait(dve, rt, i + 1)
                    nc.vector.reciprocal(n8[:, u, 3, :], n8[:, u, 2, :]).then_inc(rs, 1)
                    wait(dve, rs, 2 * i + 1)
                    nc.vector.tensor_scalar(n8[:, u, 3, 0:H], n8[:, u, 3, 0:H], float(P) ** -0.5, None, ALU.mult).then_inc(rs, 1)
                repeat(dve, NT, tile)

            @block.gpsimd
            def _(pool):
                def tile(j, u):
                    i = 2 * j + u
                    wait(pool, rot, 3 * (i + 1))
                    nc.gpsimd.tensor_tensor(t1[:, u, :], t1[:, u, :], t2[:, u, :], ALU.add).then_inc(sums, 1)
                    wait(pool, sums, i + 1)
                    wait(pool, rs, 2 * (i + 1))
                    wait(pool, stored[u], 16 * j)
                    nc.gpsimd.tensor_tensor(o[:, u, 0:2 * DN].rearrange("p (h e) -> p h e", e=P),
                                            t1[:, u, :].rearrange("p (h e) -> p h e", e=P),
                                            n8[:, u, 3, :].unsqueeze(2).to_broadcast([P, 2 * H, P]), ALU.mult).then_inc(nrm, 1)
                repeat(pool, NT, tile)

            @block.scalar
            def _(act):
                def tile(j, u):
                    i = 2 * j + u
                    wait(act, tr, i + 1)
                    wait(act, stored[u], 16 * j)
                    nc.scalar.activation(o[:, u, 2 * DN:], ps[u][:, 2, :], ACT.Copy).then_inc(vout, 1)
                    wait(act, sums, i + 1)
                    wait(act, ssum, 2 * i)
                    nc.scalar.activation(sq[:, :], t1[:, u, :], ACT.Square).then_inc(sqs, 1)
                    wait(act, ssum, 2 * (i + 1))
                    nc.scalar.activation(n8[:, u, 2, :], n8[:, u, 1, :], ACT.Sqrt).then_inc(rt, 1)
                    wait(act, nrm, i + 1)
                    wait(act, vout, i + 1)
                    act.dma_start(qkv[bass.ds(i * P, P), :], o[:, u, :]).then_inc(stored[u], 16)
                repeat(act, NT, tile)
                act.wait_ge(stored[0], 16 * (NT // 2))
                act.wait_ge(stored[1], 16 * (NT // 2))


def dn_scan(nc, tag, qkv, col, ident_dram, tri_dram, neg_dram, lev_dram, o_dir):
    with Phase(nc, tag) as ph:
        ident = ph.sb("ident", [P, P])
        tri = ph.sb("tri", [P, 3, P])
        neg = ph.sb("neg", [P, 2, P])
        lev = ph.sb("lev", [P, 2, LEVELS, P])
        D2 = range(2)
        two = lambda name, shape: [ph.sb(f"{name}{d}", shape) for d in D2]
        x = two("x", [P, 2, 3 * DN])
        kb, qg, kd, vb, gt = (two(s, [P, 2, DN]) for s in ("kb", "qg", "kd", "vb", "gt"))
        KT_, KBT, QT, QGT = (two(s, [P, DN]) for s in ("KT", "KBT", "QT", "QGT"))
        E, AT, QKD, X, XT, PM, R, U, W, VN, S = (two(s, [P, DN]) for s in
                                                 ("E", "AT", "QKD", "X", "XT", "PM", "R", "U", "W", "VN", "S"))
        CT = two("CT", [P, LEVELS, DN])
        O = two("O", [P, 2, DN])
        ps = [ph.ps(f"ps{d}", [P, 4, 512]) for d in D2]
        const, zero = ph.sem("const"), ph.sem("zero")
        sems = lambda name: [ph.sem(f"{name}{d}") for d in D2]
        ld = [[ph.sem(f"ld{d}{u}") for u in D2] for d in D2]
        stored = [[ph.sem(f"so{d}{u}") for u in D2] for d in D2]
        s_vb, s_kd, s_kb, s_qg, s_gt = (sems(s) for s in ("vb", "kd", "kb", "qg", "gt"))
        m_kT, m_kbT, m_qT, m_qgT, m_gc, m_kk, m_qk, m_a = (sems(s) for s in
            ("m_kT", "m_kbT", "m_qT", "m_qgT", "m_gc", "m_kk", "m_qk", "m_a"))
        m_ax, m_xp, m_px, m_ks, m_u, m_w, m_new, m_o, m_up = (sems(s) for s in
            ("m_ax", "m_xp", "m_px", "m_ks", "m_u", "m_w", "m_new", "m_o", "m_up"))
        kT_in, kbT_in, qT_in, qgT_in = (sems(s) for s in ("kT_in", "kbT_in", "qT_in", "qgT_in"))
        arg, dec, at_, qkd_, ct, xt0, x0, pl, xl_, xtl, r_, u_, w_, vn_, o_, s_ = (sems(s) for s in
            ("arg", "decay", "at", "qkd", "ct", "xt0", "x0", "pl", "xl", "xtl", "r", "u", "w", "vn", "o", "s"))
        h4 = lambda ap: ap.rearrange("p (h e) -> p h e", e=P)
        hd = lambda h: slice(h * P, (h + 1) * P)
        NL = LEVELS - 2

        def tile_of(d, j, u):
            if d == 0:
                return 2 * j + u
            return 1 - u if isinstance(j, int) and j == 0 else j * -2 + (NT + 1 - u)

        with nc.Block() as block:

            @block.sync
            def _(sp):
                sp.dma_start(ident[:, :], ident_dram).then_inc(const, 16)
                sp.dma_start(tri[:, :, :], tri_dram).then_inc(const, 16)
                sp.dma_start(neg[:, :, :], neg_dram).then_inc(const, 16)
                sp.dma_start(lev[:, :, :, :], lev_dram).then_inc(const, 16)

                def step(j, u):
                    for d in D2:
                        row = at(sp, tile_of(d, j, u) * P)
                        wait(sp, m_qT[d], 2 * j + u - 1)
                        sp.dma_start(x[d][:, u, :], qkv[bass.ds(row, P), :]).then_inc(ld[d][u], 16)
                repeat(sp, NT, step)

            @block.gpsimd
            def _(pool):
                for d in D2:
                    nc.gpsimd.memset(S[d][:, :], 0.0).then_inc(zero, 1)
                pool.wait_ge(const, 64)

                def step(j, u):
                    i = 2 * j + u
                    for d in D2:
                        t = tile_of(d, j, u)
                        g = lambda which: col[:, which, bass.ds(t, 1), d * H:(d + 1) * H].rearrange("p o h -> p (o h)").unsqueeze(2).to_broadcast([P, H, P])
                        part = lambda n: h4(x[d][:, u, n * DN:(n + 1) * DN])
                        wait(pool, ld[d][u], 16 * (j + 1))
                        wait(pool, r_[d], i - 1)
                        nc.gpsimd.tensor_tensor(h4(vb[d][:, u, :]), part(2), g(BETA), ALU.mult).then_inc(s_vb[d], 1)
                        wait(pool, m_up[d], i - 1)
                        nc.gpsimd.tensor_tensor(h4(kd[d][:, u, :]), part(1), g(EKD), ALU.mult).then_inc(s_kd[d], 1)
                        nc.gpsimd.tensor_tensor(h4(kb[d][:, u, :]), part(1), g(BETA), ALU.mult).then_inc(s_kb[d], 1)
                        nc.gpsimd.tensor_tensor(h4(qg[d][:, u, :]), part(0), g(EGC), ALU.mult).then_inc(s_qg[d], 1)
                        nc.gpsimd.tensor_tensor(h4(gt[d][:, u, :]), tri[:, d:d + 1, :].to_broadcast([P, H, P]), g(G_),
                                                ALU.mult).then_inc(s_gt[d], 1)
                    for L in range(LEVELS):
                        for d in D2:
                            if L == 0:
                                wait(pool, at_[d], i + 1)
                                wait(pool, m_w[d], i)
                            nc.gpsimd.tensor_tensor(h4(CT[d][:, L, :]), h4(AT[d][:, :]),
                                                    lev[:, 1 - d, L:L + 1, :].to_broadcast([P, H, P]), ALU.mult).then_inc(ct[d], 1)
                            if L == 0:
                                wait(pool, ct[d], LEVELS * i + 1)
                                wait(pool, m_new[d], i)
                                nc.gpsimd.tensor_tensor(h4(XT[d][:, :]), ident[:, :].unsqueeze(1).to_broadcast([P, H, P]),
                                                        h4(CT[d][:, 0, :]), ALU.subtract).then_inc(xt0[d], 1)
                repeat(pool, NT, step)

            @block.tensor
            def _(pe):
                pe.wait_ge(const, 64)
                pe.wait_ge(zero, 2)

                def heads(bank, lhsT, rhs, start=True, stop=True):
                    for h in range(H):
                        last = nc.tensor.matmul(bank[:, hd(h)], lhsT[:, hd(h)], rhs[:, hd(h)], start=start, stop=stop)
                    return last

                def turn(bank, src):
                    for h in range(H):
                        last = nc.tensor.transpose(bank[:, hd(h)], src[:, hd(h)], ident[:, :])
                    return last

                def step(j, u):
                    i = 2 * j + u
                    for d in D2:
                        b = ps[d]
                        wait(pe, ld[d][u], 16 * (j + 1))
                        wait(pe, o_[d], i)
                        turn(b[:, 0, :], x[d][:, u, DN:2 * DN]).then_inc(m_kT[d], 1)
                        wait(pe, s_kb[d], i + 1)
                        wait(pe, s_[d], i)
                        turn(b[:, 1, :], kb[d][:, u, :]).then_inc(m_kbT[d], 1)
                        wait(pe, s_qg[d], i + 1)
                        wait(pe, r_[d], i)
                        turn(b[:, 3, :], qg[d][:, u, :]).then_inc(m_qgT[d], 1)
                        wait(pe, vn_[d], i)
                        turn(b[:, 2, :], x[d][:, u, 0:DN]).then_inc(m_qT[d], 1)
                    for d in D2:
                        b = ps[d]
                        wait(pe, kT_in[d], i + 1)
                        wait(pe, s_gt[d], i + 1)
                        nc.tensor.matmul(b[:, 0, :], tri[:, 2, :], gt[d][:, u, :], start=True, stop=True).then_inc(m_gc[d], 1)
                        wait(pe, kbT_in[d], i + 1)
                        heads(b[:, 1, :], KT_[d], KBT[d]).then_inc(m_kk[d], 1)
                        wait(pe, qT_in[d], i + 1)
                        heads(b[:, 2, :], KT_[d], QT[d]).then_inc(m_qk[d], 1)
                    for d in D2:
                        wait(pe, ct[d], LEVELS * i + 1)
                        wait(pe, qgT_in[d], i + 1)
                        turn(ps[d][:, 3, :], CT[d][:, 0, :]).then_inc(m_a[d], 1)
                    for L in range(NL):
                        n = NL * i + L
                        for d in D2:
                            if L == 0:
                                wait(pe, x0[d], i + 1)
                                wait(pe, at_[d], i + 1)
                                wait(pe, qkd_[d], i + 1)
                            else:
                                wait(pe, xl_[d], (NL - 1) * i + L)
                            wait(pe, ct[d], LEVELS * i + L + 2)
                            heads(ps[d][:, 0, :], CT[d][:, L + 1, :], X[d]).then_inc(m_ax[d], 1)
                        for d in D2:
                            wait(pe, pl[d], n + 1)
                            if L:
                                wait(pe, xtl[d], n)
                            else:
                                wait(pe, xt0[d], i + 1)
                            if L < NL - 1:
                                heads(ps[d][:, 1, :], XT[d], PM[d]).then_inc(m_xp[d], 1)
                            heads(ps[d][:, 2, :], PM[d], XT[d]).then_inc(m_px[d], 1)
                        if L == 0:
                            for d in D2:
                                wait(pe, s_[d], i)
                                heads(ps[d][:, 3, :], KT_[d], S[d]).then_inc(m_ks[d], 1)
                    for d in D2:
                        wait(pe, xtl[d], NL * (i + 1))
                        wait(pe, r_[d], i + 1)
                        heads(ps[d][:, 0, :], XT[d], R[d]).then_inc(m_u[d], 1)
                    for d in D2:
                        wait(pe, u_[d], i + 1)
                        wait(pe, xl_[d], (NL - 1) * (i + 1))
                        wait(pe, ct[d], LEVELS * (i + 1))
                        heads(ps[d][:, 1, :], CT[d][:, LEVELS - 1, :], U[d]).then_inc(m_w[d], 1)
                    for d in D2:
                        wait(pe, w_[d], i + 1)
                        heads(ps[d][:, 2, :], XT[d], W[d]).then_inc(m_new[d], 1)
                    for d in D2:
                        wait(pe, vn_[d], i + 1)
                        for h in range(H):
                            nc.tensor.matmul(ps[d][:, 0, hd(h)], QGT[d][:, hd(h)], S[d][:, hd(h)], start=True, stop=False)
                            last = nc.tensor.matmul(ps[d][:, 0, hd(h)], QKD[d][:, hd(h)], VN[d][:, hd(h)], start=False, stop=True)
                        last.then_inc(m_o[d], 1)
                        heads(ps[d][:, 1, :], kd[d][:, u, :], VN[d]).then_inc(m_up[d], 1)
                repeat(pe, NT, step)

            @block.scalar
            def _(act):
                def step(j, u):
                    i = 2 * j + u
                    for d in D2:
                        wait(act, m_kT[d], i + 1)
                        nc.scalar.activation(KT_[d][:, :], ps[d][:, 0, :], ACT.Copy).then_inc(kT_in[d], 1)
                        wait(act, m_qgT[d], i + 1)
                        nc.scalar.activation(QGT[d][:, :], ps[d][:, 3, :], ACT.Copy).then_inc(qgT_in[d], 1)
                        wait(act, m_qT[d], i + 1)
                        nc.scalar.activation(QT[d][:, :], ps[d][:, 2, :], ACT.Copy).then_inc(qT_in[d], 1)
                    for d in D2:
                        wait(act, arg[d], H * (i + 1))
                        nc.scalar.activation(E[d][:, :], E[d][:, :], ACT.Exp).then_inc(dec[d], 1)
                    for L in range(NL):
                        for d in D2:
                            wait(act, m_ax[d], NL * i + L + 1)
                            nc.scalar.activation(PM[d][:, :], ps[d][:, 0, :], ACT.Copy).then_inc(pl[d], 1)
                    for d in D2:
                        wait(act, m_u[d], i + 1)
                        nc.scalar.activation(U[d][:, :], ps[d][:, 0, :], ACT.Copy).then_inc(u_[d], 1)
                    for d in D2:
                        wait(act, m_w[d], i + 1)
                        nc.scalar.activation(W[d][:, :], ps[d][:, 1, :], ACT.Copy).then_inc(w_[d], 1)
                    for d in D2:
                        wait(act, stored[d][u], 16 * j)
                        wait(act, m_o[d], i + 1)
                        nc.scalar.activation(O[d][:, u, :], ps[d][:, 0, :], ACT.Copy).then_inc(o_[d], 1)
                        wait(act, o_[d], i + 1)
                        act.dma_start(o_dir[d][bass.ds(tile_of(d, j, u) * P, P), :], O[d][:, u, :]).then_inc(stored[d][u], 16)
                repeat(act, NT, step)
                for d in D2:
                    for u in D2:
                        act.wait_ge(stored[d][u], 16 * (NT // 2))

            @block.vector
            def _(dve):
                dve.wait_ge(const, 64)
                dve.wait_ge(zero, 2)

                def step(j, u):
                    i = 2 * j + u
                    c = lambda d, which, h: col[:, which, bass.ds(tile_of(d, j, u), 1), d * H + h:d * H + h + 1].rearrange("p a b -> p (a b)")
                    for d in D2:
                        wait(dve, m_kbT[d], i + 1)
                        nc.vector.tensor_copy(KBT[d][:, :], ps[d][:, 1, :]).then_inc(kbT_in[d], 1)
                    for d in D2:
                        wait(dve, m_gc[d], i + 1)
                        for h in range(H):
                            nc.vector.scalar_tensor_tensor(out=E[d][:, hd(h)], in0=ps[d][:, 0, hd(h)], scalar=c(d, GC, h),
                                                           in1=neg[:, d, :], op0=ALU.subtract, op1=ALU.add).then_inc(arg[d], 1)
                    for d in D2:
                        wait(dve, dec[d], i + 1)
                        wait(dve, m_kk[d], i + 1)
                        nc.vector.tensor_tensor(AT[d][:, :], ps[d][:, 1, :], E[d][:, :], ALU.mult).then_inc(at_[d], 1)
                        wait(dve, m_qk[d], i + 1)
                        nc.vector.tensor_tensor(QKD[d][:, :], ps[d][:, 2, :], E[d][:, :], ALU.mult).then_inc(qkd_[d], 1)
                    for d in D2:
                        wait(dve, m_a[d], i + 1)
                        nc.vector.tensor_tensor(h4(X[d][:, :]), ident[:, :].unsqueeze(1).to_broadcast([P, H, P]),
                                                h4(ps[d][:, 3, :]), ALU.subtract).then_inc(x0[d], 1)
                    for L in range(NL):
                        n = NL * i + L
                        for d in D2:
                            wait(dve, m_px[d], n + 1)
                            if L == 0:
                                wait(dve, x0[d], i + 1)
                            if L < NL - 1:
                                nc.vector.tensor_tensor(X[d][:, :], X[d][:, :], ps[d][:, 1, :], ALU.subtract).then_inc(xl_[d], 1)
                            nc.vector.tensor_tensor(XT[d][:, :], XT[d][:, :], ps[d][:, 2, :], ALU.subtract).then_inc(xtl[d], 1)
                        if L == 0:
                            for d in D2:
                                wait(dve, m_ks[d], i + 1)
                                wait(dve, s_vb[d], i + 1)
                                for h in range(H):
                                    last = nc.vector.scalar_tensor_tensor(out=R[d][:, hd(h)], in0=ps[d][:, 3, hd(h)],
                                                                          scalar=c(d, NBEG, h), in1=vb[d][:, u, hd(h)],
                                                                          op0=ALU.mult, op1=ALU.add)
                                last.then_inc(r_[d], 1)
                    for d in D2:
                        wait(dve, m_new[d], i + 1)
                        wait(dve, u_[d], i + 1)
                        nc.vector.tensor_tensor(VN[d][:, :], U[d][:, :], ps[d][:, 2, :], ALU.subtract).then_inc(vn_[d], 1)
                    for d in D2:
                        wait(dve, m_up[d], i + 1)
                        for h in range(H):
                            last = nc.vector.scalar_tensor_tensor(out=S[d][:, hd(h)], in0=S[d][:, hd(h)],
                                                                  scalar=c(d, ELAST, h), in1=ps[d][:, 1, hd(h)],
                                                                  op0=ALU.mult, op1=ALU.add)
                        last.then_inc(s_[d], 1)
                repeat(dve, NT, step)


NH, DH = 4, 64
KR = 8
DR = 2 * KR - 1


def attention(nc, tag, proj, rpb, ident_dram, onehot_dram, na_out, with_ctx):
    QR = [(0, 4, "low"), (4, 28, "mid"), (28, ROWS, "high")]
    NLOC, NK = KR * GRID, KR * GRID + CTX
    NCQ = CTX // GRID if with_ctx else 0
    with Phase(nc, tag) as ph:
        ident = ph.sb("ident", [P, P])
        hot = ph.sb("hot", [32, GRID, P])
        rp = ph.sb("rp", [32, NH * DR])
        bias = ph.sb("bias", [P, 2, DR, GRID])
        qT = ph.sb("qT", [P, 2, T])
        kT = ph.sb("kT", [P, 2, T])
        vT = ph.sb("vT", [P, 2, T])
        NV = CTX // GRID // 2 + (SEQ // GRID - 1)
        v = ph.sb("v", [P, NV, NH * DH])
        qd = ph.sb("qd", [P, 2, P])
        s = ph.sb("s", [P, 2, NK])
        pr = ph.sb("pr", [P, 2, NK])
        pT = ph.sb("pT", [P, 2, NK])
        m = ph.sb("m", [P, 2, 4])
        o = ph.sb("o", [P, 2, DH])
        oT = ph.sb("oT", [P, 2, T])
        ps = [ph.ps(f"ps{p}", [P, 4, 512]) for p in range(2)]
        ld, zero, pre_pe, pre_v = ph.sem("ld"), ph.sem("zero"), ph.sem("pre_pe"), ph.sem("pre_v")
        pre_a = ph.sem("pre_a")
        sems = lambda name: [ph.sem(f"{name}{p}") for p in range(2)]
        staged, scored, biased, ctx_s, mx, negm, expd = (sems(x) for x in
            ("staged", "scored", "biased", "ctx_s", "mx", "negm", "expd"))
        turned, pt_a, pt_v, attended, inv, scaled = (sems(x) for x in
            ("turned", "pt_a", "pt_v", "attended", "inv", "scaled"))
        oturned, outp = ph.sem("oturned"), ph.sem("outp")
        st = ph.sem("st")
        SC = DH ** -0.5
        with nc.Block() as block:

            @block.sync
            def _(sp):
                sp.dma_start(ident[:, :], ident_dram).then_inc(ld, 16)
                sp.dma_start(hot[:, :, :], onehot_dram).then_inc(ld, 16)
                sp.wait_ge(zero, 1)
                sp.dma_start(rp[0:31, :], rpb.rearrange("h a b -> b (h a)"), allow_slow_non_contiguous=True).then_inc(ld, 16)
                for t_, c in ((qT, C_NAQ), (kT, C_NAK), (vT, C_NAV)):
                    sp.dma_start(t_[:, :, :], proj[c:c + 2 * P, :].rearrange("(f p) t -> p f t", p=P)).then_inc(ld, 16)
                sp.wait_ge(outp, ROWS + NCQ)
                lo = 0 if with_ctx else CTX
                for p in range(2):
                    for h in range(2):
                        r = (2 * p + h) * DH
                        sp.dma_start(na_out[r:r + DH, lo:T], oT[p * DH:(p + 1) * DH, h, lo:T]).then_inc(st, 16)
                sp.wait_ge(st, 64)

            def steps(eng, body):
                def both(i, q0):
                    for p in range(2):
                        body(i, q0, p)
                both(0, CTX)
                with eng.Fori(1, ROWS) as i:
                    both(i, i * GRID + CTX)
                for n in range(NCQ):
                    both(ROWS + n, n * GRID)

            @block.gpsimd
            def _(pool):
                nc.gpsimd.memset(rp[0:32, :], 1.0).then_inc(zero, 1)
                nc.gpsimd.memset(qd[:, :, :], 0.0).then_inc(zero, 1)
                pool.wait_ge(zero, 2)
                pool.wait_ge(ld, 96)

                def row(i, q0, p):
                    wait(pool, scored[p], i)
                    for h in range(2):
                        last = nc.gpsimd.tensor_copy(qd[h * DH:(h + 1) * DH, p, h * GRID:(h + 1) * GRID],
                                                     qT[h * DH:(h + 1) * DH, p, bass.ds(q0, GRID)])
                    last.then_inc(staged[p], 1)
                steps(pool, row)

            @block.tensor
            def _(pe):
                pe.wait_ge(ld, 96)
                pe.wait_ge(pre_a, 1)
                for c in range(GRID):
                    if c >= 8:
                        pe.wait_ge(pre_v, c - 7)
                    nc.tensor.matmul(ps[c // 4 % 2][:, c % 4, 0:NH * DR], hot[:, c, :], rp[:, :], start=True, stop=True).then_inc(pre_pe, 1)
                for w in range(NV):
                    t0 = w * P if w < 2 else CTX + (w - 2) * GRID
                    pe.wait_ge(pre_v, GRID + w - 7)
                    for f in range(2):
                        last = nc.tensor.transpose(ps[w // 4 % 2][:, w % 4, f * P:(f + 1) * P], vT[:, f, t0:t0 + P], ident[:, :])
                    last.then_inc(pre_pe, 1)
                pe.wait_ge(pre_v, GRID + NV)

                def one(i, band, ctx_only):
                    nt = 2 if ctx_only else 6
                    for p in range(2):
                        wait(pe, staged[p], i + 1)
                        if not ctx_only:
                            wait(pe, biased[p], i)
                            nc.tensor.matmul(ps[p][:, 0, :], qd[:, p, :], kT[:, p, bass.ds(band * GRID + CTX, NLOC)], start=True, stop=True)
                        wait(pe, ctx_s[p], i)
                        nc.tensor.matmul(ps[p][:, 1, 0:CTX], qd[:, p, :], kT[:, p, 0:CTX], start=True, stop=True).then_inc(scored[p], 1)
                    for p in range(2):
                        wait(pe, expd[p], i + 1)
                        wait(pe, pt_a[p], i)
                        wait(pe, pt_v[p], i)
                        if p == 0:
                            wait(pe, outp, i)
                        for c in range(6 - nt, 6):
                            last = nc.tensor.transpose(ps[p][:, 2 + c // 4, (c % 4) * P:(c % 4 + 1) * P],
                                                       pr[:, p, c * P:(c + 1) * P], ident[:, :])
                        last.then_inc(turned[p], 1)
                    for p in range(2):
                        wait(pe, pt_a[p], i + 1)
                        wait(pe, pt_v[p], i + 1)
                        wait(pe, scaled[p], 2 * i)
                        for c in range(6 - nt, 6):
                            if c < 4:
                                rhs = v[:, bass.ds(band + (2 + 2 * c), 1), p * P:(p + 1) * P].rearrange("k a e -> k (a e)")
                            else:
                                rhs = v[:, c - 4, p * P:(p + 1) * P]
                            last = nc.tensor.matmul(ps[p][:, 3, 256:384], pT[:, p, c * P:(c + 1) * P], rhs,
                                                    start=(c == 6 - nt), stop=(c == 5))
                        last.then_inc(attended[p], 1)
                    for p in range(2):
                        wait(pe, scaled[p], 2 * (i + 1))
                    nc.tensor.transpose(ps[0][:, 3, 384:512], o[:, :, :].rearrange("q p e -> q (p e)"), ident[:, :]).then_inc(oturned, 1)

                one(0, 0, False)
                with pe.Fori(1, 4) as i:
                    one(i, 0, False)
                with pe.Fori(4, ROWS - 4) as i:
                    one(i, i + -4, False)
                with pe.Fori(ROWS - 4, ROWS) as i:
                    one(i, ROWS - KR, False)
                for n in range(NCQ):
                    one(ROWS + n, 0, True)

            @block.scalar
            def _(act):
                act.wait_ge(zero, 1)
                act.wait_ge(ld, 96)
                nc.scalar.activation(rp[0:1, 0:1], rp[0:1, 0:1], ACT.Copy).then_inc(pre_a, 1)

                def row(i, q0, p, ctx_only=False):
                    lo = NLOC if ctx_only else 0
                    wait(act, scored[p], i + 1)
                    wait(act, expd[p], i)
                    nc.scalar.activation(s[:, p, NLOC:NK], ps[p][:, 1, 0:CTX], ACT.Copy, scale=SC).then_inc(ctx_s[p], 1)
                    wait(act, negm[p], i + 1)
                    wait(act, turned[p], i)
                    nc.scalar.activation(pr[:, p, lo:NK], s[:, p, lo:NK], ACT.Exp, bias=m[:, p, 1:2],
                                         accum_out=m[:, p, 2:3]).then_inc(expd[p], 1)

                def evac(i, p, ctx_only=False):
                    wait(act, turned[p], i + 1)
                    wait(act, attended[p], i)
                    if ctx_only:
                        nc.scalar.activation(m[:, p, 3:4], m[:, p, 2:3], ACT.Copy).then_inc(pt_a[p], 1)
                    else:
                        nc.scalar.activation(pT[:, p, 0:NLOC], ps[p][:, 2, :], ACT.Copy).then_inc(pt_a[p], 1)

                def both(i, ctx_only=False):
                    for p in range(2):
                        row(i, None, p, ctx_only)
                    for p in range(2):
                        evac(i, p, ctx_only)
                both(0)
                with act.Fori(1, ROWS) as i:
                    both(i)
                for n in range(NCQ):
                    both(ROWS + n, True)

            @block.vector
            def _(dve):
                for c in range(GRID):
                    dve.wait_ge(pre_pe, c + 1)
                    for hh in range(2):
                        last = nc.vector.tensor_copy(
                            bias[hh * GRID:(hh + 1) * GRID, :, :, c],
                            ps[c // 4 % 2][hh * GRID:(hh + 1) * GRID, c % 4, 0:NH * DR].rearrange("q (a h d) -> q a h d", a=2, h=2)[:, :, hh, :])
                    last.then_inc(pre_v, 1)
                for w in range(NV):
                    dve.wait_ge(pre_pe, GRID + w + 1)
                    nc.vector.tensor_copy(v[:, w, :], ps[w // 4 % 2][:, w % 4, 0:NH * DH]).then_inc(pre_v, 1)
                dve.wait_ge(pre_v, GRID + NV)

                def one(i, q0, dr0, ctx_only=False):
                    lo = NLOC if ctx_only else 0
                    for p in range(2):
                        wait(dve, scored[p], i + 1)
                        wait(dve, expd[p], i)
                        if not ctx_only:
                            nc.vector.scalar_tensor_tensor(
                                out=s[:, p, 0:NLOC], in0=ps[p][:, 0, :], scalar=SC,
                                in1=bias[:, p, bass.ds(dr0, KR), :].rearrange("q a b -> q (a b)"),
                                op0=ALU.mult, op1=ALU.add).then_inc(biased[p], 1)
                            wait(dve, biased[p], i + 1)
                        wait(dve, ctx_s[p], i + 1)
                        nc.vector.tensor_reduce(out=m[:, p, 0:1], in_=s[:, p, lo:NK], axis=AX.X, op=ALU.max).then_inc(mx[p], 1)
                        wait(dve, mx[p], i + 1)
                        nc.vector.tensor_scalar(m[:, p, 1:2], m[:, p, 0:1], -1.0, None, ALU.mult).then_inc(negm[p], 1)
                    for p in range(2):
                        wait(dve, turned[p], i + 1)
                        wait(dve, attended[p], i)
                        nc.vector.tensor_copy(pT[:, p, NLOC:NK], ps[p][:, 3, 0:CTX]).then_inc(pt_v[p], 1)
                        nc.vector.reciprocal(m[:, p, 3:4] if not ctx_only else m[:, p, 0:1], m[:, p, 2:3]).then_inc(inv[p], 1)
                    for p in range(2):
                        wait(dve, attended[p], i + 1)
                        wait(dve, inv[p], i + 1)
                        wait(dve, oturned, i)
                        rv = m[:, p, 3:4] if not ctx_only else m[:, p, 0:1]
                        for h in range(2):
                            sl = slice(h * GRID, (h + 1) * GRID)
                            nc.vector.tensor_scalar(o[sl, p, :], ps[p][sl, 3, 256 + h * DH:256 + (h + 1) * DH], rv[sl, :], None,
                                                    ALU.mult).then_inc(scaled[p], 1)
                    wait(dve, oturned, i + 1)
                    nc.vector.tensor_copy(oT[:, :, bass.ds(q0, GRID)],
                                          ps[0][:, 3, 384:512].rearrange("e (h q) -> e h q", h=2)).then_inc(outp, 1)

                one(0, CTX, KR - 1)
                with dve.Fori(1, 4) as i:
                    one(i, i * GRID + CTX, i * -1 + (KR - 1))
                with dve.Fori(4, ROWS - 4) as i:
                    one(i, i * GRID + CTX, 3)
                with dve.Fori(ROWS - 4, ROWS) as i:
                    one(i, i * GRID + CTX, i * -1 + (ROWS - 1))
                for n in range(NCQ):
                    one(ROWS + n, n * GRID, 0, True)


def output_tiles(nc, tag, tiles, proj, na, o_dir, hy, norm_w, w_out, gate_dram, mod_of, ident_dram, resid, dest):
    t_lo, t_hi = tiles
    n = t_hi - t_lo
    with Phase(nc, tag) as ph:
        ident = ph.sb("ident", [P, P])
        wo = ph.sb("wo", [P, KT, D])
        nw = ph.sb("nw", [P, P])
        gg = ph.sb("gg", [P, D])
        z = ph.sb("z", [P, 2, KT, P])
        mix = ph.sb("mix", [P, 2, KT, P])
        x = ph.sb("x", [P, 2, D])
        of, ob = ph.sb("of", [P, 2, DN]), ph.sb("ob", [P, 2, DN])
        osum = ph.sb("osum", [P, DN])
        on = ph.sb("on", [P, 2, DN])
        sq = ph.sb("sq", [P, D])
        sq4 = ph.sb("sq4", [P, DN])
        c4 = ph.sb("c4", [P, 4, H])
        c1 = ph.sb("c1", [P, 4])
        y = ph.sb("y", [P, D])
        out = ph.sb("out", [P, 2, D])
        psT = ph.ps("psT", [P, 2, 512])
        psY = ph.ps("psY", [P, 2, 2, 512])
        const = ph.sem("const")
        ld, stored = [ph.sem("ld0"), ph.sem("ld1")], [ph.sem("so0"), ph.sem("so1")]
        (summed, sq_o, chain, rt4, normed, turned, zs, gated, prod, sq_y, chain1, rt1, scaled, added) = (ph.sem(s) for s in
            ("summed", "sq_o", "chain", "rt4", "normed", "turned", "zs", "gated", "prod", "sq_y", "chain1", "rt1", "scaled", "added"))
        inv_y, inv_, gdn = ph.sem("inv_y"), ph.sem("inv"), ph.sem("gdn")
        with nc.Block() as block:

            @block.sync
            def _(sp):
                sp.dma_start(ident[:, :], ident_dram).then_inc(const, 16)
                sp.dma_start(wo[:, :, :], w_out.rearrange("(k p) n -> p k n", p=P)).then_inc(const, 16)
                sp.dma_start(nw[:, :], norm_w.partition_broadcast(P)).then_inc(const, 16)
                sp.dma_start(gg[:, :], gate_dram[mod_of].partition_broadcast(P)).then_inc(const, 16)

                def load(j, u):
                    i = 2 * j + u
                    tok = at(sp, (i + t_lo) * P)
                    row = at(sp, i * P)
                    wait(sp, added, i - 1)
                    fm = lambda ap, c, k: ap[c:c + k * P, bass.ds(tok, P)].rearrange("(f p) t -> p f t", p=P)
                    sp.dma_start(z[:, u, 0:2, :], fm(proj, C_NAZ, 2)).then_inc(ld[u], 16)
                    sp.dma_start(z[:, u, 2:8, :][:, 0:4, :], fm(proj, C_DNZ, 4)).then_inc(ld[u], 16)
                    sp.dma_start(z[:, u, 6:8, :], fm(proj, C_HYZ, 2)).then_inc(ld[u], 16)
                    sp.dma_start(mix[:, u, 0:2, :], fm(na, 0, 2)).then_inc(ld[u], 16)
                    sp.dma_start(mix[:, u, 6:8, :], fm(hy, 0, 2)).then_inc(ld[u], 16)
                    sp.dma_start(of[:, u, :], o_dir[0][bass.ds(tok, P), :]).then_inc(ld[u], 16)
                    sp.dma_start(ob[:, u, :], o_dir[1][bass.ds(tok, P), :]).then_inc(ld[u], 16)
                    sp.dma_start(x[:, u, :], resid[bass.ds(row, P), :]).then_inc(ld[u], 16)
                repeat(sp, n, load)

            @block.gpsimd
            def _(pool):
                pool.wait_ge(const, 64)

                def tile(j, u):
                    i = 2 * j + u
                    wait(pool, ld[u], 128 * (j + 1))
                    wait(pool, normed, 2 * i)
                    nc.gpsimd.tensor_tensor(osum[:, :], of[:, u, :], ob[:, u, :], ALU.add).then_inc(summed, 1)
                    wait(pool, zs, i + 1)
                    nc.gpsimd.tensor_tensor(mix[:, u, 0:2, :], mix[:, u, 0:2, :], z[:, u, 0:2, :], ALU.mult)
                    nc.gpsimd.tensor_tensor(mix[:, u, 6:8, :], mix[:, u, 6:8, :], z[:, u, 6:8, :], ALU.mult).then_inc(gated, 1)
                    if not (isinstance(i, int) and i == 0):
                        finish(i + -1, j - 1 if u == 0 and isinstance(j, int) else j + (u - 1), 1 - u)

                def finish(i, j, u):
                    wait(pool, scaled, i + 1)
                    wait(pool, stored[u], 16 * j)
                    nc.gpsimd.tensor_tensor(out[:, u, :], x[:, u, :], y[:, :], ALU.add).then_inc(added, 1)
                repeat(pool, n, tile)
                finish(n - 1, n // 2 - 1, 1)

            @block.scalar
            def _(act):
                def tile(j, u):
                    i = 2 * j + u
                    wait(act, ld[u], 128 * (j + 1))
                    nc.scalar.activation(z[:, u, :, :], z[:, u, :, :], ACT.Silu).then_inc(zs, 1)
                    wait(act, summed, i + 1)
                    wait(act, chain, 2 * i)
                    nc.scalar.activation(sq4[:, :], osum[:, :], ACT.Square).then_inc(sq_o, 1)
                    wait(act, chain, 2 * (i + 1))
                    nc.scalar.activation(c4[:, 2, :], c4[:, 1, :], ACT.Sqrt).then_inc(rt4, 1)
                    if not (isinstance(i, int) and i == 0):
                        squares(i + -1, 1 - u)
                    if not isinstance(i, int):
                        store(i + -2, u)

                def squares(i, u):
                    wait(act, prod, i + 1)
                    wait(act, chain1, i)
                    nc.scalar.activation(sq[:, :], psY[:, u, :, :].rearrange("p a b -> p (a b)"), ACT.Square,
                                         accum_out=c1[:, 0:1]).then_inc(sq_y, 1)
                    wait(act, chain1, i + 1)
                    nc.scalar.activation(c1[:, 2:3], c1[:, 1:2], ACT.Sqrt).then_inc(rt1, 1)

                def store(i, u):
                    wait(act, added, i + 1)
                    act.dma_start(dest[bass.ds(i * P, P), :], out[:, u, :]).then_inc(stored[u], 16)
                repeat(act, n, tile)
                squares(n - 1, 1)
                store(n - 2, 0)
                store(n - 1, 1)
                for u in range(2):
                    act.wait_ge(stored[u], 16 * (n // 2))

            @block.vector
            def _(dve):
                dve.wait_ge(const, 64)

                def tile(j, u):
                    i = 2 * j + u
                    wait(dve, sq_o, i + 1)
                    nc.vector.tensor_reduce(out=c4[:, 0, :], in_=sq4[:, :].rearrange("p (h e) -> p h e", e=P), axis=AX.X,
                                            op=ALU.add).then_inc(chain, 1)
                    wait(dve, chain, 2 * i + 1)
                    nc.vector.tensor_scalar(c4[:, 1, :], c4[:, 0, :], 1.0 / P, EPS, ALU.mult, ALU.add).then_inc(chain, 1)
                    wait(dve, rt4, i + 1)
                    nc.vector.reciprocal(c4[:, 3, :], c4[:, 2, :]).then_inc(inv_, 1)
                    wait(dve, inv_, i + 1)
                    wait(dve, turned, i - 1)
                    o4 = on[:, u, :].rearrange("p (h e) -> p h e", e=P)
                    nc.vector.tensor_tensor(o4, osum[:, :].rearrange("p (h e) -> p h e", e=P),
                                            c4[:, 3, :].unsqueeze(2).to_broadcast([P, H, P]), ALU.mult).then_inc(normed, 1)
                    wait(dve, normed, 2 * i + 1)
                    nc.vector.tensor_tensor(o4, o4, nw[:, :].unsqueeze(1).to_broadcast([P, H, P]), ALU.mult).then_inc(normed, 1)
                    wait(dve, turned, i + 1)
                    wait(dve, zs, i + 1)
                    nc.vector.tensor_tensor(mix[:, u, 2:6, :], psT[:, u, :].rearrange("p (h e) -> p h e", e=P),
                                            z[:, u, 2:6, :], ALU.mult).then_inc(gdn, 1)
                    if not (isinstance(i, int) and i == 0):
                        finish(i + -1, 1 - u)

                def finish(i, u):
                    wait(dve, sq_y, i + 1)
                    wait(dve, scaled, i)
                    nc.vector.tensor_scalar(c1[:, 1:2], c1[:, 0:1], 1.0 / D, EPS, ALU.mult, ALU.add).then_inc(chain1, 1)
                    wait(dve, rt1, i + 1)
                    nc.vector.reciprocal(c1[:, 3:4], c1[:, 2:3]).then_inc(inv_y, 1)
                    wait(dve, inv_y, i + 1)
                    wait(dve, added, i)
                    nc.vector.scalar_tensor_tensor(out=y[:, :], in0=psY[:, u, :, :].rearrange("p a b -> p (a b)"),
                                                   scalar=c1[:, 3:4], in1=gg[:, :], op0=ALU.mult, op1=ALU.mult).then_inc(scaled, 1)
                repeat(dve, n, tile)
                finish(n - 1, 1)
            
            @block.tensor
            def _(pe):
                pe.wait_ge(const, 64)

                def tile(j, u):
                    i = 2 * j + u
                    wait(pe, normed, 2 * (i + 1))
                    wait(pe, gdn, i - 1)
                    for h in range(H):
                        last = nc.tensor.transpose(psT[:, u, h * P:(h + 1) * P], on[:, u, h * P:(h + 1) * P], ident[:, :])
                    last.then_inc(turned, 1)
                    wait(pe, gdn, i + 1)
                    wait(pe, gated, i + 1)
                    wait(pe, scaled, i - 1)
                    for half in range(2):
                        for k in range(KT):
                            last = nc.tensor.matmul(psY[:, u, half, :], mix[:, u, k, :], wo[:, k, half * 512:(half + 1) * 512],
                                                    start=(k == 0), stop=(k == KT - 1))
                    last.then_inc(prod, 1)
                repeat(pe, n, tile)


HW = 256
HID, EMB = 64, 33
N1, N2 = 32, P
KS = N1 // 2 + 1
R0 = N1
ROUND = 1.5 * 2.0 ** 23
PI2_HI, PI2_LO = 6.28125, 2 * math.pi - 6.28125


def hyena_filters(nc, tag, feats, w1, b1, w2, b2, w3, b3, freq, wout, win, win_ctx, sums, sums_ctx):
    with Phase(nc, tag) as ph:
        z = ph.sb("z", [EMB, T])
        w = ph.sb("w", [HID, 3, HID])
        col = ph.sb("col", [HID, 2, 3])
        wo = ph.sb("wo", [HID, 4 * HW])
        hid = ph.sb("hid", [HID, T])
        y = ph.sb("y", [HID, T])
        k = ph.sb("k", [HID, T])
        wi = ph.sb("wi", [P, 2, SEQ])
        wc = ph.sb("wc", [P, 2, 2, HW])
        F, B = ph.sb("F", [P, SEQ]), ph.sb("B", [P, SEQ])
        sd = ph.sb("sd", [P, 2, SEQ])
        FB = ph.sb("FB", [P, 2, 2, HW])
        sc = ph.sb("sc", [P, 2, 2, 2, HW])
        ps = ph.ps("ps", [P, 8, 512])
        ld, zero, mm, v, sn, evf, evb, pool_s, st, stc = (ph.sem(s) for s in
            ("ld", "zero", "mm", "v", "sn", "evf", "evb", "pool", "st", "stc"))
        taps, evc, pc = ph.sem("taps"), ph.sem("evc"), ph.sem("pc")
        NC = len(CHUNKS)
        with nc.Block() as block:

            @block.sync
            def _(sp):
                sp.dma_start(z[:, :], feats).then_inc(ld, 16)
                for n, t in enumerate((w1, w2, w3)):
                    sp.dma_start(w[0:t.shape[0], n, :], t).then_inc(ld, 16)
                for n, t in enumerate((b1, b2, b3)):
                    sp.dma_start(col[:, 0, n:n + 1], t.unsqueeze(1), allow_slow_non_contiguous=True).then_inc(ld, 16)
                sp.dma_start(col[:, 1, :], freq.rearrange("n h -> h n"), allow_slow_non_contiguous=True).then_inc(ld, 16)
                sp.dma_start(wo[:, :], wout).then_inc(ld, 16)
                sp.dma_start(wi[:, :, :], win.rearrange("(f p) t -> p f t", p=P)).then_inc(ld, 16)
                sp.dma_start(wc[:, :, :, :], win_ctx.rearrange("(n p) d c -> p n d c", p=P)).then_inc(ld, 16)
                for g in range(4):
                    sp.wait_ge(pool_s, 2 * (g + 1))
                    for i in range(2):
                        sp.dma_start(sums[i, g * P:(g + 1) * P, :], sd[:, i, :]).then_inc(st, 16)
                for t in range(2):
                    sp.wait_ge(pc, 2 * (t + 1))
                    for i in range(2):
                        sp.dma_start(sums_ctx[t * P:(t + 1) * P, i, :], sc[:, t, i, :, :].rearrange("p o c -> p (o c)")).then_inc(stc, 16)
                sp.wait_ge(st, 128)
                sp.wait_ge(stc, 64)

            @block.tensor
            def _(pe):
                pe.wait_ge(ld, 16 * 11)
                for n in range(3):
                    for c, (t0, tn) in enumerate(CHUNKS):
                        if n:
                            pe.wait_ge(sn, NC * (n - 1) + c + 1)
                        rhs = (z if n == 0 else hid)
                        kk = EMB if n == 0 else HID
                        nc.tensor.matmul(ps[0:HID, c, 0:tn], w[0:kk, n, :], rhs[0:kk, t0:t0 + tn], start=True, stop=True).then_inc(mm, 1)
                pe.wait_ge(sn, 3 * NC)
                for g in range(4):
                    o, ct = g // 2, g % 2
                    for d in range(2):
                        pe.wait_ge(evf if d == 0 else evb, g) if g else None
                        for q in range(4):
                            c0 = (2 * o + d) * HW + ct * P
                            last = nc.tensor.matmul(ps[:, 4 * d + q, :], wo[:, c0:c0 + P],
                                                    hid[:, CTX + 512 * q:CTX + 512 * (q + 1)], start=True, stop=True)
                        last.then_inc(taps, 1)
                pe.wait_ge(evf, 4)
                pe.wait_ge(evb, 4)
                for t in range(2):
                    for q in range(2):
                        last = nc.tensor.matmul(ps[:, 2 * t + q, :], hid[:, t * P:(t + 1) * P], wo[:, q * 512:(q + 1) * 512],
                                                start=True, stop=True)
                    last.then_inc(taps, 1)

            @block.vector
            def _(dve):
                dve.wait_ge(ld, 16 * 11)
                dve.wait_ge(zero, 1)
                n_v = [0]

                def step(ins):
                    n_v[0] += 1
                    ins.then_inc(v, 1)
                    dve.wait_ge(v, n_v[0])
                for n in range(3):
                    for c, (t0, tn) in enumerate(CHUNKS):
                        sl = slice(t0, t0 + tn)
                        dve.wait_ge(mm, NC * n + c + 1)
                        step(nc.vector.tensor_scalar(y[:, sl], ps[0:HID, c, 0:tn], col[:, 0, n:n + 1], col[:, 1, n:n + 1],
                                                     ALU.add, ALU.mult))
                        step(nc.vector.tensor_scalar(k[:, sl], y[:, sl], 1 / (2 * math.pi), ROUND, ALU.mult, ALU.add))
                        step(nc.vector.tensor_scalar(k[:, sl], k[:, sl], ROUND, None, ALU.subtract))
                        step(nc.vector.scalar_tensor_tensor(out=y[:, sl], in0=k[:, sl], scalar=-PI2_HI, in1=y[:, sl],
                                                            op0=ALU.mult, op1=ALU.add))
                        step(nc.vector.scalar_tensor_tensor(out=y[:, sl], in0=k[:, sl], scalar=-PI2_LO, in1=y[:, sl],
                                                            op0=ALU.mult, op1=ALU.add))
                        step(nc.vector.tensor_scalar(y[:, sl], y[:, sl], 3.1415925, -3.1415925, ALU.min, ALU.max))
                for g in range(4):
                    dve.wait_ge(taps, 2 * g + 1)
                    dve.wait_ge(pool_s, 2 * g) if g else None
                    nc.vector.tensor_tensor(F[:, :], ps[:, 0:4, :].rearrange("p a b -> p (a b)"), wi[:, g % 2, :], ALU.mult).then_inc(evf, 1)
                    dve.wait_ge(taps, 2 * g + 2)
                    nc.vector.tensor_tensor(B[:, 1:], ps[:, 4:8, :].rearrange("p a b -> p (a b)")[:, 1:], wi[:, g % 2, 1:],
                                            ALU.mult).then_inc(evb, 1)
                for t in range(2):
                    dve.wait_ge(taps, 9 + t)
                    dve.wait_ge(pc, 2 * t) if t else None
                    nc.vector.tensor_tensor(FB[:, :, :, :], ps[:, 2 * t:2 * t + 2, :].rearrange("p o (d c) -> p o d c", d=2),
                                            wc[:, t, :, :].unsqueeze(1).to_broadcast([P, 2, 2, HW]), ALU.mult).then_inc(evc, 1)

            @block.scalar
            def _(act):
                for n in range(3):
                    for c, (t0, tn) in enumerate(CHUNKS):
                        act.wait_ge(v, 6 * (NC * n + c + 1))
                        nc.scalar.activation(hid[:, t0:t0 + tn], y[:, t0:t0 + tn], ACT.Sin).then_inc(sn, 1)

            @block.gpsimd
            def _(pool):
                nc.gpsimd.memset(B[:, 0:1], 0.0).then_inc(zero, 1)
                for g in range(4):
                    pool.wait_ge(evf, g + 1)
                    pool.wait_ge(evb, g + 1)
                    pool.wait_ge(st, 32 * g) if g else None
                    nc.gpsimd.tensor_tensor(sd[:, 0, :], F[:, :], B[:, :], ALU.add).then_inc(pool_s, 1)
                    nc.gpsimd.tensor_tensor(sd[:, 1, :], F[:, :], B[:, :], ALU.subtract).then_inc(pool_s, 1)
                for t in range(2):
                    pool.wait_ge(evc, t + 1)
                    nc.gpsimd.tensor_tensor(sc[:, t, 0, :, :], FB[:, :, 0, :], FB[:, :, 1, :], ALU.add).then_inc(pc, 1)
                    nc.gpsimd.tensor_tensor(sc[:, t, 1, :, :], FB[:, :, 0, :], FB[:, :, 1, :], ALU.subtract).then_inc(pc, 1)


GRP = 8


def kernel_spectrum(nc, tag, sums, tf_dram, bd_dram, spec):
    CH = 2 * HW
    NG = CH // 8
    with Phase(nc, tag) as ph:
        tf = ph.sb("tf", [P, KS, 3, P])
        bd = ph.sb("bd", [P, 8 * R0])
        U = ph.sb("U", [P, 2, GRP, P])
        A = ph.sb("A", [P, R0, CH])
        o = ph.sb("o", [P, 2, CH])
        ps = ph.ps("ps", [P, 8, 512])
        const, dft, mm = ph.sem("const"), ph.sem("dft"), ph.sem("mm")
        ld, stored = [ph.sem("ld0"), ph.sem("ld1")], [ph.sem("so0"), ph.sem("so1")]
        eva, evv, evh = ph.sem("eva"), ph.sem("evv"), ph.sem("evh")
        NR = NG // GRP
        with nc.Block() as block:

            @block.sync
            def _(sp):
                sp.dma_start(tf[:, :, :, :], tf_dram).then_inc(const, 16)
                sp.dma_start(bd[:, :], bd_dram).then_inc(const, 16)
                for w in range(2):
                    view = sums[w].rearrange("c (n1 n2) -> (c n1) n2", n2=P).rearrange("(g p) n -> p g n", p=P)

                    def load(j, u):
                        g0 = at(sp, (2 * j + u - w * NR) * GRP)
                        wait(sp, dft, 2 * j + u - 1)
                        sp.dma_start(U[:, u, :, :], view[:, bass.ds(g0, GRP), :]).then_inc(ld[u], 16)
                    repeat(sp, (w + 1) * NR, load, lo=w * NR)

            @block.tensor
            def _(pe):
                pe.wait_ge(const, 32)
                for w in range(2):
                    def groups(j, u):
                        i = 2 * j + u
                        wait(pe, ld[u], 16 * (j + 1))
                        wait(pe, eva, 2 * i)
                        wait(pe, evv, 2 * i)
                        for g in range(GRP):
                            last = nc.tensor.matmul(ps[:, g // 2, (g % 2) * 256:(g % 2 + 1) * 256], U[:, u, g, :], bd[:, :],
                                                    start=True, stop=True)
                        last.then_inc(dft, 1)
                    repeat(pe, (w + 1) * NR, groups, lo=w * NR)
                    pe.wait_ge(eva, 2 * (w + 1) * NR)
                    pe.wait_ge(evv, 2 * (w + 1) * NR)
                    for k1 in range(KS):
                        n = w * KS + k1
                        real = k1 in (0, KS - 1)
                        if n >= 4:
                            pe.wait_ge(evh, n - 3)
                        bank = ps[:, 4 + n % 4, :]
                        re, im = A[:, k1, :], None if real else A[:, KS - 1 + k1, :]
                        if w == 0:
                            last = nc.tensor.matmul(bank, tf[:, k1, 0, :], re, start=True, stop=real)
                            if not real:
                                last = nc.tensor.matmul(bank, tf[:, k1, 1, :], im, start=False, stop=True)
                        else:
                            last = nc.tensor.matmul(bank, tf[:, k1, 2, :], re, start=True, stop=real)
                            if not real:
                                last = nc.tensor.matmul(bank, tf[:, k1, 0, :], im, start=False, stop=True)
                        last.then_inc(mm, 1)

            def copy_groups(eng, ins, sem, banks, w):
                def go(j, u):
                    i = 2 * j + u
                    wait(eng, dft, i + 1)
                    if w:
                        wait(eng, mm, w * KS)
                    for b in banks:
                        c0 = (i - w * NR) * 8 * GRP + 16 * b
                        ins(A[:, :, bass.ds(c0, 16)].rearrange("p r c -> p c r"),
                            ps[:, b, :].rearrange("p (c r) -> p c r", r=R0)).then_inc(sem, 1)
                repeat(eng, (w + 1) * NR, go, lo=w * NR)

            @block.scalar
            def _(act):
                for w in range(2):
                    copy_groups(act, lambda o_, i_: nc.scalar.activation(o_, i_, ACT.Copy), eva, (0, 1), w)
                    for k1 in range(KS):
                        n = w * KS + k1
                        act.wait_ge(evh, n + 1)
                        act.dma_start(spec[:, k1, :, w, :].rearrange("o k c -> k o c"),
                                      o[:, n % 2, :].rearrange("k (o c) -> k o c", o=2)).then_inc(stored[n % 2], 16)
                act.wait_ge(stored[0], 16 * KS)
                act.wait_ge(stored[1], 16 * KS)

            @block.vector
            def _(dve):
                for w in range(2):
                    copy_groups(dve, nc.vector.tensor_copy, evv, (2, 3), w)
                    for k1 in range(KS):
                        n = w * KS + k1
                        dve.wait_ge(mm, n + 1)
                        if n >= 2:
                            dve.wait_ge(stored[n % 2], 16 * (n // 2))
                        nc.vector.tensor_copy(o[:, n % 2, :], ps[:, 4 + n % 4, :]).then_inc(evh, 1)


def long_conv(nc, tag, src, spec, tf_dram, ti_dram, bd_dram, bi_dram, ident_dram, dst):
    NG = HW // 8
    NR = NG // GRP
    with Phase(nc, tag) as ph:
        ident = ph.sb("ident", [P, P])
        tf = ph.sb("tf", [P, KS, 3, P])
        ti = ph.sb("ti", [P, KS, 3, P])
        bd = ph.sb("bd", [P, 8 * R0])
        bi = ph.sb("bi", [P, 64])
        U = ph.sb("U", [P, 2, GRP, P])
        A = ph.sb("A", [P, R0, HW])
        Bt = ph.sb("Bt", [P, HW, R0])
        h = ph.sb("h", [P, 3, 2, HW])
        m1, m2 = ph.sb("m1", [P, 2, 2, HW]), ph.sb("m2", [P, 2, 2, HW])
        Y = ph.sb("Y", [P, 2, 2, HW])
        W = ph.sb("W", [P, 2, 512])
        yo = ph.sb("yo", [64, 2, 512])
        ps = ph.ps("ps", [P, 8, 512])
        bdl, const, dft, mx, mb = ph.sem("bdl"), ph.sem("const"), ph.sem("dft"), ph.sem("mx"), ph.sem("mb")
        ld, stored = [ph.sem("ld0"), ph.sem("ld1")], [ph.sem("so0"), ph.sem("so1")]
        hl = [ph.sem(f"hl{i}") for i in range(3)]
        eva, evv, prod, comb, bev = ph.sem("eva"), ph.sem("evv"), ph.sem("prod"), ph.sem("comb"), ph.sem("bev")
        tt, wv, yy, yv = ph.sem("tt"), ph.sem("wv"), ph.sem("yy"), ph.sem("yv")
        view = src.rearrange("c (n1 n2) -> (c n1) n2", n2=P).rearrange("(g p) n -> p g n", p=P)
        out = dst.rearrange("c (n1 n2) -> (c n1) n2", n2=P).rearrange("(q g p) n -> q p g n", g=4, p=64)
        NQ = HW // 16
        with nc.Block() as block:

            @block.sync
            def _(sp):
                sp.dma_start(bd[:, :], bd_dram).then_inc(bdl, 16)

                def load(j, u):
                    g0 = at(sp, (2 * j + u) * GRP)
                    wait(sp, dft, 2 * j + u - 1)
                    sp.dma_start(U[:, u, :, :], view[:, bass.ds(g0, GRP), :]).then_inc(ld[u], 16)
                repeat(sp, NR, load)
                for k1 in range(KS):
                    if k1 >= 3:
                        sp.wait_ge(prod, 2 * (k1 - 2))
                    sp.dma_start(h[:, k1 % 3, :, :], spec[k1]).then_inc(hl[k1 % 3], 16)
                for q in range(NQ):
                    sp.wait_ge(yv, q + 1)
                    sp.dma_start(out[q], yo[:, q % 2, :].rearrange("p (g n) -> p g n", n=P)).then_inc(stored[q % 2], 16)
                sp.wait_ge(stored[0], 16 * (NQ // 2))
                sp.wait_ge(stored[1], 16 * (NQ // 2))

            @block.gpsimd
            def _(pool):
                for k1 in range(KS):
                    u = k1 % 2
                    pool.wait_ge(prod, 2 * (k1 + 1))
                    if k1 >= 2:
                        pool.wait_ge(mb, k1 - 1)
                    nc.gpsimd.tensor_tensor(Y[:, u, 0, :], m1[:, u, 0, :], m2[:, u, 1, :], ALU.subtract).then_inc(comb, 1)
                    nc.gpsimd.tensor_tensor(Y[:, u, 1, :], m1[:, u, 1, :], m2[:, u, 0, :], ALU.add).then_inc(comb, 1)

            @block.tensor
            def _(pe):
                pe.wait_ge(bdl, 16)

                def groups(j, u):
                    i = 2 * j + u
                    wait(pe, ld[u], 16 * (j + 1))
                    wait(pe, eva, 2 * i)
                    wait(pe, evv, 2 * i)
                    for g in range(GRP):
                        last = nc.tensor.matmul(ps[:, g // 2, (g % 2) * 256:(g % 2 + 1) * 256], U[:, u, g, :], bd[:, :],
                                                start=True, stop=True)
                    last.then_inc(dft, 1)
                repeat(pe, NR, groups)
                pe.wait_ge(eva, 2 * NR)
                pe.wait_ge(evv, 2 * NR)

                def pair(bank, table, k1, re, im, terms):
                    for half in range(2):
                        ts = [(m, x) for m, x in terms[half] if x is not None]
                        for n, (m, x) in enumerate(ts):
                            last = nc.tensor.matmul(bank[:, half * HW:(half + 1) * HW], table[:, k1, m, :], x,
                                                    start=(n == 0), stop=(n == len(ts) - 1))
                    return last

                def fwd(k1):
                    real = k1 in (0, KS - 1)
                    if k1 >= 2:
                        pe.wait_ge(prod, 2 * (k1 - 1))
                    re, im = A[:, k1, :], None if real else A[:, KS - 1 + k1, :]
                    pair(ps[:, 4 + k1 % 2, :], tf, k1, re, im, [[(0, re), (1, im)], [(0, im), (2, re)]]).then_inc(mx, 1)

                def inv(k1):
                    pe.wait_ge(comb, 2 * (k1 + 1))
                    if k1 >= 2:
                        pe.wait_ge(bev, k1 - 1)
                    re, im = Y[:, k1 % 2, 0, :], Y[:, k1 % 2, 1, :]
                    real = k1 in (0, KS - 1)
                    second = [(1, re), (0, im)]
                    bank = ps[:, 6 + k1 % 2, :]
                    if real:
                        nc.tensor.matmul(bank[:, 0:HW], ti[:, k1, 0, :], re, start=True, stop=False)
                        nc.tensor.matmul(bank[:, 0:HW], ti[:, k1, 2, :], im, start=False, stop=True).then_inc(mb, 1)
                    else:
                        pair(bank, ti, k1, re, im, [[(0, re), (2, im)], second]).then_inc(mb, 1)
                pe.wait_ge(const, 64)
                fwd(0)
                for k1 in range(KS):
                    if k1 + 1 < KS:
                        fwd(k1 + 1)
                    inv(k1)
                pe.wait_ge(bev, KS)

                def turn(q):
                    if q >= 2:
                        pe.wait_ge(wv, q - 1)
                    for g in range(4):
                        c0 = (4 * q + g) * 4
                        last = nc.tensor.transpose(ps[:, q % 2, g * P:(g + 1) * P],
                                                   Bt[:, c0:c0 + 4, :].rearrange("p c r -> p (c r)"), ident[:, :])
                    last.then_inc(tt, 1)
                turn(0)
                for q in range(NQ):
                    if q + 1 < NQ:
                        turn(q + 1)
                    pe.wait_ge(wv, q + 1)
                    if q >= 2:
                        pe.wait_ge(yv, q - 1)
                    nc.tensor.matmul(ps[0:64, 2 + q % 2, :], bi[:, :], W[:, q % 2, :], start=True, stop=True).then_inc(yy, 1)

            def copy_groups(eng, ins, sem, banks):
                def go(j, u):
                    i = 2 * j + u
                    wait(eng, dft, i + 1)
                    for b in banks:
                        ins(A[:, :, bass.ds(i * 8 * GRP + 16 * b, 16)].rearrange("p r c -> p c r"),
                            ps[:, b, :].rearrange("p (c r) -> p c r", r=R0)).then_inc(sem, 1)
                repeat(eng, NR, go)

            @block.scalar
            def _(act):
                for dst_, src_ in ((tf, tf_dram), (ti, ti_dram), (bi, bi_dram), (ident, ident_dram)):
                    act.dma_start(dst_[:], src_).then_inc(const, 16)
                copy_groups(act, lambda o_, i_: nc.scalar.activation(o_, i_, ACT.Copy), eva, (0, 1))
                for k1 in range(KS):
                    act.wait_ge(mb, k1 + 1)
                    if k1 in (0, KS - 1):
                        nc.scalar.activation(Bt[:, :, k1], ps[:, 6 + k1 % 2, 0:HW], ACT.Copy).then_inc(bev, 1)
                    else:
                        nc.scalar.activation(Bt[:, :, k1:k1 + KS:KS - 1].rearrange("p c z -> p z c"),
                                             ps[:, 6 + k1 % 2, :].rearrange("p (z c) -> p z c", z=2), ACT.Copy).then_inc(bev, 1)
                for q in range(NQ):
                    act.wait_ge(yy, q + 1)
                    if q >= 2:
                        act.wait_ge(stored[q % 2], 16 * (q // 2))
                    nc.scalar.activation(yo[:, q % 2, :], ps[0:64, 2 + q % 2, :], ACT.Copy).then_inc(yv, 1)

            @block.vector
            def _(dve):
                copy_groups(dve, nc.vector.tensor_copy, evv, (2, 3))
                for k1 in range(KS):
                    u = k1 % 2
                    dve.wait_ge(mx, k1 + 1)
                    dve.wait_ge(hl[k1 % 3], 16 * (k1 // 3 + 1))
                    if k1 >= 2:
                        dve.wait_ge(comb, 2 * (k1 - 1))
                    X = ps[:, 4 + u, :].rearrange("p (z c) -> p z c", z=2)
                    for m, part in ((m1, 0), (m2, 1)):
                        nc.vector.tensor_tensor(m[:, u, :, :], X, h[:, k1 % 3, part:part + 1, :].to_broadcast([P, 2, HW]),
                                                ALU.mult).then_inc(prod, 1)
                for q in range(NQ):
                    dve.wait_ge(tt, q + 1)
                    if q >= 2:
                        dve.wait_ge(yy, q - 1)
                    nc.vector.tensor_copy(W[:, q % 2, :], ps[:, q % 2, :]).then_inc(wv, 1)


def hyena_gate(nc, tag, conv, y, x_gate, skip, dst):
    with Phase(nc, tag) as ph:
        sk = ph.sb("sk", [P, 2])
        a, b, c = (ph.sb(s, [P, 2, SEQ]) for s in "abc")
        ld, v, p_, st = ph.sem("ld"), ph.sem("v"), ph.sem("p"), ph.sem("st")
        with nc.Block() as block:

            @block.sync
            def _(sp):
                sp.dma_start(sk[:, :], skip.rearrange("(f p) -> p f", p=P), allow_slow_non_contiguous=True).then_inc(ld, 16)
                for f in range(2):
                    for t, s in ((a, conv), (b, y), (c, x_gate)):
                        sp.dma_start(t[:, f, :], s[f * P:(f + 1) * P, :]).then_inc(ld, 16)
                for f in range(2):
                    sp.wait_ge(p_, f + 1)
                    sp.dma_start(dst[f * P:(f + 1) * P, :], c[:, f, :]).then_inc(st, 16)
                sp.wait_ge(st, 32)

            @block.vector
            def _(dve):
                dve.wait_ge(ld, 112)
                for f in range(2):
                    nc.vector.scalar_tensor_tensor(out=a[:, f, :], in0=b[:, f, :], scalar=sk[:, f:f + 1], in1=a[:, f, :],
                                                   op0=ALU.mult, op1=ALU.add).then_inc(v, 1)

            @block.gpsimd
            def _(pool):
                pool.wait_ge(ld, 112)
                for f in range(2):
                    pool.wait_ge(v, f + 1)
                    nc.gpsimd.tensor_tensor(c[:, f, :], c[:, f, :], a[:, f, :], ALU.mult).then_inc(p_, 1)


def context_hyena(nc, tag, sums_ctx, vx, skip, fc_dram, ic_dram, ident_dram, dst):
    KTL = [(0, P), (P, P), (2 * P, 1)]
    with Phase(nc, tag) as ph:
        ident = ph.sb("ident", [P, P])
        fc = ph.sb("fc", [P, 2, 2, CTX + 1])
        ic = ph.sb("ic", [P, 3, 2, CTX])
        sd = ph.sb("sd", [P, 2, 2, 2 * HW])
        H_ = ph.sb("H", [P, 3, 2, 2 * HW])
        sk = ph.sb("sk", [P, 2, 2])
        v = ph.sb("v", [P, 3, 2, CTX])
        yt = ph.sb("yt", [P, 2, HW])
        m1, m2, Y = (ph.sb(s, [P, 3, 2, HW]) for s in ("m1", "m2", "Y"))
        g = ph.sb("g", [P, 2, CTX])
        ps = ph.ps("ps", [P, 8, 512])
        ld, pe_s, dv, st = ph.sem("ld"), ph.sem("pe"), ph.sem("dve"), ph.sem("st")
        with nc.Block() as block:

            @block.sync
            def _(sp):
                for t, s in ((ident[:, :], ident_dram), (fc[:, :, :, :], fc_dram), (ic[:, :, :, :], ic_dram),
                             (sd[:, :, :, :], sums_ctx.rearrange("(n p) w c -> p n w c", p=P))):
                    sp.dma_start(t, s).then_inc(ld, 16)
                sp.dma_start(v[:, :, :, :], vx.rearrange("(w f p) t -> p w f t", p=P, f=2)).then_inc(ld, 16)
                for o in range(2):
                    sp.dma_start(sk[:, o, :], skip[o].rearrange("(f p) -> p f", p=P), allow_slow_non_contiguous=True).then_inc(ld, 16)
                sp.wait_ge(dv, 6 + 2 * 13)
                sp.dma_start(dst[:, 0:CTX].rearrange("(f p) t -> p f t", p=P), v[:, 0, :, :]).then_inc(st, 16)
                sp.wait_ge(st, 16)

            @block.tensor
            def _(pe):
                pe.wait_ge(ld, 112)
                for w in range(2):
                    for kt, (k0, kn) in enumerate(KTL):
                        for n in range(2):
                            last = nc.tensor.matmul(ps[0:kn, 3 * w + kt, :], fc[:, n, w, k0:k0 + kn], sd[:, n, w, :],
                                                    start=(n == 0), stop=(n == 1))
                        last.then_inc(pe_s, 1)
                for o in range(2):
                    base = 6 + 13 * o
                    pe.wait_ge(dv, base)
                    for f in range(2):
                        for n in range(2):
                            last = nc.tensor.transpose(ps[:, 0, (2 * n + f) * P:(2 * n + f + 1) * P], v[:, 0, f, n * P:(n + 1) * P], ident[:, :])
                    last.then_inc(pe_s, 1)
                    pe.wait_ge(dv, base + 1)
                    for kt, (k0, kn) in enumerate(KTL):
                        for w in range(2):
                            for n in range(2):
                                last = nc.tensor.matmul(ps[0:kn, 1 + kt, w * HW:(w + 1) * HW], fc[:, n, w, k0:k0 + kn], yt[:, n, :],
                                                        start=(n == 0), stop=(n == 1))
                    last.then_inc(pe_s, 1)
                    pe.wait_ge(dv, base + 9)
                    for f in range(2):
                        terms = [(kt, w, kn) for kt, (_, kn) in enumerate(KTL) for w in range(2)]
                        for n, (kt, w, kn) in enumerate(terms):
                            last = nc.tensor.matmul(ps[:, 4, f * CTX:(f + 1) * CTX], Y[0:kn, kt, w, f * P:(f + 1) * P], ic[0:kn, kt, w, :],
                                                    start=(n == 0), stop=(n == len(terms) - 1))
                    last.then_inc(pe_s, 1)

            @block.vector
            def _(dve):
                n_v = [0]

                def step(ins):
                    n_v[0] += 1
                    ins.then_inc(dv, 1)
                    dve.wait_ge(dv, n_v[0])
                dve.wait_ge(ld, 112)
                for w in range(2):
                    for kt, (k0, kn) in enumerate(KTL):
                        dve.wait_ge(pe_s, 3 * w + kt + 1)
                        step(nc.vector.tensor_copy(H_[0:kn, kt, w, :], ps[0:kn, 3 * w + kt, :]))
                for o in range(2):
                    base = 6 + 3 * o
                    dve.wait_ge(pe_s, base + 1)
                    step(nc.vector.tensor_copy(yt[:, :, :], ps[:, 0, :].rearrange("p (n c) -> p n c", n=2)))
                    dve.wait_ge(pe_s, base + 2)
                    for lo, hi, kn in ((0, 2, P), (2, 3, 1)):
                        X = ps[0:kn, 1 + lo:1 + hi, :].rearrange("p k (w c) -> p k w c", w=2)
                        hh = lambda w: H_[0:kn, lo:hi, w:w + 1, o * HW:(o + 1) * HW].to_broadcast([kn, hi - lo, 2, HW])
                        step(nc.vector.tensor_tensor(m1[0:kn, lo:hi, :, :], X, hh(0), ALU.mult))
                        step(nc.vector.tensor_tensor(m2[0:kn, lo:hi, :, :], X, hh(1), ALU.mult))
                        step(nc.vector.tensor_tensor(Y[0:kn, lo:hi, 0, :], m1[0:kn, lo:hi, 0, :], m2[0:kn, lo:hi, 1, :], ALU.subtract))
                        step(nc.vector.tensor_tensor(Y[0:kn, lo:hi, 1, :], m1[0:kn, lo:hi, 1, :], m2[0:kn, lo:hi, 0, :], ALU.add))
                    dve.wait_ge(pe_s, base + 3)
                    for f in range(2):
                        step(nc.vector.scalar_tensor_tensor(out=g[:, f, :], in0=v[:, 0, f, :], scalar=sk[:, o, f:f + 1],
                                                            in1=ps[:, 4, f * CTX:(f + 1) * CTX], op0=ALU.mult, op1=ALU.add))
                    for f in range(2):
                        step(nc.vector.tensor_tensor(v[:, 0, f, :], g[:, f, :], v[:, 1 + o, f, :], ALU.mult))


def constants():
    c={}
    i=np.arange(P)
    c['ident']=np.eye(P,dtype=np.float32)
    tri=np.zeros((P,3,P),np.float32)
    tri[:,0,:]=i[:,None]<=i[None,:]; tri[:,1,:]=i[:,None]>=i[None,:]; tri[:,2,:]=1
    c['tri']=tri
    neg=np.zeros((P,2,P),np.float32)
    neg[:,0,:]=np.where(i[None,:]>=i[:,None],0,-1e30); neg[:,1,:]=np.where(i[None,:]<=i[:,None],0,-1e30)
    c['neg']=neg
    lev=np.zeros((P,2,7,P),np.float32)
    for L in range(7):
        s=1<<L
        m=(i[:,None]//(2*s)==i[None,:]//(2*s))&((i[:,None]//s)%2==1)&((i[None,:]//s)%2==0)
        lev[:,0,L,:]=m; lev[:,1,L,:]=m.T
    c['lev']=lev
    t=np.arange(2048); nf=32
    inv=np.float32(10000.0)**(-np.arange(nf,dtype=np.float32)/np.float32(nf))
    rope=np.zeros((2304,2,P),np.float32); rope[:256,0,:]=1
    for g,pos in enumerate((t//64,t%64)):
        ang=pos.astype(np.float32)[:,None]*inv[None,:]
        co,si=np.cos(ang),np.sin(ang)
        o=g*64
        rope[256:,0,o:o+32]=co; rope[256:,0,o+32:o+64]=co
        rope[256:,1,o:o+32]=-si; rope[256:,1,o+32:o+64]=si
    c['rope']=rope
    hot=np.zeros((32,64,2,64),np.float32)
    q=np.arange(64); c0=np.clip(q-8,0,48)
    for kc in range(64):
        inw=(kc>=c0)&(kc<c0+16)
        for qq in range(64):
            if inw[qq]: hot[kc-qq+15,kc,:,qq]=1
            else: hot[31,kc,:,qq]=-1e30
    f32=np.float32
    def feats(l):
        t=np.linspace(0.0,1.0,l,dtype=f32)[:,None]
        fr=np.linspace(1e-4,15,16,dtype=f32)
        ang=(f32(2.0*math.pi/l)*np.arange(l,dtype=f32)[:,None])*fr[None,:]
        return t,np.concatenate([t,np.cos(ang),-np.sin(ang)],-1).astype(f32)
    mx=math.log(1e-2)/0.3; mn=math.log(1e-2)/1.5
    deltas=np.abs(np.linspace(mn,mx,256,dtype=f32))
    tc,zc=feats(256); tx,zx=feats(2048)
    c['feats']=np.ascontiguousarray(np.concatenate([zc,zx],0).T)
    c['win']=np.ascontiguousarray(np.exp(-tx*deltas[None,:]).T.astype(f32))
    wc=np.exp(-tc*deltas[None,:]).astype(f32)
    wc2=np.stack([wc,wc],1); wc2[0,1]=0
    c['win_ctx']=wc2
    n2=np.arange(128)[:,None,None]; k1=np.arange(17)[None,:,None]; k2=np.arange(128)[None,None,:]
    th=2*math.pi*((n2*(k1+32*k2))%4096)/4096
    tf=np.stack([np.cos(th),np.sin(th),-np.sin(th)],2)
    c['tf']=tf.astype(f32)
    c['ti']=np.ascontiguousarray(tf.transpose(3,1,2,0)).astype(f32)
    n1=np.arange(16)[:,None]; kk=np.arange(17)[None,:]
    ph=2*math.pi*((n1*kk)%32)/32
    F=np.concatenate([np.cos(ph),-np.sin(ph[:,1:16])],1)
    bd=np.zeros((8,16,8,32)); bi=np.zeros((4,32,4,16))
    wgt=np.where((kk==0)|(kk==16),1,2)/4096.0
    G=np.concatenate([np.cos(ph)*wgt,-np.sin(ph[:,1:16])*2/4096.0],1).T
    for i_ in range(8): bd[i_,:,i_,:]=F
    for i_ in range(4): bi[i_,:,i_,:]=G
    c['bd']=bd.reshape(128,256).astype(f32); c['bi']=bi.reshape(128,64).astype(f32)
    n=np.arange(256)[:,None]; k=np.arange(257)[None,:]
    th=2*math.pi*((n*k)%512)/512
    c['fc']=np.stack([np.cos(th),-np.sin(th)],1).reshape(2,128,2,257).transpose(1,0,2,3).astype(f32).copy()
    w=np.where((k==0)|(k==256),1,2)/512.0
    ic=np.zeros((384,2,256)); ic[:257]=np.stack([(np.cos(th)*w).T,(-np.sin(th)*w).T],1)
    c['ic']=ic.reshape(3,128,2,256).transpose(1,0,2,3).astype(f32).copy()
    c['hot']=hot.reshape(32,64,128)
    return c


def build(nc, a, k, out):
    dram = lambda name, shape: nc.dram_tensor(name, shape, F32).ap()
    proj, gate = dram("proj", (IN_WIDTH, T)), dram("gate", (2, D))
    dnT, qkv = dram("dn_conv_out", (3 * DN, T)), dram("dn_qkv", (T, 3 * DN))
    o_dir = [dram("dn_forward", (T, DN)), dram("dn_backward", (T, DN))]
    na = dram("na_out", (NH * DH, T))
    vx, vx_ctx = dram("hy_vx", (3 * HW, SEQ)), dram("hy_vx_ctx", (3 * HW, CTX))
    sums, sums_ctx = dram("hy_sums", (2, 2 * HW, SEQ)), dram("hy_sums_ctx", (CTX, 2, 2 * HW))
    spec, conv, y1 = dram("hy_spec", (2, KS, P, 2, HW)), dram("hy_conv_out", (HW, SEQ)), dram("hy_y1", (HW, SEQ))
    hy = dram("hy_out", (HW, T))
    mid = dram("mid", (T, D))
    x, ctx = a["x"][0], a["ctx"][0]
    flat = lambda ap: ap.rearrange("a b -> (a b)")
    for i in range(DEPTH):
        last = i == DEPTH - 1
        n = lambda s: f"l{i}{s}"
        with nc.sbuf_tensor(n("aff"), [P, 2, KT, 2], F32) as aff:
            modulation(nc, n("mod"), a["c"][0], a["c_ctx"], a["w_ada"][i], a["b_ada"][i], a["g_pre"][i], a["g_post"][i], aff, gate)
            norm_project(nc, n("proj"), [(ctx, 0, 2, 1), (x, 2, SEQ // P, 0)], aff, a["w_in"][i], k["ident"], proj)
        attention(nc, n("na"), proj, a["na_rpb"][i], k["ident"], k["hot"], na, not last)
        with nc.sbuf_tensor(n("col"), [P, 7, NT, 2 * H], F32) as col:
            short_conv(nc, n("dc"), proj, C_DN, 12, a["dn_conv"][i], True, dnT[:, 0:CTX], dnT[:, CTX:T])
            dn_gates(nc, n("dg"), proj, flat(a["dn_a_log"][i]), flat(a["dn_dt_bias"][i]), k["ident"], k["tri"], col)
            dn_tokens(nc, n("dt"), dnT, k["rope"], k["ident"], qkv)
            dn_scan(nc, n("ds"), qkv, col, k["ident"], k["tri"], k["neg"], k["lev"], o_dir)
        short_conv(nc, n("hc"), proj, C_HY, 6, a["hy_conv"][i], False, vx_ctx, vx)
        hyena_filters(nc, n("hf"), k["feats"], *(a[f"hy_{s}"][i] for s in ("w1", "b1", "w2", "b2", "w3", "b3", "freq", "wout")),
                      k["win"], k["win_ctx"], sums, sums_ctx)
        kernel_spectrum(nc, n("hk"), sums, k["tf"], k["bd"], spec)
        src = vx[0:HW, :]
        for o in range(2):
            long_conv(nc, n(f"hl{o}"), src, spec[o], k["tf"], k["ti"], k["bd"], k["bi"], k["ident"], conv)
            hyena_gate(nc, n(f"hg{o}"), conv, src, vx[HW * (o + 1):HW * (o + 2), :], a["hy_skip"][i][o],
                       y1 if o == 0 else hy[:, CTX:T])
            src = y1
        if not last:
            context_hyena(nc, n("hx"), sums_ctx, vx_ctx, a["hy_skip"][i], k["fc"], k["ic"], k["ident"], hy)
            output_tiles(nc, n("oc"), (0, 2), proj, na, o_dir, hy, a["dn_norm"][i], a["w_out"][i], gate, 1, k["ident"],
                         ctx, mid[0:CTX, :])
        output_tiles(nc, n("ox"), (2, NT), proj, na, o_dir, hy, a["dn_norm"][i], a["w_out"][i], gate, 0, k["ident"],
                     x, out[0] if last else mid[CTX:T, :])
        x, ctx = mid[CTX:T, :], mid[0:CTX, :]


def kernel(**inputs):
    from concourse.bacc import Bacc
    from concourse.bass_utils import run_bass_kernel_spmd

    nc = Bacc("TRN2", target_bir_lowering=False, num_devices=1)
    arrays = {}

    def put(name, a):
        arrays[name] = np.ascontiguousarray(a)
        return nc.dram_tensor(name, a.shape, F32, kind="ExternalInput").ap()
    a = {name: put("in_" + name, np.asarray(v)) for name, v in inputs.items()}
    k = {name: put("table_" + name, v) for name, v in constants().items()}
    out = nc.dram_tensor("out", (1, SEQ, D), F32, kind="ExternalOutput").ap()
    build(nc, a, k, out)
    return run_bass_kernel_spmd(nc, [arrays], core_ids=[0]).results[0]["out"]
```

```python
import math
from contextlib import ExitStack

import numpy as np
import concourse.bass as bass
from concourse import mybir

F32 = mybir.dt.float32
F32R = mybir.dt.float32r
ALU = mybir.AluOpType
ACT = mybir.ActivationFunctionType
AX = mybir.AxisListType

P = 128
D = 1024
KT = D // P
SEQ, CTX = 2048, 256
T = CTX + SEQ
NT = T // P
DEPTH = 2
IN_WIDTH = 4112
EPS = 1e-6
C_NAQ, C_NAK, C_NAV, C_NAZ = 0, 256, 512, 768
C_DN, C_DNZ, C_DNB, C_HY, C_HYZ = 1024, 2560, 3072, 3088, 3856
GRID = 64
ROWS = SEQ // GRID
NEG = -1e30
CHUNKS = [(0, 512), (512, 512), (1024, 512), (1536, 512), (2048, 256)]


class Phase:

    def __init__(self, nc, tag):
        self.nc, self.tag, self.stack, self.sems = nc, tag, ExitStack(), []

    def __enter__(self):
        return self

    def sb(self, name, shape, dtype=F32):
        return self.stack.enter_context(self.nc.sbuf_tensor(f"{self.tag}_{name}", shape, dtype))

    def ps(self, name, shape):
        return self.stack.enter_context(self.nc.psum_tensor(f"{self.tag}_{name}", shape, F32))

    def sem(self, name):
        s = self.stack.enter_context(self.nc.semaphore(f"{self.tag}_{name}"))
        self.sems.append(s)
        return s

    def __exit__(self, kind, value, trace):
        if kind is None:
            for s in self.sems:
                self.nc.sync.sem_clear(s)
            self.nc.all_engine_barrier()
        self.stack.close()


def wait(eng, sem, value):
    if isinstance(value, int) and value <= 0:
        return
    eng.wait_ge(sem, value)


def at(eng, value):
    return value if isinstance(value, int) else eng.snap(value)


def repeat(eng, n, body, unroll=2, lo=0):
    first, last = lo // unroll, n // unroll
    if first == 0:
        for u in range(unroll):
            body(0, u)
        first = 1
    if last > first:
        with eng.Fori(first, last) as j:
            for u in range(unroll):
                body(j, u)


def modulation(nc, tag, c, c_ctx, w_ada, b_ada, g_pre, g_post, aff, gate_dram):
    GW, NG = 384, 8
    MB = GW // P
    with Phase(nc, tag) as ph:
        cond = ph.sb("cond", [P, 2, KT])
        act = ph.sb("act", [P, KT, 2])
        wa = ph.sb("wa", [P, 2, KT, GW])
        bias = ph.sb("bias", [P, 3 * KT])
        gp = ph.sb("gp", [P, 2, KT])
        mod = ph.sb("mod", [P, 3 * KT, 2])
        gate = ph.sb("gate", [P, 2, KT])
        ps = ph.ps("ps", [P, 2, 512])
        small, wl = ph.sem("small"), [ph.sem("w0"), ph.sem("w1")]
        silu, mm, ev, fin, st = ph.sem("silu"), ph.sem("mm"), ph.sem("ev"), ph.sem("fin"), ph.sem("st")
        wd = w_ada.rearrange("(k p) n -> p k n", p=P)
        with nc.Block() as block:

            @block.sync
            def _(sp):
                def load(j, u):
                    col = at(sp, (2 * j + u) * GW)
                    wait(sp, mm, 2 * j + u - 1)
                    sp.dma_start(wa[:, u, :, :], wd[:, :, bass.ds(col, GW)]).then_inc(wl[u], 16)
                repeat(sp, NG, load)
                sp.wait_ge(fin, 2)
                for j in range(2):
                    sp.dma_start(gate_dram[j].rearrange("(k p) -> p k", p=P), gate[:, j, :],
                                 allow_slow_non_contiguous=True).then_inc(st, 16)
                sp.wait_ge(st, 32)

            @block.scalar
            def _(act_e):
                act_e.dma_start(cond[:, 0, :], c.rearrange("(k p) -> p k", p=P), allow_slow_non_contiguous=True).then_inc(small, 16)
                act_e.dma_start(cond[:, 1, :], c_ctx.rearrange("(k p) -> p k", p=P), allow_slow_non_contiguous=True).then_inc(small, 16)
                act_e.dma_start(bias[:, :], b_ada.rearrange("(m p) -> p m", p=P), allow_slow_non_contiguous=True).then_inc(small, 16)
                act_e.dma_start(gp[:, 0, :], g_pre.rearrange("(k p) -> p k", p=P), allow_slow_non_contiguous=True).then_inc(small, 16)
                act_e.dma_start(gp[:, 1, :], g_post.rearrange("(k p) -> p k", p=P), allow_slow_non_contiguous=True).then_inc(small, 16)
                act_e.wait_ge(small, 80)
                nc.scalar.activation(act[:, :, :].rearrange("p k j -> p j k"), cond[:, :, :], ACT.Silu).then_inc(silu, 1)

            @block.tensor
            def _(pe):
                pe.wait_ge(silu, 1)

                def group(j, u):
                    wait(pe, wl[u], 16 * (j + 1))
                    wait(pe, ev, 2 * j + u - 1)
                    for m in range(MB):
                        for k in range(KT):
                            last = nc.tensor.matmul(ps[:, u, 2 * m:2 * m + 2], wa[:, u, k, m * P:(m + 1) * P],
                                                    act[:, k, :], start=(k == 0), stop=(k == KT - 1))
                    last.then_inc(mm, 1)
                repeat(pe, NG, group)

            @block.vector
            def _(dve):
                dve.wait_ge(small, 80)

                def copy(j, u):
                    wait(dve, mm, 2 * j + u + 1)
                    nc.vector.tensor_copy(mod[:, bass.ds((2 * j + u) * MB, MB), :],
                                          ps[:, u, 0:2 * MB].rearrange("p (m j) -> p m j", j=2)).then_inc(ev, 1)
                repeat(dve, NG, copy)
                dve.wait_ge(ev, NG)
                for j in range(2):
                    nc.vector.tensor_tensor(mod[:, :, j], mod[:, :, j], bias[:, :], ALU.add).then_inc(ev, 1)
                dve.wait_ge(ev, NG + 2)
                for j in range(2):
                    nc.vector.tensor_tensor(gate[:, j, :], mod[:, 2 * KT:, j], gp[:, 1, :], ALU.mult).then_inc(fin, 1)
                for j in range(2):
                    nc.vector.tensor_copy(aff[:, 1, :, j], mod[:, 0:KT, j]).then_inc(fin, 1)
                    nc.vector.scalar_tensor_tensor(out=aff[:, 0, :, j], in0=mod[:, KT:2 * KT, j], scalar=1.0,
                                                   in1=gp[:, 0, :], op0=ALU.add, op1=ALU.mult).then_inc(fin, 1)
                dve.wait_ge(fin, 6)


def norm_project(nc, tag, srcs, aff, w_in, ident_dram, proj):
    with Phase(nc, tag) as ph:
        ident = ph.sb("ident", [P, P])
        hi = ph.sb("hT_high", [P, KT, T], F32R)
        lo = ph.sb("hT_low", [P, KT, T], F32R)
        whole = ph.sb("whole", [P, 2, 512])
        sq = ph.sb("sq", [P, D])
        st4 = ph.sb("st4", [P, 2, 4])
        w = ph.sb("w", [P, 2, KT, P])
        w_hi = ph.sb("w_high", [P, 2, KT, P], F32R)
        w_lo = ph.sb("w_low", [P, 2, KT, P], F32R)
        o = ph.sb("o", [P, 2, T])
        x = o[:, 0, 0:2 * D].rearrange("p (u d) -> p u d", u=2)
        xn = o[:, 1, 0:2 * D].rearrange("p (u d) -> p u d", u=2)
        psT = ph.ps("psT", [P, 2, 512])
        ps = ph.ps("ps", [P, 5, 512])
        const = ph.sem("const")
        xl = [ph.sem("xl0"), ph.sem("xl1")]
        ssq, ms, rt, rs, nrm, tr, hv = (ph.sem(s) for s in ("ssq", "ms", "rt", "rs", "nrm", "tr", "hv"))
        wl = [ph.sem("wl0"), ph.sem("wl1")]
        stored = [ph.sem("so0"), ph.sem("so1")]
        mm, evv, eva = ph.sem("mm"), ph.sem("evv"), ph.sem("eva")
        hh, split, wh, ws = ph.sem("high"), ph.sem("split"), ph.sem("w_high"), ph.sem("w_split")
        wd = w_in.rearrange("(k p) n -> p k n", p=P)
        NB = 32
        rounds = [(src, first, n, j) for src, first, n, j in srcs]

        with nc.Block() as block:

            @block.sync
            def _(sp):
                sp.dma_start(ident[:, :], ident_dram).then_inc(const, 16)
                for src, first, n, _ in rounds:
                    def load(j, u):
                        row = at(sp, (2 * j + u - first) * P)
                        wait(sp, nrm, 2 * j + u - 1)
                        sp.dma_start(x[:, u, :], src[bass.ds(row, P), :]).then_inc(xl[u], 16)
                    repeat(sp, first + n, load, lo=first)

                def store(j, u, off, m=P):
                    b = 2 * j + u
                    wait(sp, eva, 2 * (b + 1))
                    sp.dma_start(proj[bass.ds(b * P + off, m), 0:1024], o[0:m, u, 0:1024]).then_inc(stored[u], 16)
                    wait(sp, evv, 3 * (b + 1))
                    sp.dma_start(proj[bass.ds(b * P + off, m), 1024:T], o[0:m, u, 1024:T]).then_inc(stored[u], 16)

                def blocks(j, off, prev_off):
                    for u in range(2):
                        b = 2 * j + u
                        wait(sp, ws, b - 1)
                        sp.dma_start(w[:, u, :, :], wd[:, :, bass.ds(b * P + off, P)]).then_inc(wl[u], 16)
                        if u:
                            store(j, 0, off)
                        elif not (isinstance(j, int) and j == 0):
                            store(j - 1 if isinstance(j, int) else j + -1, 1, prev_off)
                blocks(0, 0, 0)
                with sp.Fori(1, 12) as j:
                    blocks(j, 0, 0)
                blocks(12, 16, 0)
                with sp.Fori(13, 16) as j:
                    blocks(j, 16, 16)
                sp.wait_ge(ws, 31)
                sp.dma_start(w[:, 0, :, 0:16], wd[:, :, C_DNB:C_DNB + 16]).then_inc(wl[0], 16)
                store(15, 1, 16)
                store(16, 0, C_DNB - 32 * P, 16)
                sp.wait_ge(stored[0], 32 * 17)
                sp.wait_ge(stored[1], 32 * 16)

            @block.scalar
            def _(act):
                def square(j, u):
                    i = 2 * j + u
                    wait(act, xl[u], 16 * (j + 1))
                    wait(act, ms, i)
                    wait(act, rs, i - 1)
                    nc.scalar.activation(sq[:, :], x[:, u, :], ACT.Square, accum_out=st4[:, u, 0:1]).then_inc(ssq, 1)
                    wait(act, ms, i + 1)
                    nc.scalar.activation(st4[:, u, 2:3], st4[:, u, 1:2], ACT.Sqrt).then_inc(rt, 1)

                def modulate(j, u, mj):
                    i = 2 * j + u
                    for h in range(2):
                        wait(act, tr, 2 * i + h + 1)
                        wait(act, split, 2 * i + h - 1)
                        for q in range(4):
                            k = 4 * h + q
                            last = nc.scalar.activation(whole[:, h, q * P:(q + 1) * P], psT[:, h, q * P:(q + 1) * P],
                                                        ACT.Identity, scale=aff[:, 0, k, mj:mj + 1],
                                                        bias=aff[:, 1, k, mj:mj + 1])
                        last.then_inc(hv, 1)
                square(0, 0)
                for _, first, n, mj in rounds:
                    def tile(j, u):
                        if u == 0:
                            square(j, 1)
                        elif isinstance(j, int) or n > 2:
                            square(j + 1, 0)
                        modulate(j, u, mj)
                    if first + n < NT:
                        repeat(act, first + n, tile, lo=first)
                    else:
                        repeat(act, first + n - 2, tile, lo=first)
                        square(NT // 2 - 1, 1)
                        modulate(NT // 2 - 1, 0, mj)
                        modulate(NT // 2 - 1, 1, mj)

                def evict(j, u, m=P):
                    b = 2 * j + u
                    wait(act, stored[u], 32 * j)
                    for c in (0, 1):
                        wait(act, mm, 5 * b + c + 1)
                        nc.scalar.activation(o[0:m, u, CHUNKS[c][0]:CHUNKS[c][0] + CHUNKS[c][1]],
                                             ps[0:m, c, 0:CHUNKS[c][1]], ACT.Copy).then_inc(eva, 1)
                repeat(act, NB, evict)
                evict(16, 0, 16)

            @block.vector
            def _(dve):
                for _, first, n, _ in rounds:
                    def tile(j, u):
                        i = 2 * j + u
                        wait(dve, ssq, i + 1)
                        nc.vector.tensor_scalar(st4[:, u, 1:2], st4[:, u, 0:1], 1.0 / D, EPS, ALU.mult, ALU.add).then_inc(ms, 1)
                        wait(dve, rt, i + 1)
                        nc.vector.reciprocal(st4[:, u, 3:4], st4[:, u, 2:3]).then_inc(rs, 1)
                        wait(dve, rs, i + 1)
                        wait(dve, tr, 2 * (i - 1))
                        nc.vector.tensor_scalar(xn[:, u, :], x[:, u, :], st4[:, u, 3:4], None, ALU.mult).then_inc(nrm, 1)
                    repeat(dve, first + n, tile, lo=first)

                def high(j, u, m=P):
                    wait(dve, wl[u], 16 * (j + 1))
                    wait(dve, mm, 5 * (2 * j + u - 1))
                    nc.vector.tensor_copy(w_hi[:, u, :, 0:m], w[:, u, :, 0:m]).then_inc(wh, 1)

                def both(j, u):
                    if u == 0:
                        high(j, 1)
                    else:
                        high(j + 1, 0)
                    evict(j, u)
                def evict(j, u, m=P):
                    b = 2 * j + u
                    for c in (2, 3, 4):
                        wait(dve, mm, 5 * b + c + 1)
                        if c == 2:
                            wait(dve, stored[u], 32 * j)
                        nc.vector.tensor_copy(o[0:m, u, CHUNKS[c][0]:CHUNKS[c][0] + CHUNKS[c][1]],
                                              ps[0:m, c, 0:CHUNKS[c][1]]).then_inc(evv, 1)
                high(0, 0)
                repeat(dve, NB - 2, both)
                both(15, 0)
                high(16, 0, 16)
                evict(15, 1)
                evict(16, 0, 16)

            @block.gpsimd
            def _(pool):
                def split_tokens(j, u):
                    i = 2 * j + u
                    for h in range(2):
                        src = whole[:, h, :].rearrange("p (q t) -> p q t", q=4)
                        dst = [t[:, 4 * h:4 * h + 4, bass.ds(i * P, P)] for t in (hi, lo)]
                        wait(pool, hv, 2 * i + h + 1)
                        nc.gpsimd.tensor_copy(dst[0], src).then_inc(hh, 1)
                        wait(pool, hh, 2 * i + h + 1)
                        nc.gpsimd.tensor_tensor(dst[1], src, dst[0].bitcast(F32), ALU.subtract).then_inc(split, 1)
                repeat(pool, NT, split_tokens)

                def low(j, u, m=P):
                    wait(pool, wh, 2 * j + u + 1)
                    nc.gpsimd.tensor_tensor(w_lo[:, u, :, 0:m], w[:, u, :, 0:m], w_hi[:, u, :, 0:m].bitcast(F32),
                                            ALU.subtract).then_inc(ws, 1)
                repeat(pool, NB, low)
                low(16, 0, 16)

            @block.tensor
            def _(pe):
                pe.wait_ge(const, 16)

                def tile(j, u):
                    i = 2 * j + u
                    wait(pe, nrm, i + 1)
                    for h in range(2):
                        wait(pe, hv, 2 * i + h - 1)
                        for q in range(4):
                            last = nc.tensor.transpose(psT[:, h, q * P:(q + 1) * P],
                                                       xn[:, u, (4 * h + q) * P:(4 * h + q + 1) * P], ident[:, :])
                        last.then_inc(tr, 1)
                repeat(pe, NT, tile)
                pe.wait_ge(split, 2 * NT)

                def block_(j, u, m=P):
                    b = 2 * j + u
                    wait(pe, ws, b + 1)
                    for c, (t0, tn) in enumerate(CHUNKS):
                        if c < 2:
                            wait(pe, eva, 2 * (b - 1) + c + 1)
                        else:
                            wait(pe, evv, 3 * (b - 1) + c - 1)
                        for k in range(KT):
                            terms = [(w_hi, hi), (w_hi, lo), (w_lo, hi)]
                            for n, (wt, ht) in enumerate(terms):
                                last = nc.tensor.matmul(ps[0:m, c, 0:tn], wt[:, u, k, 0:m], ht[:, k, t0:t0 + tn],
                                                        start=(k == 0 and n == 0), stop=(k == KT - 1 and n == 2))
                        last.then_inc(mm, 1)
                repeat(pe, NB, block_)
                block_(16, 0, 16)


H = 4
DN = H * P
LEVELS = 7


def after(j, u):
    return (j, 1) if u == 0 else (j + 1, 0)


def short_conv(nc, tag, proj, row0, tiles, weight, silu, out_ctx, out):
    taps = weight.shape[0]
    h = taps // 2
    W = T + h
    with Phase(nc, tag) as ph:
        wcol = ph.sb("wcol", [P, taps, tiles])
        x = ph.sb("x", [P, 2, W + 2 * h])
        acc = ph.sb("acc", [P, 2, W])
        y = ph.sb("y", [P, 2, W])
        wl, zero = ph.sem("wl"), ph.sem("zero")
        xl = [ph.sem("xl0"), ph.sem("xl1")]
        stored = [ph.sem("so0"), ph.sem("so1")]
        first, tap, done = ph.sem("first"), ph.sem("tap"), ph.sem("done")
        VT = taps - 1
        with nc.Block() as block:

            @block.sync
            def _(sp):
                sp.wait_ge(zero, 1)

                def load(j, u):
                    row = at(sp, row0 + (2 * j + u) * P)
                    wait(sp, tap, VT * (2 * j + u - 1))
                    sp.dma_start(x[:, u, h:h + CTX], proj[bass.ds(row, P), 0:CTX]).then_inc(xl[u], 16)
                    sp.dma_start(x[:, u, 2 * h + CTX:2 * h + T], proj[bass.ds(row, P), CTX:T]).then_inc(xl[u], 16)
                repeat(sp, tiles, load)

            @block.gpsimd
            def _(pool):
                for u in range(2):
                    nc.gpsimd.memset(x[:, u, 0:h], 0.0)
                    nc.gpsimd.memset(x[:, u, h + CTX:2 * h + CTX], 0.0)
                    last = nc.gpsimd.memset(x[:, u, 2 * h + T:3 * h + T], 0.0)
                last.then_inc(zero, 1)

            @block.scalar
            def _(act):
                for t in range(taps):
                    act.dma_start(wcol[:, t, :], weight[t].rearrange("(f p) -> p f", p=P),
                                  allow_slow_non_contiguous=True).then_inc(wl, 16)
                act.wait_ge(wl, 16 * taps)
                act.wait_ge(zero, 1)

                def finish(i, j, u):
                    wait(act, tap, VT * (i + 1))
                    wait(act, stored[u], 32 * j)
                    nc.scalar.activation(y[:, u, :], acc[:, u, :], ACT.Silu if silu else ACT.Copy).then_inc(done, 1)
                    wait(act, done, i + 1)
                    act.dma_start(out_ctx[bass.ds(i * P, P), :], y[:, u, 0:CTX]).then_inc(stored[u], 16)
                    act.dma_start(out[bass.ds(i * P, P), :], y[:, u, CTX + h:W]).then_inc(stored[u], 16)

                def begin(i, j, u):
                    wait(act, xl[u], 32 * (j + 1))
                    nc.scalar.activation(acc[:, u, :], x[:, u, 0:W], ACT.Identity,
                                         scale=wcol[:, 0, bass.ds(i, 1)]).then_inc(first, 1)

                def tile(j, u):
                    begin(2 * j + u + 1, *after(j, u))
                    finish(2 * j + u, j, u)
                begin(0, 0, 0)
                repeat(act, tiles - 2, tile)
                tile(tiles // 2 - 1, 0)
                finish(tiles - 1, tiles // 2 - 1, 1)
                act.wait_ge(stored[0], 16 * tiles)
                act.wait_ge(stored[1], 16 * tiles)

            @block.vector
            def _(dve):
                dve.wait_ge(wl, 16 * taps)

                def tile(j, u):
                    i = 2 * j + u
                    wait(dve, first, i + 1)
                    for t in range(1, taps):
                        wait(dve, tap, VT * i + t - 1)
                        nc.vector.scalar_tensor_tensor(out=acc[:, u, :], in0=x[:, u, t:t + W],
                                                       scalar=wcol[:, t, bass.ds(i, 1)], in1=acc[:, u, :],
                                                       op0=ALU.mult, op1=ALU.add).then_inc(tap, 1)
                repeat(dve, tiles, tile)


G_, GC, BETA, EGC, NBEG, EKD, ELAST = range(7)


def dn_gates(nc, tag, proj, a_log, dt_bias, ident_dram, tri_dram, col):
    N8 = 2 * H
    with Phase(nc, tag) as ph:
        ident = ph.sb("ident", [P, P])
        tri = ph.sb("tri", [P, 3, P])
        ba = ph.sb("ba", [16, T])
        raw = ph.sb("raw", [P, NT, 16])
        rows = ph.sb("rows", [P, 2, N8])
        t = ph.sb("t", [P, 4, NT, N8])
        ps = ph.ps("ps", [P, 3, 512])
        ld, pe_s, v, a = ph.sem("ld"), ph.sem("products"), ph.sem("vector"), ph.sem("scalar")
        b3 = lambda r: rows[:, r:r + 1, :].to_broadcast([P, NT, N8])
        with nc.Block() as block:

            @block.sync
            def _(sp):
                sp.dma_start(ident[:, :], ident_dram).then_inc(ld, 16)
                sp.dma_start(tri[:, :, :], tri_dram).then_inc(ld, 16)
                sp.dma_start(ba[:, :], proj[C_DNB:C_DNB + 16, :]).then_inc(ld, 16)
                sp.dma_start(rows[:, 0, :], a_log.partition_broadcast(P)).then_inc(ld, 16)
                sp.dma_start(rows[:, 1, :], dt_bias.partition_broadcast(P)).then_inc(ld, 16)

            @block.tensor
            def _(pe):
                pe.wait_ge(ld, 80)
                for i in range(NT):
                    last = nc.tensor.transpose(ps[:, 0, 16 * i:16 * i + 16], ba[:, i * P:(i + 1) * P], ident[0:16, 0:16])
                last.then_inc(pe_s, 1)
                pe.wait_ge(v, 6)
                nc.tensor.matmul(ps[:, 1, 0:NT * H], tri[:, 0, :], col[:, G_, :, 0:H], start=True, stop=True)
                nc.tensor.matmul(ps[:, 1, NT * H:NT * N8], tri[:, 1, :], col[:, G_, :, H:N8], start=True, stop=True)
                nc.tensor.matmul(ps[:, 2, 0:NT * N8], tri[:, 2, :], col[:, G_, :, :], start=True, stop=True).then_inc(pe_s, 1)

            @block.scalar
            def _(act):
                act.wait_ge(v, 2)
                nc.scalar.activation(t[:, 1, :, :], t[:, 0, :, :], ACT.Exp).then_inc(a, 1)
                nc.scalar.activation(t[:, 3, :, :], raw[:, :, 0:N8], ACT.Exp, scale=-1.0).then_inc(a, 1)
                nc.scalar.activation(rows[:, 0, :], rows[:, 0, :], ACT.Exp).then_inc(a, 1)
                act.wait_ge(a, 1)
                nc.scalar.activation(t[:, 0, :, :], t[:, 1, :, :], ACT.Ln, bias=1.0).then_inc(a, 1)
                act.wait_ge(v, 9)
                nc.scalar.activation(col[:, EGC, :, :], col[:, GC, :, :], ACT.Exp).then_inc(a, 1)
                nc.scalar.activation(col[:, EKD, :, :], t[:, 1, :, :], ACT.Exp).then_inc(a, 1)
                nc.scalar.activation(col[:, ELAST, :, :], ps[:, 2, 0:NT * N8].rearrange("p (n e) -> p n e", e=N8),
                                     ACT.Exp).then_inc(a, 1)
                act.wait_ge(a, 7)

            @block.vector
            def _(dve):
                def step(ins, n):
                    ins.then_inc(v, 1)
                    dve.wait_ge(v, n)
                dve.wait_ge(pe_s, 1)
                dve.wait_ge(ld, 80)
                step(nc.vector.tensor_copy(raw[:, :, :], ps[:, 0, 0:NT * 16].rearrange("p (n e) -> p n e", e=16)), 1)
                nc.vector.tensor_tensor(t[:, 2, :, :], raw[:, :, N8:16], b3(1), ALU.add).then_inc(pe_s, 1)
                dve.wait_ge(pe_s, 2)
                step(nc.vector.scalar_tensor_tensor(out=t[:, 0, :, :], in0=t[:, 2, :, :], scalar=-1.0, in1=t[:, 2, :, :],
                                                    op0=ALU.mult, op1=ALU.min), 2)
                dve.wait_ge(a, 4)
                step(nc.vector.scalar_tensor_tensor(out=t[:, 2, :, :], in0=t[:, 2, :, :], scalar=0.0, in1=t[:, 0, :, :],
                                                    op0=ALU.max, op1=ALU.add), 3)
                step(nc.vector.tensor_scalar(rows[:, 0, :], rows[:, 0, :], -1.0, None, ALU.mult), 4)
                step(nc.vector.tensor_scalar(t[:, 3, :, :], t[:, 3, :, :], 1.0, None, ALU.add), 5)
                step(nc.vector.tensor_tensor(col[:, G_, :, :], t[:, 2, :, :], b3(0), ALU.mult), 6)
                step(nc.vector.reciprocal(col[:, BETA, :, :], t[:, 3, :, :]), 7)
                dve.wait_ge(pe_s, 3)
                step(nc.vector.tensor_copy(col[:, GC, :, :].rearrange("p n (d h) -> p d n h", d=2),
                                           ps[:, 1, 0:NT * N8].rearrange("p (d n h) -> p d n h", d=2, h=H)), 8)
                step(nc.vector.tensor_tensor(t[:, 1, :, :], ps[:, 2, 0:NT * N8].rearrange("p (n e) -> p n e", e=N8),
                                             col[:, GC, :, :], ALU.subtract), 9)
                dve.wait_ge(a, 7)
                step(nc.vector.scalar_tensor_tensor(out=col[:, NBEG, :, :], in0=col[:, BETA, :, :], scalar=-1.0,
                                                    in1=col[:, EGC, :, :], op0=ALU.mult, op1=ALU.mult), 10)


def dn_tokens(nc, tag, dnT, rope_dram, ident_dram, qkv):
    with Phase(nc, tag) as ph:
        ident = ph.sb("ident", [P, P])
        f = ph.sb("f", [P, 2, 12, P])
        rope = ph.sb("rope", [P, 2, 2, P])
        t1 = ph.sb("t1", [P, 2, 2 * DN])
        t2 = ph.sb("t2", [P, 2, 2 * DN])
        sq = ph.sb("sq", [P, 2 * DN])
        n8 = ph.sb("n8", [P, 2, 4, 2 * H])
        o = ph.sb("o", [P, 2, 3 * DN])
        ps = [ph.ps("ps0", [P, 3, 512]), ph.ps("ps1", [P, 3, 512])]
        const = ph.sem("const")
        ld, stored = [ph.sem("ld0"), ph.sem("ld1")], [ph.sem("so0"), ph.sem("so1")]
        tr, rot, sums, vout, sqs, ssum, rt, rs, nrm = (ph.sem(s) for s in
            ("transposed", "rotated", "summed", "v_out", "squares", "square_sums", "roots", "inverse", "normalised"))
        src = dnT.rearrange("(f p) t -> p f t", p=P)
        with nc.Block() as block:

            @block.sync
            def _(sp):
                sp.dma_start(ident[:, :], ident_dram).then_inc(const, 16)

                def load(j, u):
                    i = 2 * j + u
                    wait(sp, rot, 3 * (i - 1))
                    sp.dma_start(f[:, u, :, :], src[:, :, bass.ds(i * P, P)]).then_inc(ld[u], 16)
                    sp.dma_start(rope[:, u, :, :], rope_dram[bass.ds(i * P, P), :, :]).then_inc(ld[u], 16)
                repeat(sp, NT, load)

            @block.tensor
            def _(pe):
                pe.wait_ge(const, 16)

                def tile(j, u):
                    i = 2 * j + u
                    wait(pe, ld[u], 32 * (j + 1))
                    wait(pe, rot, 3 * (i - 1))
                    wait(pe, vout, i - 1)
                    for m in range(12):
                        last = nc.tensor.transpose(ps[u][:, m // 4, (m % 4) * P:(m % 4 + 1) * P], f[:, u, m, :], ident[:, :])
                    last.then_inc(tr, 1)
                repeat(pe, NT, tile)

            @block.vector
            def _(dve):
                def rotate(j, u):
                    i = 2 * j + u
                    wait(dve, tr, i + 1)
                    wait(dve, nrm, i - 1)
                    x = ps[u][:, 0:2, :].rearrange("p a (h e) -> p (a h) e", e=P)
                    nc.vector.tensor_tensor(t1[:, u, :].rearrange("p (h e) -> p h e", e=P), x,
                                            rope[:, u, 0:1, :].to_broadcast([P, 2 * H, P]), ALU.mult).then_inc(rot, 1)
                    x4 = ps[u][:, 0:2, :].rearrange("p a (h g b e) -> p (a h) g b e", g=2, b=2, e=32)
                    t4 = t2[:, u, :].rearrange("p (h g b e) -> p h g b e", g=2, b=2, e=32)
                    s4 = rope[:, u, 1, :].rearrange("p (g b e) -> p g b e", g=2, b=2)
                    for b in range(2):
                        sb = s4[:, :, b, :].unsqueeze(1).to_broadcast([P, 2 * H, 2, 32])
                        nc.vector.tensor_tensor(t4[:, :, :, b, :], x4[:, :, :, 1 - b, :], sb, ALU.mult).then_inc(rot, 1)

                def norms(j, u):
                    i = 2 * j + u
                    wait(dve, sqs, i + 1)
                    nc.vector.tensor_reduce(out=n8[:, u, 0, :], in_=sq[:, :].rearrange("p (h e) -> p h e", e=P),
                                            axis=AX.X, op=ALU.add).then_inc(ssum, 1)
                    wait(dve, ssum, 2 * i + 1)
                    nc.vector.tensor_scalar(n8[:, u, 1, :], n8[:, u, 0, :], EPS, None, ALU.add).then_inc(ssum, 1)
                    wait(dve, rt, i + 1)
                    nc.vector.reciprocal(n8[:, u, 3, :], n8[:, u, 2, :]).then_inc(rs, 1)
                    wait(dve, rs, 2 * i + 1)
                    nc.vector.tensor_scalar(n8[:, u, 3, 0:H], n8[:, u, 3, 0:H], float(P) ** -0.5, None, ALU.mult).then_inc(rs, 1)

                def tile(j, u):
                    rotate(*after(j, u))
                    norms(j, u)
                rotate(0, 0)
                repeat(dve, NT - 2, tile)
                tile(NT // 2 - 1, 0)
                norms(NT // 2 - 1, 1)

            @block.gpsimd
            def _(pool):
                def add(j, u):
                    wait(pool, rot, 3 * (2 * j + u + 1))
                    nc.gpsimd.tensor_tensor(t1[:, u, :], t1[:, u, :], t2[:, u, :], ALU.add).then_inc(sums, 1)

                def normalise(j, u):
                    i = 2 * j + u
                    wait(pool, sums, i + 1)
                    wait(pool, rs, 2 * (i + 1))
                    wait(pool, stored[u], 16 * j)
                    nc.gpsimd.tensor_tensor(o[:, u, 0:2 * DN].rearrange("p (h e) -> p h e", e=P),
                                            t1[:, u, :].rearrange("p (h e) -> p h e", e=P),
                                            n8[:, u, 3, :].unsqueeze(2).to_broadcast([P, 2 * H, P]), ALU.mult).then_inc(nrm, 1)

                def tile(j, u):
                    add(*after(j, u))
                    normalise(j, u)
                add(0, 0)
                repeat(pool, NT - 2, tile)
                tile(NT // 2 - 1, 0)
                normalise(NT // 2 - 1, 1)

            @block.scalar
            def _(act):
                def value(j, u):
                    i = 2 * j + u
                    wait(act, tr, i + 1)
                    wait(act, stored[u], 16 * j)
                    nc.scalar.activation(o[:, u, 2 * DN:], ps[u][:, 2, :], ACT.Copy).then_inc(vout, 1)

                def squares(j, u):
                    i = 2 * j + u
                    wait(act, sums, i + 1)
                    wait(act, ssum, 2 * i)
                    nc.scalar.activation(sq[:, :], t1[:, u, :], ACT.Square).then_inc(sqs, 1)
                    wait(act, ssum, 2 * (i + 1))
                    nc.scalar.activation(n8[:, u, 2, :], n8[:, u, 1, :], ACT.Sqrt).then_inc(rt, 1)

                def store(i, u):
                    wait(act, nrm, i + 1)
                    wait(act, vout, i + 1)
                    act.dma_start(qkv[bass.ds(i * P, P), :], o[:, u, :]).then_inc(stored[u], 16)

                def tile(j, u):
                    value(j, u)
                    squares(j, u)
                    if not (isinstance(j, int) and j == 0 and u == 0):
                        store(2 * j + u - 1, 1 - u)
                repeat(act, NT, tile)
                store(NT - 1, 1)
                act.wait_ge(stored[0], 16 * (NT // 2))
                act.wait_ge(stored[1], 16 * (NT // 2))


def dn_scan(nc, tag, qkv, col, ident_dram, tri_dram, neg_dram, lev_dram, o_dir):
    with Phase(nc, tag) as ph:
        ident = ph.sb("ident", [P, P])
        tri = ph.sb("tri", [P, 3, P])
        neg = ph.sb("neg", [P, 2, P])
        lev = ph.sb("lev", [P, 2, LEVELS, P])
        D2 = range(2)
        two = lambda name, shape: [ph.sb(f"{name}{d}", shape) for d in D2]
        x = two("x", [P, 2, 3 * DN])
        kb, kd, vb, gt = (two(s, [P, 2, DN]) for s in ("kb", "kd", "vb", "gt"))
        KT_, KBT, QT, EG = (two(s, [P, DN]) for s in ("KT", "KBT", "QT", "EG"))
        QGT, QKD = (two(s, [P, 2, DN]) for s in ("QGT", "QKD"))
        E, AT, X, XT, PM, R, U, W, VN, S = (two(s, [P, DN]) for s in
                                            ("E", "AT", "X", "XT", "PM", "R", "U", "W", "VN", "S"))
        CT = two("CT", [P, LEVELS, DN])
        O = two("O", [P, 2, DN])
        ps = [ph.ps(f"ps{d}", [P, 4, 512]) for d in D2]
        const, zero = ph.sem("const"), ph.sem("zero")
        sems = lambda name: [ph.sem(f"{name}{d}") for d in D2]
        ld = [[ph.sem(f"ld{d}{u}") for u in D2] for d in D2]
        stored = [[ph.sem(f"so{d}{u}") for u in D2] for d in D2]
        s_vb, s_kd, s_kb, s_gt = (sems(s) for s in ("vb", "kd", "kb", "gt"))
        m_kT, m_kbT, m_qT, m_gc, m_kk, m_qk, m_a = (sems(s) for s in
            ("m_kT", "m_kbT", "m_qT", "m_gc", "m_kk", "m_qk", "m_a"))
        m_ax, m_xp, m_px, m_ks, m_u, m_w, m_new, m_o, m_up = (sems(s) for s in
            ("m_ax", "m_xp", "m_px", "m_ks", "m_u", "m_w", "m_new", "m_o", "m_up"))
        kT_in, kbT_in, qT_in, eg, qgT = (sems(s) for s in ("kT_in", "kbT_in", "qT_in", "exp_gc", "qgT"))
        arg, dec, at_, qkd_, ct, xt0, x0, pl, xl_, xtl, r_, u_, w_, vn_, o_, s_ = (sems(s) for s in
            ("arg", "decay", "at", "qkd", "ct", "xt0", "x0", "pl", "xl", "xtl", "r", "u", "w", "vn", "o", "s"))
        h4 = lambda ap: ap.rearrange("p (h e) -> p h e", e=P)
        hd = lambda h: slice(h * P, (h + 1) * P)
        NL = LEVELS - 2

        def tile_of(d, j, u):
            if d == 0:
                return 2 * j + u
            return 1 - u if isinstance(j, int) and j == 0 else j * -2 + (NT + 1 - u)

        def steps(eng, step):
            repeat(eng, NT - 2, step)
            step(NT // 2 - 1, 0)
            step(NT // 2 - 1, 1, False)

        with nc.Block() as block:

            @block.sync
            def _(sp):
                sp.dma_start(ident[:, :], ident_dram).then_inc(const, 16)
                sp.dma_start(tri[:, :, :], tri_dram).then_inc(const, 16)
                sp.dma_start(neg[:, :, :], neg_dram).then_inc(const, 16)
                sp.dma_start(lev[:, :, :, :], lev_dram).then_inc(const, 16)

                def step(j, u):
                    for d in D2:
                        row = at(sp, tile_of(d, j, u) * P)
                        wait(sp, m_qT[d], 2 * j + u - 1)
                        sp.dma_start(x[d][:, u, :], qkv[bass.ds(row, P), :]).then_inc(ld[d][u], 16)
                repeat(sp, NT, step)

            @block.gpsimd
            def _(pool):
                for d in D2:
                    nc.gpsimd.memset(S[d][:, :], 0.0).then_inc(zero, 1)
                pool.wait_ge(const, 64)

                def step(j, u):
                    i = 2 * j + u
                    for d in D2:
                        t = tile_of(d, j, u)
                        g = lambda which: col[:, which, bass.ds(t, 1), d * H:(d + 1) * H].rearrange("p o h -> p (o h)").unsqueeze(2).to_broadcast([P, H, P])
                        part = lambda n: h4(x[d][:, u, n * DN:(n + 1) * DN])
                        wait(pool, ld[d][u], 16 * (j + 1))
                        wait(pool, r_[d], i - 1)
                        nc.gpsimd.tensor_tensor(h4(vb[d][:, u, :]), part(2), g(BETA), ALU.mult).then_inc(s_vb[d], 1)
                        wait(pool, m_up[d], i - 1)
                        nc.gpsimd.tensor_tensor(h4(kd[d][:, u, :]), part(1), g(EKD), ALU.mult).then_inc(s_kd[d], 1)
                        nc.gpsimd.tensor_tensor(h4(kb[d][:, u, :]), part(1), g(BETA), ALU.mult).then_inc(s_kb[d], 1)
                        nc.gpsimd.tensor_tensor(h4(gt[d][:, u, :]), tri[:, d:d + 1, :].to_broadcast([P, H, P]), g(G_),
                                                ALU.mult).then_inc(s_gt[d], 1)
                    for d in D2:
                        wait(pool, qT_in[d], i + 1)
                        wait(pool, eg[d], i + 1)
                        nc.gpsimd.tensor_tensor(QGT[d][:, u, :], QT[d][:, :], EG[d][:, :], ALU.mult).then_inc(qgT[d], 1)
                    for L in range(LEVELS):
                        for d in D2:
                            if L == 0:
                                wait(pool, at_[d], i + 1)
                                wait(pool, m_w[d], i)
                            nc.gpsimd.tensor_tensor(h4(CT[d][:, L, :]), h4(AT[d][:, :]),
                                                    lev[:, 1 - d, L:L + 1, :].to_broadcast([P, H, P]), ALU.mult).then_inc(ct[d], 1)
                            if L == 0:
                                wait(pool, ct[d], LEVELS * i + 1)
                                wait(pool, m_new[d], i)
                                nc.gpsimd.tensor_tensor(h4(XT[d][:, :]), ident[:, :].unsqueeze(1).to_broadcast([P, H, P]),
                                                        h4(CT[d][:, 0, :]), ALU.subtract).then_inc(xt0[d], 1)
                repeat(pool, NT, step)

            @block.tensor
            def _(pe):
                pe.wait_ge(const, 64)
                pe.wait_ge(zero, 2)

                def heads(bank, lhsT, rhs, start=True, stop=True):
                    for h in range(H):
                        last = nc.tensor.matmul(bank[:, hd(h)], lhsT[:, hd(h)], rhs[:, hd(h)], start=start, stop=stop)
                    return last

                def turn(bank, src):
                    for h in range(H):
                        last = nc.tensor.transpose(bank[:, hd(h)], src[:, hd(h)], ident[:, :])
                    return last

                def prepare(piece, j, u):
                    i = 2 * j + u
                    for d in D2:
                        bank = ps[d][:, 3, :]
                        if piece == "kT":
                            wait(pe, ld[d][u], 16 * (j + 1))
                            wait(pe, r_[d], i)
                            turn(bank, x[d][:, u, DN:2 * DN]).then_inc(m_kT[d], 1)
                        elif piece == "kbT":
                            wait(pe, s_kb[d], i + 1)
                            wait(pe, kT_in[d], i + 1)
                            turn(bank, kb[d][:, u, :]).then_inc(m_kbT[d], 1)
                        elif piece == "gc":
                            wait(pe, s_gt[d], i + 1)
                            wait(pe, kbT_in[d], i + 1)
                            nc.tensor.matmul(bank, tri[:, 2, :], gt[d][:, u, :], start=True, stop=True).then_inc(m_gc[d], 1)
                        elif piece == "qT":
                            wait(pe, eg[d], i + 1)
                            turn(bank, x[d][:, u, 0:DN]).then_inc(m_qT[d], 1)
                        elif piece == "kk":
                            wait(pe, qT_in[d], i + 1)
                            heads(bank, KT_[d], KBT[d]).then_inc(m_kk[d], 1)
                        elif piece == "qk":
                            wait(pe, at_[d], i + 1)
                            heads(bank, KT_[d], QT[d]).then_inc(m_qk[d], 1)
                        elif piece == "a":
                            wait(pe, ct[d], LEVELS * i + 1)
                            wait(pe, qkd_[d], i + 1)
                            turn(bank, CT[d][:, 0, :]).then_inc(m_a[d], 1)

                for piece in ("kT", "kbT", "gc", "qT", "kk", "qk", "a"):
                    prepare(piece, 0, 0)

                def step(j, u, more=True):
                    i = 2 * j + u
                    following = after(j, u)
                    for L in range(NL):
                        n = NL * i + L
                        for d in D2:
                            if L == 0:
                                wait(pe, x0[d], i + 1)
                                wait(pe, o_[d], i)
                            else:
                                wait(pe, xl_[d], (NL - 1) * i + L)
                            wait(pe, ct[d], LEVELS * i + L + 2)
                            heads(ps[d][:, 0, :], CT[d][:, L + 1, :], X[d]).then_inc(m_ax[d], 1)
                        if L and more:
                            prepare(("kT", "kbT", "gc", "qT")[L - 1], *following)
                        for d in D2:
                            wait(pe, pl[d], n + 1)
                            if L:
                                wait(pe, xtl[d], n)
                            else:
                                wait(pe, xt0[d], i + 1)
                                wait(pe, s_[d], i)
                                wait(pe, vn_[d], i)
                            if L < NL - 1:
                                heads(ps[d][:, 1, :], XT[d], PM[d]).then_inc(m_xp[d], 1)
                            heads(ps[d][:, 2, :], PM[d], XT[d]).then_inc(m_px[d], 1)
                        if L == 0:
                            for d in D2:
                                heads(ps[d][:, 3, :], KT_[d], S[d]).then_inc(m_ks[d], 1)
                    for d in D2:
                        wait(pe, xtl[d], NL * (i + 1))
                        wait(pe, r_[d], i + 1)
                        heads(ps[d][:, 0, :], XT[d], R[d]).then_inc(m_u[d], 1)
                    if more:
                        prepare("kk", *following)
                    for d in D2:
                        wait(pe, u_[d], i + 1)
                        wait(pe, xl_[d], (NL - 1) * (i + 1))
                        wait(pe, ct[d], LEVELS * (i + 1))
                        heads(ps[d][:, 1, :], CT[d][:, LEVELS - 1, :], U[d]).then_inc(m_w[d], 1)
                    if more:
                        prepare("qk", *following)
                    for d in D2:
                        wait(pe, w_[d], i + 1)
                        heads(ps[d][:, 2, :], XT[d], W[d]).then_inc(m_new[d], 1)
                    for d in D2:
                        wait(pe, vn_[d], i + 1)
                        wait(pe, qgT[d], i + 1)
                        for h in range(H):
                            nc.tensor.matmul(ps[d][:, 0, hd(h)], QGT[d][:, u, hd(h)], S[d][:, hd(h)], start=True, stop=False)
                            last = nc.tensor.matmul(ps[d][:, 0, hd(h)], QKD[d][:, u, hd(h)], VN[d][:, hd(h)], start=False, stop=True)
                        last.then_inc(m_o[d], 1)
                        heads(ps[d][:, 1, :], kd[d][:, u, :], VN[d]).then_inc(m_up[d], 1)
                    if more:
                        prepare("a", *following)
                steps(pe, step)

            @block.scalar
            def _(act):
                def prepare(piece, j, u):
                    i = 2 * j + u
                    for d in D2:
                        bank = ps[d][:, 3, :]
                        if piece == "kT":
                            wait(act, m_kT[d], i + 1)
                            nc.scalar.activation(KT_[d][:, :], bank, ACT.Copy).then_inc(kT_in[d], 1)
                        elif piece == "exp":
                            wait(act, arg[d], H * (i + 1))
                            nc.scalar.activation(E[d][:, :], E[d][:, :], ACT.Exp).then_inc(dec[d], 1)
                        elif piece == "exp_gc":
                            wait(act, arg[d], H * (i + 1))
                            wait(act, qgT[d], i)
                            nc.scalar.activation(EG[d][:, :], bank, ACT.Exp).then_inc(eg[d], 1)
                        elif piece == "qT":
                            wait(act, m_qT[d], i + 1)
                            nc.scalar.activation(QT[d][:, :], bank, ACT.Copy).then_inc(qT_in[d], 1)

                for piece in ("kT", "exp_gc", "exp", "qT"):
                    prepare(piece, 0, 0)

                def step(j, u, more=True):
                    i = 2 * j + u
                    following = after(j, u)
                    for L in range(NL):
                        for d in D2:
                            wait(act, m_ax[d], NL * i + L + 1)
                            nc.scalar.activation(PM[d][:, :], ps[d][:, 0, :], ACT.Copy).then_inc(pl[d], 1)
                        if more and L == 1:
                            prepare("kT", *following)
                        if more and L == 3:
                            prepare("exp_gc", *following)
                        if more and L == 4:
                            prepare("qT", *following)
                            prepare("exp", *following)
                    for d in D2:
                        wait(act, m_u[d], i + 1)
                        nc.scalar.activation(U[d][:, :], ps[d][:, 0, :], ACT.Copy).then_inc(u_[d], 1)
                    for d in D2:
                        wait(act, m_w[d], i + 1)
                        nc.scalar.activation(W[d][:, :], ps[d][:, 1, :], ACT.Copy).then_inc(w_[d], 1)
                    for d in D2:
                        wait(act, stored[d][u], 16 * j)
                        wait(act, m_o[d], i + 1)
                        nc.scalar.activation(O[d][:, u, :], ps[d][:, 0, :], ACT.Copy).then_inc(o_[d], 1)
                        wait(act, o_[d], i + 1)
                        act.dma_start(o_dir[d][bass.ds(tile_of(d, j, u) * P, P), :], O[d][:, u, :]).then_inc(stored[d][u], 16)
                steps(act, step)
                for d in D2:
                    for u in D2:
                        act.wait_ge(stored[d][u], 16 * (NT // 2))

            @block.vector
            def _(dve):
                dve.wait_ge(const, 64)
                dve.wait_ge(zero, 2)

                c = lambda d, which, j, u, h: col[:, which, bass.ds(tile_of(d, j, u), 1), d * H + h:d * H + h + 1].rearrange("p a b -> p (a b)")

                def prepare(piece, j, u):
                    i = 2 * j + u
                    for d in D2:
                        bank = ps[d][:, 3, :]
                        if piece == "kbT":
                            wait(dve, m_kbT[d], i + 1)
                            nc.vector.tensor_copy(KBT[d][:, :], bank).then_inc(kbT_in[d], 1)
                        elif piece == "gc":
                            wait(dve, m_gc[d], i + 1)
                            for h in range(H):
                                nc.vector.scalar_tensor_tensor(out=E[d][:, hd(h)], in0=bank[:, hd(h)], scalar=c(d, GC, j, u, h),
                                                               in1=neg[:, d, :], op0=ALU.subtract, op1=ALU.add).then_inc(arg[d], 1)
                        elif piece == "kk":
                            wait(dve, dec[d], i + 1)
                            wait(dve, ct[d], LEVELS * i)
                            wait(dve, m_kk[d], i + 1)
                            nc.vector.tensor_tensor(AT[d][:, :], bank, E[d][:, :], ALU.mult).then_inc(at_[d], 1)
                        elif piece == "qk":
                            wait(dve, m_qk[d], i + 1)
                            nc.vector.tensor_tensor(QKD[d][:, u, :], bank, E[d][:, :], ALU.mult).then_inc(qkd_[d], 1)
                        elif piece == "a":
                            wait(dve, m_a[d], i + 1)
                            nc.vector.tensor_tensor(h4(X[d][:, :]), ident[:, :].unsqueeze(1).to_broadcast([P, H, P]),
                                                    h4(bank), ALU.subtract).then_inc(x0[d], 1)

                for piece in ("kbT", "gc", "kk", "qk", "a"):
                    prepare(piece, 0, 0)

                def step(j, u, more=True):
                    i = 2 * j + u
                    following = after(j, u)
                    for L in range(NL):
                        n = NL * i + L
                        if more and L in (2, 3):
                            prepare(("kbT", "gc")[L - 2], *following)
                        for d in D2:
                            wait(dve, m_px[d], n + 1)
                            if L == 0:
                                wait(dve, x0[d], i + 1)
                            if L < NL - 1:
                                nc.vector.tensor_tensor(X[d][:, :], X[d][:, :], ps[d][:, 1, :], ALU.subtract).then_inc(xl_[d], 1)
                            nc.vector.tensor_tensor(XT[d][:, :], XT[d][:, :], ps[d][:, 2, :], ALU.subtract).then_inc(xtl[d], 1)
                        if L == 0:
                            for d in D2:
                                wait(dve, m_ks[d], i + 1)
                                wait(dve, s_vb[d], i + 1)
                                for h in range(H):
                                    last = nc.vector.scalar_tensor_tensor(out=R[d][:, hd(h)], in0=ps[d][:, 3, hd(h)],
                                                                          scalar=c(d, NBEG, j, u, h), in1=vb[d][:, u, hd(h)],
                                                                          op0=ALU.mult, op1=ALU.add)
                                last.then_inc(r_[d], 1)
                    if more:
                        prepare("kk", *following)
                        prepare("qk", *following)
                    for d in D2:
                        wait(dve, m_new[d], i + 1)
                        wait(dve, u_[d], i + 1)
                        nc.vector.tensor_tensor(VN[d][:, :], U[d][:, :], ps[d][:, 2, :], ALU.subtract).then_inc(vn_[d], 1)
                    for d in D2:
                        wait(dve, m_up[d], i + 1)
                        for h in range(H):
                            last = nc.vector.scalar_tensor_tensor(out=S[d][:, hd(h)], in0=S[d][:, hd(h)],
                                                                  scalar=c(d, ELAST, j, u, h), in1=ps[d][:, 1, hd(h)],
                                                                  op0=ALU.mult, op1=ALU.add)
                        last.then_inc(s_[d], 1)
                    if more:
                        prepare("a", *following)
                steps(dve, step)


NH, DH = 4, 64
KR = 8
DR = 2 * KR - 1


def attention(nc, tag, proj, rpb, ident_dram, onehot_dram, na_out, with_ctx):
    QR = [(0, 4, "low"), (4, 28, "mid"), (28, ROWS, "high")]
    NLOC, NK = KR * GRID, KR * GRID + CTX
    NCQ = CTX // GRID if with_ctx else 0
    with Phase(nc, tag) as ph:
        ident = ph.sb("ident", [P, P])
        hot = ph.sb("hot", [32, GRID, P])
        rp = ph.sb("rp", [32, NH * DR])
        bias = ph.sb("bias", [P, 2, DR, GRID])
        qT = ph.sb("qT", [P, 2, T])
        kT = ph.sb("kT", [P, 2, T])
        vT = ph.sb("vT", [P, 2, T])
        NV = CTX // GRID // 2 + (SEQ // GRID - 1)
        v = ph.sb("v", [P, NV, NH * DH])
        qd = ph.sb("qd", [P, 2, P])
        s = ph.sb("s", [P, 2, NK])
        pr = ph.sb("pr", [P, 2, NK])
        pT = ph.sb("pT", [P, 2, NK])
        m = ph.sb("m", [P, 2, 4])
        spare = ph.sb("spare", [P, 2])
        o = ph.sb("o", [P, 2, DH])
        oT = ph.sb("oT", [P, 2, T])
        ps = [ph.ps(f"ps{p}", [P, 4, 512]) for p in range(2)]
        ld, zero, pre_pe, pre_v = ph.sem("ld"), ph.sem("zero"), ph.sem("pre_pe"), ph.sem("pre_v")
        pre_a = ph.sem("pre_a")
        sems = lambda name: [ph.sem(f"{name}{p}") for p in range(2)]
        staged, scored, biased, ctx_s, mx, negm, expd = (sems(x) for x in
            ("staged", "scored", "biased", "ctx_s", "mx", "negm", "expd"))
        turned, pt_a, pt_v, attended, inv, scaled = (sems(x) for x in
            ("turned", "pt_a", "pt_v", "attended", "inv", "scaled"))
        oturned, outp = ph.sem("oturned"), ph.sem("outp")
        st = ph.sem("st")
        SC = DH ** -0.5
        with nc.Block() as block:

            @block.sync
            def _(sp):
                sp.dma_start(ident[:, :], ident_dram).then_inc(ld, 16)
                sp.dma_start(hot[:, :, :], onehot_dram).then_inc(ld, 16)
                sp.wait_ge(zero, 1)
                sp.dma_start(rp[0:31, :], rpb.rearrange("h a b -> b (h a)"), allow_slow_non_contiguous=True).then_inc(ld, 16)
                for t_, c in ((qT, C_NAQ), (kT, C_NAK), (vT, C_NAV)):
                    sp.dma_start(t_[:, :, :], proj[c:c + 2 * P, :].rearrange("(f p) t -> p f t", p=P)).then_inc(ld, 16)
                sp.wait_ge(outp, ROWS + NCQ)
                lo = 0 if with_ctx else CTX
                for p in range(2):
                    for h in range(2):
                        r = (2 * p + h) * DH
                        sp.dma_start(na_out[r:r + DH, lo:T], oT[p * DH:(p + 1) * DH, h, lo:T]).then_inc(st, 16)
                sp.wait_ge(st, 64)

            def steps(eng, body):
                def both(i, q0):
                    for p in range(2):
                        body(i, q0, p)
                both(0, CTX)
                with eng.Fori(1, ROWS) as i:
                    both(i, i * GRID + CTX)
                for n in range(NCQ):
                    both(ROWS + n, n * GRID)

            @block.gpsimd
            def _(pool):
                nc.gpsimd.memset(rp[0:32, :], 1.0).then_inc(zero, 1)
                nc.gpsimd.memset(qd[:, :, :], 0.0).then_inc(zero, 1)
                pool.wait_ge(zero, 2)
                pool.wait_ge(ld, 96)

                def row(i, q0, p):
                    wait(pool, scored[p], i)
                    for h in range(2):
                        last = nc.gpsimd.tensor_copy(qd[h * DH:(h + 1) * DH, p, h * GRID:(h + 1) * GRID],
                                                     qT[h * DH:(h + 1) * DH, p, bass.ds(q0, GRID)])
                    last.then_inc(staged[p], 1)
                steps(pool, row)

            @block.tensor
            def _(pe):
                pe.wait_ge(ld, 96)
                pe.wait_ge(pre_a, 1)
                for c in range(GRID):
                    if c >= 8:
                        pe.wait_ge(pre_v, c - 7)
                    nc.tensor.matmul(ps[c // 4 % 2][:, c % 4, 0:NH * DR], hot[:, c, :], rp[:, :], start=True, stop=True).then_inc(pre_pe, 1)
                for w in range(NV):
                    t0 = w * P if w < 2 else CTX + (w - 2) * GRID
                    pe.wait_ge(pre_v, GRID + w - 7)
                    for f in range(2):
                        last = nc.tensor.transpose(ps[w // 4 % 2][:, w % 4, f * P:(f + 1) * P], vT[:, f, t0:t0 + P], ident[:, :])
                    last.then_inc(pre_pe, 1)
                pe.wait_ge(pre_v, GRID + NV)

                def scores(i, band, ctx_only=False):
                    for p in range(2):
                        wait(pe, staged[p], i + 1)
                        if not ctx_only:
                            wait(pe, biased[p], i)
                            nc.tensor.matmul(ps[p][:, 0, :], qd[:, p, :], kT[:, p, bass.ds(band * GRID + CTX, NLOC)],
                                             start=True, stop=True)
                        wait(pe, ctx_s[p], i)
                        nc.tensor.matmul(ps[p][:, 1, 0:CTX], qd[:, p, :], kT[:, p, 0:CTX], start=True, stop=True).then_inc(scored[p], 1)

                def turn(i, ctx_only=False):
                    for p in range(2):
                        wait(pe, expd[p], i + 1)
                        wait(pe, pt_a[p], i)
                        wait(pe, pt_v[p], i)
                        if p == 0:
                            wait(pe, outp, i)
                        for c in range(4 if ctx_only else 0, 6):
                            last = nc.tensor.transpose(ps[p][:, 2 + c // 4, (c % 4) * P:(c % 4 + 1) * P],
                                                       pr[:, p, c * P:(c + 1) * P], ident[:, :])
                        last.then_inc(turned[p], 1)

                def values(i, band, ctx_only=False):
                    first = 4 if ctx_only else 0
                    for p in range(2):
                        wait(pe, pt_a[p], i + 1)
                        wait(pe, pt_v[p], i + 1)
                        wait(pe, scaled[p], 2 * i)
                        for c in range(first, 6):
                            if c < 4:
                                rhs = v[:, bass.ds(band + (2 + 2 * c), 1), p * P:(p + 1) * P].rearrange("k a e -> k (a e)")
                            else:
                                rhs = v[:, c - 4, p * P:(p + 1) * P]
                            last = nc.tensor.matmul(ps[p][:, 3, 256:384], pT[:, p, c * P:(c + 1) * P], rhs,
                                                    start=(c == first), stop=(c == 5))
                        last.then_inc(attended[p], 1)
                    for p in range(2):
                        wait(pe, scaled[p], 2 * (i + 1))
                    nc.tensor.transpose(ps[0][:, 3, 384:512], o[:, :, :].rearrange("q p e -> q (p e)"), ident[:, :]).then_inc(oturned, 1)

                def one(i, band, prev):
                    turn(i + -1)
                    scores(i, band)
                    values(i + -1, prev)
                scores(0, 0)
                with pe.Fori(1, 5) as i:
                    one(i, 0, 0)
                with pe.Fori(5, ROWS - 3) as i:
                    one(i, i + -4, i + -5)
                with pe.Fori(ROWS - 3, ROWS) as i:
                    one(i, ROWS - KR, ROWS - KR)
                turn(ROWS - 1)
                values(ROWS - 1, ROWS - KR)
                for n in range(NCQ):
                    scores(ROWS + n, 0, True)
                    turn(ROWS + n, True)
                    values(ROWS + n, 0, True)

            @block.scalar
            def _(act):
                act.wait_ge(zero, 1)
                act.wait_ge(ld, 96)
                nc.scalar.activation(rp[0:1, 0:1], rp[0:1, 0:1], ACT.Copy).then_inc(pre_a, 1)

                def row(i, q0, p, ctx_only=False):
                    lo = NLOC if ctx_only else 0
                    wait(act, scored[p], i + 1)
                    wait(act, expd[p], i)
                    nc.scalar.activation(s[:, p, NLOC:NK], ps[p][:, 1, 0:CTX], ACT.Copy, scale=SC).then_inc(ctx_s[p], 1)
                    wait(act, negm[p], i + 1)
                    wait(act, turned[p], i)
                    wait(act, inv[p], i)
                    nc.scalar.activation(pr[:, p, lo:NK], s[:, p, lo:NK], ACT.Exp, bias=m[:, p, 1:2],
                                         accum_out=m[:, p, 2:3]).then_inc(expd[p], 1)

                def evac(i, p, ctx_only=False):
                    wait(act, turned[p], i + 1)
                    wait(act, attended[p], i)
                    if ctx_only:
                        nc.scalar.activation(spare[:, p:p + 1], m[:, p, 2:3], ACT.Copy).then_inc(pt_a[p], 1)
                    else:
                        nc.scalar.activation(pT[:, p, 0:NLOC], ps[p][:, 2, :], ACT.Copy).then_inc(pt_a[p], 1)

                for p in range(2):
                    row(0, None, p)
                with act.Fori(1, ROWS) as i:
                    for p in range(2):
                        evac(i + -1, p)
                    for p in range(2):
                        row(i, None, p)
                for p in range(2):
                    evac(ROWS - 1, p)
                for n in range(NCQ):
                    for p in range(2):
                        row(ROWS + n, None, p, True)
                    for p in range(2):
                        evac(ROWS + n, p, True)

            @block.vector
            def _(dve):
                for c in range(GRID):
                    dve.wait_ge(pre_pe, c + 1)
                    for hh in range(2):
                        last = nc.vector.tensor_copy(
                            bias[hh * GRID:(hh + 1) * GRID, :, :, c],
                            ps[c // 4 % 2][hh * GRID:(hh + 1) * GRID, c % 4, 0:NH * DR].rearrange("q (a h d) -> q a h d", a=2, h=2)[:, :, hh, :])
                    last.then_inc(pre_v, 1)
                for w in range(NV):
                    dve.wait_ge(pre_pe, GRID + w + 1)
                    nc.vector.tensor_copy(v[:, w, :], ps[w // 4 % 2][:, w % 4, 0:NH * DH]).then_inc(pre_v, 1)
                dve.wait_ge(pre_v, GRID + NV)

                def soften(i, dr0, ctx_only=False):
                    lo = NLOC if ctx_only else 0
                    for p in range(2):
                        wait(dve, scored[p], i + 1)
                        wait(dve, expd[p], i)
                        if not ctx_only:
                            nc.vector.scalar_tensor_tensor(
                                out=s[:, p, 0:NLOC], in0=ps[p][:, 0, :], scalar=SC,
                                in1=bias[:, p, bass.ds(dr0, KR), :].rearrange("q a b -> q (a b)"),
                                op0=ALU.mult, op1=ALU.add).then_inc(biased[p], 1)
                            wait(dve, biased[p], i + 1)
                        wait(dve, ctx_s[p], i + 1)
                        nc.vector.tensor_reduce(out=m[:, p, 0:1], in_=s[:, p, lo:NK], axis=AX.X, op=ALU.max).then_inc(mx[p], 1)
                        wait(dve, mx[p], i + 1)
                        nc.vector.tensor_scalar(m[:, p, 1:2], m[:, p, 0:1], -1.0, None, ALU.mult).then_inc(negm[p], 1)

                def turned_in(i):
                    for p in range(2):
                        wait(dve, turned[p], i + 1)
                        wait(dve, attended[p], i)
                        nc.vector.tensor_copy(pT[:, p, NLOC:NK], ps[p][:, 3, 0:CTX]).then_inc(pt_v[p], 1)
                        nc.vector.reciprocal(m[:, p, 3:4], m[:, p, 2:3]).then_inc(inv[p], 1)

                def leave(i, q0):
                    for p in range(2):
                        wait(dve, attended[p], i + 1)
                        wait(dve, inv[p], i + 1)
                        wait(dve, oturned, i)
                        for h in range(2):
                            sl = slice(h * GRID, (h + 1) * GRID)
                            nc.vector.tensor_scalar(o[sl, p, :], ps[p][sl, 3, 256 + h * DH:256 + (h + 1) * DH], m[sl, p, 3:4], None,
                                                    ALU.mult).then_inc(scaled[p], 1)
                    wait(dve, oturned, i + 1)
                    nc.vector.tensor_copy(oT[:, :, bass.ds(q0, GRID)],
                                          ps[0][:, 3, 384:512].rearrange("e (h q) -> e h q", h=2)).then_inc(outp, 1)

                def one(i, dr0):
                    turned_in(i + -1)
                    soften(i, dr0)
                    leave(i + -1, (i + -1) * GRID + CTX)
                soften(0, KR - 1)
                with dve.Fori(1, 5) as i:
                    one(i, i * -1 + (KR - 1))
                with dve.Fori(5, ROWS - 3) as i:
                    one(i, 3)
                with dve.Fori(ROWS - 3, ROWS) as i:
                    one(i, i * -1 + (ROWS - 1))
                turned_in(ROWS - 1)
                leave(ROWS - 1, (ROWS - 1) * GRID + CTX)
                for n in range(NCQ):
                    soften(ROWS + n, 0, True)
                    turned_in(ROWS + n)
                    leave(ROWS + n, n * GRID)


def output_tiles(nc, tag, tiles, proj, na, o_dir, hy, norm_w, w_out, gate_dram, mod_of, ident_dram, resid, dest):
    t_lo, t_hi = tiles
    n = t_hi - t_lo
    with Phase(nc, tag) as ph:
        ident = ph.sb("ident", [P, P])
        wo = ph.sb("wo", [P, KT, D])
        nw = ph.sb("nw", [P, P])
        gg = ph.sb("gg", [P, D])
        z = ph.sb("z", [P, 2, KT, P])
        mix = ph.sb("mix", [P, 2, KT, P])
        x = ph.sb("x", [P, 2, D])
        of, ob = ph.sb("of", [P, 2, DN]), ph.sb("ob", [P, 2, DN])
        osum = ph.sb("osum", [P, DN])
        on = ph.sb("on", [P, 2, DN])
        sq = ph.sb("sq", [P, D])
        sq4 = ph.sb("sq4", [P, DN])
        c4 = ph.sb("c4", [P, 4, H])
        c1 = ph.sb("c1", [P, 4])
        y = ph.sb("y", [P, D])
        out = ph.sb("out", [P, 2, D])
        psT = ph.ps("psT", [P, 2, 512])
        psY = ph.ps("psY", [P, 2, 2, 512])
        const = ph.sem("const")
        ld, stored = [ph.sem("ld0"), ph.sem("ld1")], [ph.sem("so0"), ph.sem("so1")]
        (summed, sq_o, chain, rt4, normed, turned, zs, gated, prod, sq_y, chain1, rt1, scaled, added) = (ph.sem(s) for s in
            ("summed", "sq_o", "chain", "rt4", "normed", "turned", "zs", "gated", "prod", "sq_y", "chain1", "rt1", "scaled", "added"))
        inv_y, inv_, gdn = ph.sem("inv_y"), ph.sem("inv"), ph.sem("gdn")
        with nc.Block() as block:

            @block.sync
            def _(sp):
                sp.dma_start(ident[:, :], ident_dram).then_inc(const, 16)
                sp.dma_start(wo[:, :, :], w_out.rearrange("(k p) n -> p k n", p=P)).then_inc(const, 16)
                sp.dma_start(nw[:, :], norm_w.partition_broadcast(P)).then_inc(const, 16)
                sp.dma_start(gg[:, :], gate_dram[mod_of].partition_broadcast(P)).then_inc(const, 16)

                def load(j, u):
                    i = 2 * j + u
                    tok = at(sp, (i + t_lo) * P)
                    row = at(sp, i * P)
                    wait(sp, added, i - 1)
                    fm = lambda ap, c, k, t0=tok: ap[c:c + k * P, bass.ds(t0, P)].rearrange("(f p) t -> p f t", p=P)
                    sp.dma_start(z[:, u, 0:2, :], fm(proj, C_NAZ, 2)).then_inc(ld[u], 16)
                    sp.dma_start(z[:, u, 2:8, :][:, 0:4, :], fm(proj, C_DNZ, 4)).then_inc(ld[u], 16)
                    sp.dma_start(z[:, u, 6:8, :], fm(proj, C_HYZ, 2)).then_inc(ld[u], 16)
                    sp.dma_start(mix[:, u, 0:2, :], fm(na, 0, 2)).then_inc(ld[u], 16)
                    sp.dma_start(mix[:, u, 6:8, :], fm(hy, 0, 2, row)).then_inc(ld[u], 16)
                    sp.dma_start(of[:, u, :], o_dir[0][bass.ds(tok, P), :]).then_inc(ld[u], 16)
                    sp.dma_start(ob[:, u, :], o_dir[1][bass.ds(tok, P), :]).then_inc(ld[u], 16)
                    sp.dma_start(x[:, u, :], resid[bass.ds(row, P), :]).then_inc(ld[u], 16)
                repeat(sp, n, load)

            @block.gpsimd
            def _(pool):
                pool.wait_ge(const, 64)

                def tile(j, u):
                    i = 2 * j + u
                    wait(pool, ld[u], 128 * (j + 1))
                    wait(pool, normed, 2 * i)
                    nc.gpsimd.tensor_tensor(osum[:, :], of[:, u, :], ob[:, u, :], ALU.add).then_inc(summed, 1)
                    wait(pool, zs, i + 1)
                    nc.gpsimd.tensor_tensor(mix[:, u, 0:2, :], mix[:, u, 0:2, :], z[:, u, 0:2, :], ALU.mult)
                    nc.gpsimd.tensor_tensor(mix[:, u, 6:8, :], mix[:, u, 6:8, :], z[:, u, 6:8, :], ALU.mult).then_inc(gated, 1)
                    if not (isinstance(i, int) and i == 0):
                        finish(i + -1, j - 1 if u == 0 and isinstance(j, int) else j + (u - 1), 1 - u)

                def finish(i, j, u):
                    wait(pool, scaled, i + 1)
                    wait(pool, stored[u], 16 * j)
                    nc.gpsimd.tensor_tensor(out[:, u, :], x[:, u, :], y[:, :], ALU.add).then_inc(added, 1)
                repeat(pool, n, tile)
                finish(n - 1, n // 2 - 1, 1)

            @block.scalar
            def _(act):
                def tile(j, u):
                    i = 2 * j + u
                    wait(act, ld[u], 128 * (j + 1))
                    nc.scalar.activation(z[:, u, :, :], z[:, u, :, :], ACT.Silu).then_inc(zs, 1)
                    wait(act, summed, i + 1)
                    wait(act, chain, 2 * i)
                    nc.scalar.activation(sq4[:, :], osum[:, :], ACT.Square).then_inc(sq_o, 1)
                    wait(act, chain, 2 * (i + 1))
                    nc.scalar.activation(c4[:, 2, :], c4[:, 1, :], ACT.Sqrt).then_inc(rt4, 1)
                    if not (isinstance(i, int) and i == 0):
                        squares(i + -1, 1 - u)
                    if not isinstance(i, int):
                        store(i + -2, u)

                def squares(i, u):
                    wait(act, prod, i + 1)
                    wait(act, chain1, i)
                    nc.scalar.activation(sq[:, :], psY[:, u, :, :].rearrange("p a b -> p (a b)"), ACT.Square,
                                         accum_out=c1[:, 0:1]).then_inc(sq_y, 1)
                    wait(act, chain1, i + 1)
                    nc.scalar.activation(c1[:, 2:3], c1[:, 1:2], ACT.Sqrt).then_inc(rt1, 1)

                def store(i, u):
                    wait(act, added, i + 1)
                    act.dma_start(dest[bass.ds(i * P, P), :], out[:, u, :]).then_inc(stored[u], 16)
                repeat(act, n, tile)
                squares(n - 1, 1)
                store(n - 2, 0)
                store(n - 1, 1)
                for u in range(2):
                    act.wait_ge(stored[u], 16 * (n // 2))

            @block.vector
            def _(dve):
                dve.wait_ge(const, 64)

                def tile(j, u):
                    i = 2 * j + u
                    wait(dve, sq_o, i + 1)
                    nc.vector.tensor_reduce(out=c4[:, 0, :], in_=sq4[:, :].rearrange("p (h e) -> p h e", e=P), axis=AX.X,
                                            op=ALU.add).then_inc(chain, 1)
                    wait(dve, chain, 2 * i + 1)
                    nc.vector.tensor_scalar(c4[:, 1, :], c4[:, 0, :], 1.0 / P, EPS, ALU.mult, ALU.add).then_inc(chain, 1)
                    wait(dve, rt4, i + 1)
                    nc.vector.reciprocal(c4[:, 3, :], c4[:, 2, :]).then_inc(inv_, 1)
                    wait(dve, inv_, i + 1)
                    wait(dve, turned, i - 1)
                    o4 = on[:, u, :].rearrange("p (h e) -> p h e", e=P)
                    nc.vector.tensor_tensor(o4, osum[:, :].rearrange("p (h e) -> p h e", e=P),
                                            c4[:, 3, :].unsqueeze(2).to_broadcast([P, H, P]), ALU.mult).then_inc(normed, 1)
                    wait(dve, normed, 2 * i + 1)
                    nc.vector.tensor_tensor(o4, o4, nw[:, :].unsqueeze(1).to_broadcast([P, H, P]), ALU.mult).then_inc(normed, 1)
                    wait(dve, turned, i + 1)
                    wait(dve, zs, i + 1)
                    nc.vector.tensor_tensor(mix[:, u, 2:6, :], psT[:, u, :].rearrange("p (h e) -> p h e", e=P),
                                            z[:, u, 2:6, :], ALU.mult).then_inc(gdn, 1)
                    if not (isinstance(i, int) and i == 0):
                        finish(i + -1, 1 - u)

                def finish(i, u):
                    wait(dve, sq_y, i + 1)
                    wait(dve, scaled, i)
                    nc.vector.tensor_scalar(c1[:, 1:2], c1[:, 0:1], 1.0 / D, EPS, ALU.mult, ALU.add).then_inc(chain1, 1)
                    wait(dve, rt1, i + 1)
                    nc.vector.reciprocal(c1[:, 3:4], c1[:, 2:3]).then_inc(inv_y, 1)
                    wait(dve, inv_y, i + 1)
                    wait(dve, added, i)
                    nc.vector.scalar_tensor_tensor(out=y[:, :], in0=psY[:, u, :, :].rearrange("p a b -> p (a b)"),
                                                   scalar=c1[:, 3:4], in1=gg[:, :], op0=ALU.mult, op1=ALU.mult).then_inc(scaled, 1)
                repeat(dve, n, tile)
                finish(n - 1, 1)
            
            @block.tensor
            def _(pe):
                pe.wait_ge(const, 64)

                def tile(j, u):
                    i = 2 * j + u
                    wait(pe, normed, 2 * (i + 1))
                    wait(pe, gdn, i - 1)
                    for h in range(H):
                        last = nc.tensor.transpose(psT[:, u, h * P:(h + 1) * P], on[:, u, h * P:(h + 1) * P], ident[:, :])
                    last.then_inc(turned, 1)
                    wait(pe, gdn, i + 1)
                    wait(pe, gated, i + 1)
                    wait(pe, scaled, i - 1)
                    for half in range(2):
                        for k in range(KT):
                            last = nc.tensor.matmul(psY[:, u, half, :], mix[:, u, k, :], wo[:, k, half * 512:(half + 1) * 512],
                                                    start=(k == 0), stop=(k == KT - 1))
                    last.then_inc(prod, 1)
                repeat(pe, n, tile)


HW = 256
HID, EMB = 64, 33
N1, N2 = 32, P
KS = N1 // 2 + 1
R0 = N1
ROUND = 1.5 * 2.0 ** 23
PI2_HI, PI2_LO = 6.28125, 2 * math.pi - 6.28125


def hyena_filters(nc, tag, feats, w1, b1, w2, b2, w3, b3, freq, wout, win, win_ctx, sums, sums_ctx):
    with Phase(nc, tag) as ph:
        z = ph.sb("z", [EMB, T])
        w = ph.sb("w", [HID, 3, HID])
        col = ph.sb("col", [HID, 2, 3])
        wo = ph.sb("wo", [HID, 4 * HW])
        hid = ph.sb("hid", [HID, T])
        y = ph.sb("y", [HID, T])
        k = ph.sb("k", [HID, T])
        wi = ph.sb("wi", [P, 2, SEQ])
        wc = ph.sb("wc", [P, 2, 2, HW])
        F, B = ph.sb("F", [P, SEQ]), ph.sb("B", [P, SEQ])
        sd = ph.sb("sd", [P, 2, SEQ])
        FB = ph.sb("FB", [P, 2, 2, HW])
        sc = ph.sb("sc", [P, 2, 2, 2, HW])
        ps = ph.ps("ps", [P, 8, 512])
        ld, zero, mm, v, sn, evf, evb, pool_s, st, stc = (ph.sem(s) for s in
            ("ld", "zero", "mm", "v", "sn", "evf", "evb", "pool", "st", "stc"))
        taps, evc, pc = ph.sem("taps"), ph.sem("evc"), ph.sem("pc")
        NC = len(CHUNKS)
        with nc.Block() as block:

            @block.sync
            def _(sp):
                sp.dma_start(z[:, :], feats).then_inc(ld, 16)
                for n, t in enumerate((w1, w2, w3)):
                    sp.dma_start(w[0:t.shape[0], n, :], t).then_inc(ld, 16)
                for n, t in enumerate((b1, b2, b3)):
                    sp.dma_start(col[:, 0, n:n + 1], t.unsqueeze(1), allow_slow_non_contiguous=True).then_inc(ld, 16)
                sp.dma_start(col[:, 1, :], freq.rearrange("n h -> h n"), allow_slow_non_contiguous=True).then_inc(ld, 16)
                sp.dma_start(wo[:, :], wout).then_inc(ld, 16)
                sp.dma_start(wi[:, :, :], win.rearrange("(f p) t -> p f t", p=P)).then_inc(ld, 16)
                sp.dma_start(wc[:, :, :, :], win_ctx.rearrange("(n p) d c -> p n d c", p=P)).then_inc(ld, 16)
                for g in range(4):
                    sp.wait_ge(pool_s, 2 * (g + 1))
                    for i in range(2):
                        sp.dma_start(sums[i, g * P:(g + 1) * P, :], sd[:, i, :]).then_inc(st, 16)
                for t in range(2):
                    sp.wait_ge(pc, 2 * (t + 1))
                    for i in range(2):
                        sp.dma_start(sums_ctx[t * P:(t + 1) * P, i, :], sc[:, t, i, :, :].rearrange("p o c -> p (o c)")).then_inc(stc, 16)
                sp.wait_ge(st, 128)
                sp.wait_ge(stc, 64)

            @block.tensor
            def _(pe):
                pe.wait_ge(ld, 16 * 11)
                for n in range(3):
                    for c, (t0, tn) in enumerate(CHUNKS):
                        if n:
                            pe.wait_ge(sn, NC * (n - 1) + c + 1)
                        rhs = (z if n == 0 else hid)
                        kk = EMB if n == 0 else HID
                        nc.tensor.matmul(ps[0:HID, c, 0:tn], w[0:kk, n, :], rhs[0:kk, t0:t0 + tn], start=True, stop=True).then_inc(mm, 1)
                pe.wait_ge(sn, 3 * NC)
                for g in range(4):
                    o, ct = g // 2, g % 2
                    for d in range(2):
                        pe.wait_ge(evf if d == 0 else evb, g) if g else None
                        for q in range(4):
                            c0 = (2 * o + d) * HW + ct * P
                            last = nc.tensor.matmul(ps[:, 4 * d + q, :], wo[:, c0:c0 + P],
                                                    hid[:, CTX + 512 * q:CTX + 512 * (q + 1)], start=True, stop=True)
                        last.then_inc(taps, 1)
                pe.wait_ge(evf, 4)
                pe.wait_ge(evb, 4)
                for t in range(2):
                    for q in range(2):
                        last = nc.tensor.matmul(ps[:, 2 * t + q, :], hid[:, t * P:(t + 1) * P], wo[:, q * 512:(q + 1) * 512],
                                                start=True, stop=True)
                    last.then_inc(taps, 1)

            @block.vector
            def _(dve):
                dve.wait_ge(ld, 16 * 11)
                dve.wait_ge(zero, 1)
                n_v = [0]

                def step(ins):
                    n_v[0] += 1
                    ins.then_inc(v, 1)
                    dve.wait_ge(v, n_v[0])
                for n in range(3):
                    for c, (t0, tn) in enumerate(CHUNKS):
                        sl = slice(t0, t0 + tn)
                        dve.wait_ge(mm, NC * n + c + 1)
                        step(nc.vector.tensor_scalar(y[:, sl], ps[0:HID, c, 0:tn], col[:, 0, n:n + 1], col[:, 1, n:n + 1],
                                                     ALU.add, ALU.mult))
                        step(nc.vector.tensor_scalar(k[:, sl], y[:, sl], 1 / (2 * math.pi), ROUND, ALU.mult, ALU.add))
                        step(nc.vector.tensor_scalar(k[:, sl], k[:, sl], ROUND, None, ALU.subtract))
                        step(nc.vector.scalar_tensor_tensor(out=y[:, sl], in0=k[:, sl], scalar=-PI2_HI, in1=y[:, sl],
                                                            op0=ALU.mult, op1=ALU.add))
                        step(nc.vector.scalar_tensor_tensor(out=y[:, sl], in0=k[:, sl], scalar=-PI2_LO, in1=y[:, sl],
                                                            op0=ALU.mult, op1=ALU.add))
                        step(nc.vector.tensor_scalar(y[:, sl], y[:, sl], 3.1415925, -3.1415925, ALU.min, ALU.max))
                for g in range(4):
                    dve.wait_ge(taps, 2 * g + 1)
                    dve.wait_ge(pool_s, 2 * g) if g else None
                    nc.vector.tensor_tensor(F[:, :], ps[:, 0:4, :].rearrange("p a b -> p (a b)"), wi[:, g % 2, :], ALU.mult).then_inc(evf, 1)
                    dve.wait_ge(taps, 2 * g + 2)
                    nc.vector.tensor_tensor(B[:, 1:], ps[:, 4:8, :].rearrange("p a b -> p (a b)")[:, 1:], wi[:, g % 2, 1:],
                                            ALU.mult).then_inc(evb, 1)
                for t in range(2):
                    dve.wait_ge(taps, 9 + t)
                    dve.wait_ge(pc, 2 * t) if t else None
                    nc.vector.tensor_tensor(FB[:, :, :, :], ps[:, 2 * t:2 * t + 2, :].rearrange("p o (d c) -> p o d c", d=2),
                                            wc[:, t, :, :].unsqueeze(1).to_broadcast([P, 2, 2, HW]), ALU.mult).then_inc(evc, 1)

            @block.scalar
            def _(act):
                for n in range(3):
                    for c, (t0, tn) in enumerate(CHUNKS):
                        act.wait_ge(v, 6 * (NC * n + c + 1))
                        nc.scalar.activation(hid[:, t0:t0 + tn], y[:, t0:t0 + tn], ACT.Sin).then_inc(sn, 1)

            @block.gpsimd
            def _(pool):
                nc.gpsimd.memset(B[:, 0:1], 0.0).then_inc(zero, 1)
                for g in range(4):
                    pool.wait_ge(evf, g + 1)
                    pool.wait_ge(evb, g + 1)
                    pool.wait_ge(st, 32 * g) if g else None
                    nc.gpsimd.tensor_tensor(sd[:, 0, :], F[:, :], B[:, :], ALU.add).then_inc(pool_s, 1)
                    nc.gpsimd.tensor_tensor(sd[:, 1, :], F[:, :], B[:, :], ALU.subtract).then_inc(pool_s, 1)
                for t in range(2):
                    pool.wait_ge(evc, t + 1)
                    nc.gpsimd.tensor_tensor(sc[:, t, 0, :, :], FB[:, :, 0, :], FB[:, :, 1, :], ALU.add).then_inc(pc, 1)
                    nc.gpsimd.tensor_tensor(sc[:, t, 1, :, :], FB[:, :, 0, :], FB[:, :, 1, :], ALU.subtract).then_inc(pc, 1)


GRP = 8


def kernel_spectrum(nc, tag, sums, tf_dram, bd_dram, spec):
    CH = 2 * HW
    NG = CH // 8
    with Phase(nc, tag) as ph:
        tf = ph.sb("tf", [P, KS, 3, P])
        bd = ph.sb("bd", [P, 8 * R0])
        U = ph.sb("U", [P, 2, GRP, P])
        A = ph.sb("A", [P, R0, CH])
        o = ph.sb("o", [P, 2, CH])
        ps = ph.ps("ps", [P, 8, 512])
        const, dft, mm = ph.sem("const"), ph.sem("dft"), ph.sem("mm")
        ld, stored = [ph.sem("ld0"), ph.sem("ld1")], [ph.sem("so0"), ph.sem("so1")]
        eva, evv, evh = ph.sem("eva"), ph.sem("evv"), ph.sem("evh")
        NR = NG // GRP
        with nc.Block() as block:

            @block.sync
            def _(sp):
                sp.dma_start(tf[:, :, :, :], tf_dram).then_inc(const, 16)
                sp.dma_start(bd[:, :], bd_dram).then_inc(const, 16)
                for w in range(2):
                    view = sums[w].rearrange("c (n1 n2) -> (c n1) n2", n2=P).rearrange("(g p) n -> p g n", p=P)

                    def load(j, u):
                        g0 = at(sp, (2 * j + u - w * NR) * GRP)
                        wait(sp, dft, 2 * j + u - 1)
                        sp.dma_start(U[:, u, :, :], view[:, bass.ds(g0, GRP), :]).then_inc(ld[u], 16)
                    repeat(sp, (w + 1) * NR, load, lo=w * NR)

            @block.tensor
            def _(pe):
                pe.wait_ge(const, 32)
                for w in range(2):
                    def groups(j, u):
                        i = 2 * j + u
                        wait(pe, ld[u], 16 * (j + 1))
                        wait(pe, eva, 2 * i)
                        wait(pe, evv, 2 * i)
                        for g in range(GRP):
                            last = nc.tensor.matmul(ps[:, g // 2, (g % 2) * 256:(g % 2 + 1) * 256], U[:, u, g, :], bd[:, :],
                                                    start=True, stop=True)
                        last.then_inc(dft, 1)
                    repeat(pe, (w + 1) * NR, groups, lo=w * NR)
                    pe.wait_ge(eva, 2 * (w + 1) * NR)
                    pe.wait_ge(evv, 2 * (w + 1) * NR)
                    for k1 in range(KS):
                        n = w * KS + k1
                        real = k1 in (0, KS - 1)
                        if n >= 4:
                            pe.wait_ge(evh, n - 3)
                        bank = ps[:, 4 + n % 4, :]
                        re, im = A[:, k1, :], None if real else A[:, KS - 1 + k1, :]
                        if w == 0:
                            last = nc.tensor.matmul(bank, tf[:, k1, 0, :], re, start=True, stop=real)
                            if not real:
                                last = nc.tensor.matmul(bank, tf[:, k1, 1, :], im, start=False, stop=True)
                        else:
                            last = nc.tensor.matmul(bank, tf[:, k1, 2, :], re, start=True, stop=real)
                            if not real:
                                last = nc.tensor.matmul(bank, tf[:, k1, 0, :], im, start=False, stop=True)
                        last.then_inc(mm, 1)

            def copy_groups(eng, ins, sem, banks, w):
                def go(j, u):
                    i = 2 * j + u
                    wait(eng, dft, i + 1)
                    if w:
                        wait(eng, mm, w * KS)
                    for b in banks:
                        c0 = (i - w * NR) * 8 * GRP + 16 * b
                        ins(A[:, :, bass.ds(c0, 16)].rearrange("p r c -> p c r"),
                            ps[:, b, :].rearrange("p (c r) -> p c r", r=R0)).then_inc(sem, 1)
                repeat(eng, (w + 1) * NR, go, lo=w * NR)

            @block.scalar
            def _(act):
                for w in range(2):
                    copy_groups(act, lambda o_, i_: nc.scalar.activation(o_, i_, ACT.Copy), eva, (0, 1), w)
                    for k1 in range(KS):
                        n = w * KS + k1
                        act.wait_ge(evh, n + 1)
                        act.dma_start(spec[:, k1, :, w, :].rearrange("o k c -> k o c"),
                                      o[:, n % 2, :].rearrange("k (o c) -> k o c", o=2)).then_inc(stored[n % 2], 16)
                act.wait_ge(stored[0], 16 * KS)
                act.wait_ge(stored[1], 16 * KS)

            @block.vector
            def _(dve):
                for w in range(2):
                    copy_groups(dve, nc.vector.tensor_copy, evv, (2, 3), w)
                    for k1 in range(KS):
                        n = w * KS + k1
                        dve.wait_ge(mm, n + 1)
                        if n >= 2:
                            dve.wait_ge(stored[n % 2], 16 * (n // 2))
                        nc.vector.tensor_copy(o[:, n % 2, :], ps[:, 4 + n % 4, :]).then_inc(evh, 1)


def long_conv(nc, tag, src, spec, x_gate, skip, tf_dram, ti_dram, bd_dram, bi_dram, ident_dram, dst):
    NG = HW // 8
    NR = NG // GRP
    with Phase(nc, tag) as ph:
        ident = ph.sb("ident", [P, P])
        tf = ph.sb("tf", [P, KS, 3, P])
        ti = ph.sb("ti", [P, KS, 3, P])
        bd = ph.sb("bd", [P, 8 * R0])
        bi = ph.sb("bi", [P, 64])
        U = ph.sb("U", [P, 2, GRP, P])
        A = ph.sb("A", [P, R0, HW])
        Bt = ph.sb("Bt", [P, HW, R0])
        h = ph.sb("h", [P, 3, 2, HW])
        m1, m2 = ph.sb("m1", [P, 2, 2, HW]), ph.sb("m2", [P, 2, 2, HW])
        Y = ph.sb("Y", [P, 2, 2, HW])
        W = ph.sb("W", [P, 2, 512])
        yo = ph.sb("yo", [64, 2, 512])
        val, gate = ph.sb("val", [64, 2, 16, P]), ph.sb("gate", [64, 2, 16, P])
        sk = ph.sb("sk", [64, HW // 4])
        skipped, total = ph.sb("skipped", [64, 2, 512]), ph.sb("total", [64, 2, 512])
        ps = ph.ps("ps", [P, 8, 512])
        skl, vl = ph.sem("skl"), [ph.sem("vl0"), ph.sem("vl1")]
        s_skip, s_total, gated = ph.sem("skipped"), ph.sem("total"), ph.sem("gated")
        bdl, const, dft, mx, mb = ph.sem("bdl"), ph.sem("const"), ph.sem("dft"), ph.sem("mx"), ph.sem("mb")
        ld, stored = [ph.sem("ld0"), ph.sem("ld1")], [ph.sem("so0"), ph.sem("so1")]
        hl = [ph.sem(f"hl{i}") for i in range(3)]
        eva, evv, prod, comb, bev = ph.sem("eva"), ph.sem("evv"), ph.sem("prod"), ph.sem("comb"), ph.sem("bev")
        tt, wv, yy = ph.sem("tt"), ph.sem("wv"), ph.sem("yy")
        by_q = lambda ap: ap.rearrange("c (n1 n2) -> (c n1) n2", n2=P).rearrange("(r m p) n -> r p m n", m=16, p=64)
        view = src.rearrange("c (n1 n2) -> (c n1) n2", n2=P).rearrange("(g p) n -> p g n", p=P)
        out = dst.rearrange("c (n1 n2) -> (c n1) n2", n2=P).rearrange("(q g p) n -> q p g n", g=4, p=64)
        NQ = HW // 16
        with nc.Block() as block:

            @block.sync
            def _(sp):
                sp.dma_start(bd[:, :], bd_dram).then_inc(bdl, 16)

                def load(j, u):
                    g0 = at(sp, (2 * j + u) * GRP)
                    wait(sp, dft, 2 * j + u - 1)
                    sp.dma_start(U[:, u, :, :], view[:, bass.ds(g0, GRP), :]).then_inc(ld[u], 16)
                repeat(sp, NR, load)
                for k1 in range(KS):
                    if k1 >= 3:
                        sp.wait_ge(prod, 2 * (k1 - 2))
                    sp.dma_start(h[:, k1 % 3, :, :], spec[k1]).then_inc(hl[k1 % 3], 16)
                for q in range(NQ):
                    if q % 4 == 0:
                        for n in ((0, 1) if q == 0 else (q // 4 + 1,)):
                            if n < NQ // 4:
                                if n >= 2:
                                    sp.wait_ge(gated, 4 * (n - 1))
                                sp.dma_start(val[:, n % 2, :, :], by_q(src)[n]).then_inc(vl[n % 2], 16)
                                sp.dma_start(gate[:, n % 2, :, :], by_q(x_gate)[n]).then_inc(vl[n % 2], 16)
                    sp.wait_ge(gated, q + 1)
                    sp.dma_start(out[q], yo[:, q % 2, :].rearrange("p (g n) -> p g n", n=P)).then_inc(stored[q % 2], 16)
                sp.wait_ge(stored[0], 16 * (NQ // 2))
                sp.wait_ge(stored[1], 16 * (NQ // 2))

            @block.gpsimd
            def _(pool):
                for k1 in range(KS):
                    u = k1 % 2
                    pool.wait_ge(prod, 2 * (k1 + 1))
                    if k1 >= 2:
                        pool.wait_ge(mb, k1 - 1)
                    nc.gpsimd.tensor_tensor(Y[:, u, 0, :], m1[:, u, 0, :], m2[:, u, 1, :], ALU.subtract).then_inc(comb, 1)
                    nc.gpsimd.tensor_tensor(Y[:, u, 1, :], m1[:, u, 1, :], m2[:, u, 0, :], ALU.add).then_inc(comb, 1)

                def skip_part(q):
                    n, m = q // 4, 4 * (q % 4)
                    pool.wait_ge(vl[n % 2], 32 * (n // 2 + 1))
                    if q >= 2:
                        pool.wait_ge(s_total, q - 1)
                    nc.gpsimd.tensor_tensor(skipped[:, q % 2, :].rearrange("p (g n) -> p g n", n=P), val[:, n % 2, m:m + 4, :],
                                            sk[:, 4 * q:4 * q + 4].unsqueeze(2).to_broadcast([64, 4, P]), ALU.mult).then_inc(s_skip, 1)
                pool.wait_ge(skl, 64)
                skip_part(0)
                for q in range(NQ):
                    if q + 1 < NQ:
                        skip_part(q + 1)
                    pool.wait_ge(s_total, q + 1)
                    if q >= 2:
                        pool.wait_ge(stored[q % 2], 16 * (q // 2))
                    nc.gpsimd.tensor_tensor(yo[:, q % 2, :].rearrange("p (g n) -> p g n", n=P),
                                            total[:, q % 2, :].rearrange("p (g n) -> p g n", n=P),
                                            gate[:, (q // 4) % 2, 4 * (q % 4):4 * (q % 4) + 4, :], ALU.mult).then_inc(gated, 1)

            @block.tensor
            def _(pe):
                pe.wait_ge(bdl, 16)

                def groups(j, u):
                    i = 2 * j + u
                    wait(pe, ld[u], 16 * (j + 1))
                    wait(pe, eva, 2 * i)
                    wait(pe, evv, 2 * i)
                    for g in range(GRP):
                        last = nc.tensor.matmul(ps[:, g // 2, (g % 2) * 256:(g % 2 + 1) * 256], U[:, u, g, :], bd[:, :],
                                                start=True, stop=True)
                    last.then_inc(dft, 1)
                repeat(pe, NR, groups)
                pe.wait_ge(eva, 2 * NR)
                pe.wait_ge(evv, 2 * NR)

                def pair(bank, table, k1, re, im, terms):
                    for half in range(2):
                        ts = [(m, x) for m, x in terms[half] if x is not None]
                        for n, (m, x) in enumerate(ts):
                            last = nc.tensor.matmul(bank[:, half * HW:(half + 1) * HW], table[:, k1, m, :], x,
                                                    start=(n == 0), stop=(n == len(ts) - 1))
                    return last

                def fwd(k1):
                    real = k1 in (0, KS - 1)
                    if k1 >= 2:
                        pe.wait_ge(prod, 2 * (k1 - 1))
                    re, im = A[:, k1, :], None if real else A[:, KS - 1 + k1, :]
                    pair(ps[:, 4 + k1 % 2, :], tf, k1, re, im, [[(0, re), (1, im)], [(0, im), (2, re)]]).then_inc(mx, 1)

                def inv(k1):
                    pe.wait_ge(comb, 2 * (k1 + 1))
                    if k1 >= 2:
                        pe.wait_ge(bev, k1 - 1)
                    re, im = Y[:, k1 % 2, 0, :], Y[:, k1 % 2, 1, :]
                    real = k1 in (0, KS - 1)
                    second = [(1, re), (0, im)]
                    bank = ps[:, 6 + k1 % 2, :]
                    if real:
                        nc.tensor.matmul(bank[:, 0:HW], ti[:, k1, 0, :], re, start=True, stop=False)
                        nc.tensor.matmul(bank[:, 0:HW], ti[:, k1, 2, :], im, start=False, stop=True).then_inc(mb, 1)
                    else:
                        pair(bank, ti, k1, re, im, [[(0, re), (2, im)], second]).then_inc(mb, 1)
                pe.wait_ge(const, 64)
                fwd(0)
                for k1 in range(KS):
                    if k1 + 1 < KS:
                        fwd(k1 + 1)
                    inv(k1)
                pe.wait_ge(bev, KS)

                def turn(q):
                    if q >= 2:
                        pe.wait_ge(wv, q - 1)
                    for g in range(4):
                        c0 = (4 * q + g) * 4
                        last = nc.tensor.transpose(ps[:, q % 2, g * P:(g + 1) * P],
                                                   Bt[:, c0:c0 + 4, :].rearrange("p c r -> p (c r)"), ident[:, :])
                    last.then_inc(tt, 1)
                turn(0)
                for q in range(NQ):
                    if q + 1 < NQ:
                        turn(q + 1)
                    pe.wait_ge(wv, q + 1)
                    if q >= 2:
                        pe.wait_ge(s_total, q - 1)
                    nc.tensor.matmul(ps[0:64, 2 + q % 2, :], bi[:, :], W[:, q % 2, :], start=True, stop=True).then_inc(yy, 1)

            def copy_groups(eng, ins, sem, banks):
                def go(j, u):
                    i = 2 * j + u
                    wait(eng, dft, i + 1)
                    for b in banks:
                        ins(A[:, :, bass.ds(i * 8 * GRP + 16 * b, 16)].rearrange("p r c -> p c r"),
                            ps[:, b, :].rearrange("p (c r) -> p c r", r=R0)).then_inc(sem, 1)
                repeat(eng, NR, go)

            @block.scalar
            def _(act):
                for dst_, src_ in ((tf, tf_dram), (ti, ti_dram), (bi, bi_dram), (ident, ident_dram)):
                    act.dma_start(dst_[:], src_).then_inc(const, 16)
                for c in range(4):
                    act.dma_start(sk[16 * c:16 * (c + 1), :], skip.rearrange("(m c) -> c m", c=4)[c].partition_broadcast(16),
                                  allow_slow_non_contiguous=True).then_inc(skl, 16)
                copy_groups(act, lambda o_, i_: nc.scalar.activation(o_, i_, ACT.Copy), eva, (0, 1))
                for k1 in range(KS):
                    act.wait_ge(mb, k1 + 1)
                    if k1 in (0, KS - 1):
                        nc.scalar.activation(Bt[:, :, k1], ps[:, 6 + k1 % 2, 0:HW], ACT.Copy).then_inc(bev, 1)
                    else:
                        nc.scalar.activation(Bt[:, :, k1:k1 + KS:KS - 1].rearrange("p c z -> p z c"),
                                             ps[:, 6 + k1 % 2, :].rearrange("p (z c) -> p z c", z=2), ACT.Copy).then_inc(bev, 1)

            @block.vector
            def _(dve):
                copy_groups(dve, nc.vector.tensor_copy, evv, (2, 3))
                for k1 in range(KS):
                    u = k1 % 2
                    dve.wait_ge(mx, k1 + 1)
                    dve.wait_ge(hl[k1 % 3], 16 * (k1 // 3 + 1))
                    if k1 >= 2:
                        dve.wait_ge(comb, 2 * (k1 - 1))
                    X = ps[:, 4 + u, :].rearrange("p (z c) -> p z c", z=2)
                    for m, part in ((m1, 0), (m2, 1)):
                        nc.vector.tensor_tensor(m[:, u, :, :], X, h[:, k1 % 3, part:part + 1, :].to_broadcast([P, 2, HW]),
                                                ALU.mult).then_inc(prod, 1)

                def copy_turned(q):
                    dve.wait_ge(tt, q + 1)
                    if q >= 2:
                        dve.wait_ge(yy, q - 1)
                    nc.vector.tensor_copy(W[:, q % 2, :], ps[:, q % 2, :]).then_inc(wv, 1)
                copy_turned(0)
                for q in range(NQ):
                    if q + 1 < NQ:
                        copy_turned(q + 1)
                    dve.wait_ge(yy, q + 1)
                    dve.wait_ge(s_skip, q + 1)
                    if q >= 2:
                        dve.wait_ge(gated, q - 1)
                    nc.vector.tensor_tensor(total[:, q % 2, :], ps[0:64, 2 + q % 2, :], skipped[:, q % 2, :],
                                            ALU.add).then_inc(s_total, 1)


def context_hyena(nc, tag, sums_ctx, vx, skip, fc_dram, ic_dram, ident_dram, dst):
    KTL = [(0, P), (P, P), (2 * P, 1)]
    with Phase(nc, tag) as ph:
        ident = ph.sb("ident", [P, P])
        fc = ph.sb("fc", [P, 2, 2, CTX + 1])
        ic = ph.sb("ic", [P, 3, 2, CTX])
        sd = ph.sb("sd", [P, 2, 2, 2 * HW])
        H_ = ph.sb("H", [P, 3, 2, 2 * HW])
        sk = ph.sb("sk", [P, 2, 2])
        v = ph.sb("v", [P, 3, 2, CTX])
        yt = ph.sb("yt", [P, 2, HW])
        m1, m2, Y = (ph.sb(s, [P, 3, 2, HW]) for s in ("m1", "m2", "Y"))
        g = ph.sb("g", [P, 2, CTX])
        ps = ph.ps("ps", [P, 8, 512])
        ld, pe_s, dv, st = ph.sem("ld"), ph.sem("pe"), ph.sem("dve"), ph.sem("st")
        with nc.Block() as block:

            @block.sync
            def _(sp):
                for t, s in ((ident[:, :], ident_dram), (fc[:, :, :, :], fc_dram), (ic[:, :, :, :], ic_dram),
                             (sd[:, :, :, :], sums_ctx.rearrange("(n p) w c -> p n w c", p=P))):
                    sp.dma_start(t, s).then_inc(ld, 16)
                sp.dma_start(v[:, :, :, :], vx.rearrange("(w f p) t -> p w f t", p=P, f=2)).then_inc(ld, 16)
                for o in range(2):
                    sp.dma_start(sk[:, o, :], skip[o].rearrange("(f p) -> p f", p=P), allow_slow_non_contiguous=True).then_inc(ld, 16)
                sp.wait_ge(dv, 6 + 2 * 13)
                sp.dma_start(dst[:, 0:CTX].rearrange("(f p) t -> p f t", p=P), v[:, 0, :, :]).then_inc(st, 16)
                sp.wait_ge(st, 16)

            @block.tensor
            def _(pe):
                pe.wait_ge(ld, 112)
                for w in range(2):
                    for kt, (k0, kn) in enumerate(KTL):
                        for n in range(2):
                            last = nc.tensor.matmul(ps[0:kn, 3 * w + kt, :], fc[:, n, w, k0:k0 + kn], sd[:, n, w, :],
                                                    start=(n == 0), stop=(n == 1))
                        last.then_inc(pe_s, 1)
                for o in range(2):
                    base = 6 + 13 * o
                    pe.wait_ge(dv, base)
                    for f in range(2):
                        for n in range(2):
                            last = nc.tensor.transpose(ps[:, 0, (2 * n + f) * P:(2 * n + f + 1) * P], v[:, 0, f, n * P:(n + 1) * P], ident[:, :])
                    last.then_inc(pe_s, 1)
                    pe.wait_ge(dv, base + 1)
                    for kt, (k0, kn) in enumerate(KTL):
                        for w in range(2):
                            for n in range(2):
                                last = nc.tensor.matmul(ps[0:kn, 1 + kt, w * HW:(w + 1) * HW], fc[:, n, w, k0:k0 + kn], yt[:, n, :],
                                                        start=(n == 0), stop=(n == 1))
                    last.then_inc(pe_s, 1)
                    pe.wait_ge(dv, base + 9)
                    for f in range(2):
                        terms = [(kt, w, kn) for kt, (_, kn) in enumerate(KTL) for w in range(2)]
                        for n, (kt, w, kn) in enumerate(terms):
                            last = nc.tensor.matmul(ps[:, 4, f * CTX:(f + 1) * CTX], Y[0:kn, kt, w, f * P:(f + 1) * P], ic[0:kn, kt, w, :],
                                                    start=(n == 0), stop=(n == len(terms) - 1))
                    last.then_inc(pe_s, 1)

            @block.vector
            def _(dve):
                n_v = [0]

                def step(ins):
                    n_v[0] += 1
                    ins.then_inc(dv, 1)
                    dve.wait_ge(dv, n_v[0])
                dve.wait_ge(ld, 112)
                for w in range(2):
                    for kt, (k0, kn) in enumerate(KTL):
                        dve.wait_ge(pe_s, 3 * w + kt + 1)
                        step(nc.vector.tensor_copy(H_[0:kn, kt, w, :], ps[0:kn, 3 * w + kt, :]))
                for o in range(2):
                    base = 6 + 3 * o
                    dve.wait_ge(pe_s, base + 1)
                    step(nc.vector.tensor_copy(yt[:, :, :], ps[:, 0, :].rearrange("p (n c) -> p n c", n=2)))
                    dve.wait_ge(pe_s, base + 2)
                    for lo, hi, kn in ((0, 2, P), (2, 3, 1)):
                        X = ps[0:kn, 1 + lo:1 + hi, :].rearrange("p k (w c) -> p k w c", w=2)
                        hh = lambda w: H_[0:kn, lo:hi, w:w + 1, o * HW:(o + 1) * HW].to_broadcast([kn, hi - lo, 2, HW])
                        step(nc.vector.tensor_tensor(m1[0:kn, lo:hi, :, :], X, hh(0), ALU.mult))
                        step(nc.vector.tensor_tensor(m2[0:kn, lo:hi, :, :], X, hh(1), ALU.mult))
                        step(nc.vector.tensor_tensor(Y[0:kn, lo:hi, 0, :], m1[0:kn, lo:hi, 0, :], m2[0:kn, lo:hi, 1, :], ALU.subtract))
                        step(nc.vector.tensor_tensor(Y[0:kn, lo:hi, 1, :], m1[0:kn, lo:hi, 1, :], m2[0:kn, lo:hi, 0, :], ALU.add))
                    dve.wait_ge(pe_s, base + 3)
                    for f in range(2):
                        step(nc.vector.scalar_tensor_tensor(out=g[:, f, :], in0=v[:, 0, f, :], scalar=sk[:, o, f:f + 1],
                                                            in1=ps[:, 4, f * CTX:(f + 1) * CTX], op0=ALU.mult, op1=ALU.add))
                    for f in range(2):
                        step(nc.vector.tensor_tensor(v[:, 0, f, :], g[:, f, :], v[:, 1 + o, f, :], ALU.mult))


def constants():
    c={}
    i=np.arange(P)
    c['ident']=np.eye(P,dtype=np.float32)
    tri=np.zeros((P,3,P),np.float32)
    tri[:,0,:]=i[:,None]<=i[None,:]; tri[:,1,:]=i[:,None]>=i[None,:]; tri[:,2,:]=1
    c['tri']=tri
    neg=np.zeros((P,2,P),np.float32)
    neg[:,0,:]=np.where(i[None,:]>=i[:,None],0,-1e30); neg[:,1,:]=np.where(i[None,:]<=i[:,None],0,-1e30)
    c['neg']=neg
    lev=np.zeros((P,2,7,P),np.float32)
    for L in range(7):
        s=1<<L
        m=(i[:,None]//(2*s)==i[None,:]//(2*s))&((i[:,None]//s)%2==1)&((i[None,:]//s)%2==0)
        lev[:,0,L,:]=m; lev[:,1,L,:]=m.T
    c['lev']=lev
    t=np.arange(2048); nf=32
    inv=np.float32(10000.0)**(-np.arange(nf,dtype=np.float32)/np.float32(nf))
    rope=np.zeros((2304,2,P),np.float32); rope[:256,0,:]=1
    for g,pos in enumerate((t//64,t%64)):
        ang=pos.astype(np.float32)[:,None]*inv[None,:]
        co,si=np.cos(ang),np.sin(ang)
        o=g*64
        rope[256:,0,o:o+32]=co; rope[256:,0,o+32:o+64]=co
        rope[256:,1,o:o+32]=-si; rope[256:,1,o+32:o+64]=si
    c['rope']=rope
    hot=np.zeros((32,64,2,64),np.float32)
    q=np.arange(64); c0=np.clip(q-8,0,48)
    for kc in range(64):
        inw=(kc>=c0)&(kc<c0+16)
        for qq in range(64):
            if inw[qq]: hot[kc-qq+15,kc,:,qq]=1
            else: hot[31,kc,:,qq]=-1e30
    f32=np.float32
    def feats(l):
        t=np.linspace(0.0,1.0,l,dtype=f32)[:,None]
        fr=np.linspace(1e-4,15,16,dtype=f32)
        ang=(f32(2.0*math.pi/l)*np.arange(l,dtype=f32)[:,None])*fr[None,:]
        return t,np.concatenate([t,np.cos(ang),-np.sin(ang)],-1).astype(f32)
    mx=math.log(1e-2)/0.3; mn=math.log(1e-2)/1.5
    deltas=np.abs(np.linspace(mn,mx,256,dtype=f32))
    tc,zc=feats(256); tx,zx=feats(2048)
    c['feats']=np.ascontiguousarray(np.concatenate([zc,zx],0).T)
    c['win']=np.ascontiguousarray(np.exp(-tx*deltas[None,:]).T.astype(f32))
    wc=np.exp(-tc*deltas[None,:]).astype(f32)
    wc2=np.stack([wc,wc],1); wc2[0,1]=0
    c['win_ctx']=wc2
    n2=np.arange(128)[:,None,None]; k1=np.arange(17)[None,:,None]; k2=np.arange(128)[None,None,:]
    th=2*math.pi*((n2*(k1+32*k2))%4096)/4096
    tf=np.stack([np.cos(th),np.sin(th),-np.sin(th)],2)
    c['tf']=tf.astype(f32)
    c['ti']=np.ascontiguousarray(tf.transpose(3,1,2,0)).astype(f32)
    n1=np.arange(16)[:,None]; kk=np.arange(17)[None,:]
    ph=2*math.pi*((n1*kk)%32)/32
    F=np.concatenate([np.cos(ph),-np.sin(ph[:,1:16])],1)
    bd=np.zeros((8,16,8,32)); bi=np.zeros((4,32,4,16))
    wgt=np.where((kk==0)|(kk==16),1,2)/4096.0
    G=np.concatenate([np.cos(ph)*wgt,-np.sin(ph[:,1:16])*2/4096.0],1).T
    for i_ in range(8): bd[i_,:,i_,:]=F
    for i_ in range(4): bi[i_,:,i_,:]=G
    c['bd']=bd.reshape(128,256).astype(f32); c['bi']=bi.reshape(128,64).astype(f32)
    n=np.arange(256)[:,None]; k=np.arange(257)[None,:]
    th=2*math.pi*((n*k)%512)/512
    c['fc']=np.stack([np.cos(th),-np.sin(th)],1).reshape(2,128,2,257).transpose(1,0,2,3).astype(f32).copy()
    w=np.where((k==0)|(k==256),1,2)/512.0
    ic=np.zeros((384,2,256)); ic[:257]=np.stack([(np.cos(th)*w).T,(-np.sin(th)*w).T],1)
    c['ic']=ic.reshape(3,128,2,256).transpose(1,0,2,3).astype(f32).copy()
    c['hot']=hot.reshape(32,64,128)
    return c


def build(nc, a, k, out):
    dram = lambda name, shape: nc.dram_tensor(name, shape, F32).ap()
    proj, gate = dram("proj", (IN_WIDTH, T)), dram("gate", (2, D))
    dnT, qkv = dram("dn_conv_out", (3 * DN, T)), dram("dn_qkv", (T, 3 * DN))
    o_dir = [dram("dn_forward", (T, DN)), dram("dn_backward", (T, DN))]
    na = dram("na_out", (NH * DH, T))
    vx, vx_ctx = dram("hy_vx", (3 * HW, SEQ)), dram("hy_vx_ctx", (3 * HW, CTX))
    sums, sums_ctx = dram("hy_sums", (2, 2 * HW, SEQ)), dram("hy_sums_ctx", (CTX, 2, 2 * HW))
    spec, y1 = dram("hy_spec", (2, KS, P, 2, HW)), dram("hy_y1", (HW, SEQ))
    hy, hy_ctx = dram("hy_out", (HW, SEQ)), dram("hy_out_ctx", (HW, CTX))
    mid = dram("mid", (T, D))
    x, ctx = a["x"][0], a["ctx"][0]
    flat = lambda ap: ap.rearrange("a b -> (a b)")
    for i in range(DEPTH):
        last = i == DEPTH - 1
        n = lambda s: f"l{i}{s}"
        with nc.sbuf_tensor(n("aff"), [P, 2, KT, 2], F32) as aff:
            modulation(nc, n("mod"), a["c"][0], a["c_ctx"], a["w_ada"][i], a["b_ada"][i], a["g_pre"][i], a["g_post"][i], aff, gate)
            norm_project(nc, n("proj"), [(ctx, 0, 2, 1), (x, 2, SEQ // P, 0)], aff, a["w_in"][i], k["ident"], proj)
        attention(nc, n("na"), proj, a["na_rpb"][i], k["ident"], k["hot"], na, not last)
        with nc.sbuf_tensor(n("col"), [P, 7, NT, 2 * H], F32) as col:
            short_conv(nc, n("dc"), proj, C_DN, 12, a["dn_conv"][i], True, dnT[:, 0:CTX], dnT[:, CTX:T])
            dn_gates(nc, n("dg"), proj, flat(a["dn_a_log"][i]), flat(a["dn_dt_bias"][i]), k["ident"], k["tri"], col)
            dn_tokens(nc, n("dt"), dnT, k["rope"], k["ident"], qkv)
            dn_scan(nc, n("ds"), qkv, col, k["ident"], k["tri"], k["neg"], k["lev"], o_dir)
        short_conv(nc, n("hc"), proj, C_HY, 6, a["hy_conv"][i], False, vx_ctx, vx)
        hyena_filters(nc, n("hf"), k["feats"], *(a[f"hy_{s}"][i] for s in ("w1", "b1", "w2", "b2", "w3", "b3", "freq", "wout")),
                      k["win"], k["win_ctx"], sums, sums_ctx)
        kernel_spectrum(nc, n("hk"), sums, k["tf"], k["bd"], spec)
        src = vx[0:HW, :]
        for o in range(2):
            long_conv(nc, n(f"hl{o}"), src, spec[o], vx[HW * (o + 1):HW * (o + 2), :], a["hy_skip"][i][o],
                      k["tf"], k["ti"], k["bd"], k["bi"], k["ident"], y1 if o == 0 else hy)
            src = y1
        if not last:
            context_hyena(nc, n("hx"), sums_ctx, vx_ctx, a["hy_skip"][i], k["fc"], k["ic"], k["ident"], hy_ctx)
            output_tiles(nc, n("oc"), (0, 2), proj, na, o_dir, hy_ctx, a["dn_norm"][i], a["w_out"][i], gate, 1, k["ident"],
                         ctx, mid[0:CTX, :])
        output_tiles(nc, n("ox"), (2, NT), proj, na, o_dir, hy, a["dn_norm"][i], a["w_out"][i], gate, 0, k["ident"],
                     x, out[0] if last else mid[CTX:T, :])
        x, ctx = mid[CTX:T, :], mid[0:CTX, :]


def kernel(**inputs):
    from concourse.bacc import Bacc
    from concourse.bass_utils import run_bass_kernel_spmd

    nc = Bacc("TRN2", target_bir_lowering=False, num_devices=1)
    arrays = {}

    def put(name, a):
        arrays[name] = np.ascontiguousarray(a)
        return nc.dram_tensor(name, a.shape, F32, kind="ExternalInput").ap()
    a = {name: put("in_" + name, np.asarray(v)) for name, v in inputs.items()}
    k = {name: put("table_" + name, v) for name, v in constants().items()}
    out = nc.dram_tensor("out", (1, SEQ, D), F32, kind="ExternalOutput").ap()
    build(nc, a, k, out)
    return run_bass_kernel_spmd(nc, [arrays], core_ids=[0]).results[0]["out"]
```
